# Optimizing a Trainium2 kernel written in Bass

```python
import math
import jax, jax.numpy as jnp
from jax import lax
import numpy as np
import jax
import jax.numpy as jnp

D_MODEL = 1024
BATCH = 1
SEQ = 256
DEPTH = 2

GRID_W = 64
CHUNK = 128
EPS = 1e-6
MIX_WIDTH = D_MODEL
RET_HEADS = 8
RET_DH = (MIX_WIDTH // 2) // RET_HEADS
RET_WIDTH = RET_HEADS * RET_DH
ROPE_BASE = 10000.0
NA_HEADS = 8
NA_DH = (MIX_WIDTH // 2) // NA_HEADS
NA_WIDTH = NA_HEADS * NA_DH
NA_WIN_R = 8
NA_WIN_C = 16
NA_QBLK = 16
AB_IN_DIM = 4 * RET_WIDTH + 3 * NA_WIDTH
SSD_INNER = 2 * D_MODEL
SSD_HEADDIM = 64
SSD_HEADS = SSD_INNER // SSD_HEADDIM
SSD_GROUPS = 4
SSD_HPG = SSD_HEADS // SSD_GROUPS
SSD_STATE = 128
SSD_CONV = 5
SSD_XBC = SSD_INNER + 2 * SSD_GROUPS * SSD_STATE
SSD_IN_DIM = SSD_INNER + SSD_XBC + 2 * SSD_HEADS
FFN_DIM = 2816
FFN_CONV = 3
N_EVEN = (DEPTH + 1) // 2
N_ODD = DEPTH // 2


def rms_norm(x, g):
    xf = x.astype(jnp.float32)
    y = xf * lax.rsqrt(jnp.mean(xf * xf, axis=-1, keepdims=True) + EPS)
    return (y * g.astype(jnp.float32)).astype(x.dtype)

def depthwise_conv_centered(x, w, b):
    width, ch = w.shape
    pad = width // 2
    y = lax.conv_general_dilated(x, w[:, None, :].astype(x.dtype), window_strides=(1,),
                                 padding=[(pad, pad)], dimension_numbers=('NWC', 'WIO', 'NWC'),
                                 feature_group_count=ch)
    return y + b.astype(x.dtype)

def rotary(x, pos):
    half = x.shape[-1] // 2
    inv = 1.0 / (ROPE_BASE ** (jnp.arange(half, dtype=jnp.float32) / half))
    ang = pos.astype(jnp.float32)[:, None] * inv[None, :]
    cos = jnp.cos(ang)[None, :, None, :]
    sin = jnp.sin(ang)[None, :, None, :]
    xf = x.astype(jnp.float32)
    x1, x2 = xf[..., :half], xf[..., half:]
    return jnp.concatenate([x1 * cos - x2 * sin, x1 * sin + x2 * cos], axis=-1).astype(x.dtype)

def chunked_scan(q, k, v, log_a, include_diag):
    f32 = jnp.float32
    bsz, s, g, n = q.shape
    hg, p = v.shape[3], v.shape[4]
    n_chunks = s // CHUNK

    def to_chunks(t):
        return jnp.moveaxis(t.astype(f32).reshape(bsz, n_chunks, CHUNK, *t.shape[2:]), 1, 0)

    qc, kc, vc, ac = to_chunks(q), to_chunks(k), to_chunks(v), to_chunks(log_a)
    idx = jnp.arange(CHUNK)
    mask = (idx[:, None] >= idx[None, :]) if include_diag else (idx[:, None] > idx[None, :])

    def step(h, inp):
        qq, kk, vv, aa = inp
        cs = jnp.cumsum(aa, axis=1)
        seg = cs[:, :, None] - cs[:, None, :]
        decay = jnp.exp(jnp.where(mask[None, :, :, None, None], seg, -jnp.inf))
        qk = jnp.einsum('bjgn,blgn->bjlg', qq, kk)
        y_intra = jnp.einsum('bjlgh,blghp->bjghp', qk[..., None] * decay, vv)
        y_inter = jnp.einsum('bjgn,bghnp->bjghp', qq, h) * jnp.exp(cs)[..., None]
        tail = jnp.exp(cs[:, -1:] - cs)
        h_new = h * jnp.exp(cs[:, -1])[..., None, None] + jnp.einsum('blgn,blghp->bghnp', kk, vv * tail[..., None])
        return h_new, y_intra + y_inter

    h0 = jnp.zeros((bsz, g, hg, n, p), f32)
    _, ys = lax.scan(step, h0, (qc, kc, vc, ac))
    return jnp.moveaxis(ys, 0, 1).reshape(bsz, s, g, hg, p)

def bidir_scan(q, k, v_f, v_b, a_f, a_b):
    y_f = chunked_scan(q, k, v_f, a_f, True)
    flip = lambda t: jnp.flip(t, axis=1)
    y_b = flip(chunked_scan(flip(q), flip(k), flip(v_b), flip(a_b), False))
    return y_f + y_b

def neighborhood_attention(q, k, v, rpb):
    f32 = jnp.float32
    bsz, s, h, dh = q.shape
    rows = s // GRID_W
    win_r = min(NA_WIN_R, rows)
    n_cb = GRID_W // NA_QBLK
    span = NA_QBLK + NA_WIN_C
    qb_all = (q.astype(f32) * dh ** -0.5).reshape(bsz, rows, n_cb, NA_QBLK, h, dh)
    qb_all = jnp.moveaxis(qb_all, 2, 0)
    k = k.reshape(bsz, rows, GRID_W, h, dh)
    v = v.reshape(bsz, rows, GRID_W, h, dh)
    r = jnp.arange(rows)
    key_rows = jnp.clip(r - win_r // 2, 0, rows - win_r)[:, None] + jnp.arange(win_r)[None, :]
    dr = key_rows - r[:, None] + (NA_WIN_R - 1)
    c0s = jnp.arange(n_cb) * NA_QBLK

    def block(args):
        qb, c0 = args
        qcols = c0 + jnp.arange(NA_QBLK)
        kcols = jnp.clip(c0 - NA_WIN_C // 2, 0, GRID_W - span) + jnp.arange(span)
        cstart = jnp.clip(qcols - NA_WIN_C // 2, 0, GRID_W - NA_WIN_C)
        valid = (kcols[None, :] >= cstart[:, None]) & (kcols[None, :] < cstart[:, None] + NA_WIN_C)
        dc = jnp.clip(kcols[None, :] - qcols[:, None], -(NA_WIN_C - 1), NA_WIN_C - 1) + (NA_WIN_C - 1)
        kb = k[:, key_rows[:, :, None], kcols[None, None, :]].astype(f32)
        vb = v[:, key_rows[:, :, None], kcols[None, None, :]].astype(f32)
        bias = rpb[:, dr[:, None, :, None], dc[None, :, None, :]].astype(f32)
        sc = jnp.einsum('brqhd,brwchd->bhrqwc', qb, kb) + bias[None]
        sc = jnp.where(valid[:, None, :], sc, -jnp.inf)
        pr = jax.nn.softmax(sc.reshape(*sc.shape[:4], -1), axis=-1).reshape(sc.shape)
        return jnp.einsum('bhrqwc,brwchd->brqhd', pr, vb)

    out = lax.map(block, (qb_all, c0s))
    return jnp.moveaxis(out, 0, 2).reshape(bsz, s, h * dh)

def retention_na_mixer(hn, w_in, ret_decay_logit, ret_gn_g, na_rpb, w_out):
    f32 = jnp.float32
    bsz, s, _ = hn.shape
    proj = hn @ w_in
    R, N = RET_WIDTH, NA_WIDTH
    rq, rk, rv, rg, nq, nk, nv = jnp.split(proj, [R, 2 * R, 3 * R, 4 * R, 4 * R + N, 4 * R + 2 * N], axis=-1)
    pos = jnp.arange(s)
    rshape = (bsz, s, RET_HEADS, RET_DH)
    rq = rotary(rq.reshape(rshape), pos)
    rk = rotary(rk.reshape(rshape), pos) * (RET_DH ** -0.5)
    rv = rv.reshape(bsz, s, RET_HEADS, 1, RET_DH)
    log_gamma = -jax.nn.softplus(-ret_decay_logit.astype(f32))
    a_f = jnp.broadcast_to(log_gamma[0][None, None, :, None], (bsz, s, RET_HEADS, 1))
    a_b = jnp.broadcast_to(log_gamma[1][None, None, :, None], (bsz, s, RET_HEADS, 1))
    y = bidir_scan(rq, rk, rv, rv, a_f, a_b).reshape(rshape)
    mu = jnp.mean(y, axis=-1, keepdims=True)
    var = jnp.mean(jnp.square(y - mu), axis=-1, keepdims=True)
    y = ((y - mu) * lax.rsqrt(var + EPS)).reshape(bsz, s, RET_WIDTH) * ret_gn_g.astype(f32)
    ret_out = (jax.nn.silu(rg.astype(f32)) * y).astype(hn.dtype)
    nshape = (bsz, s, NA_HEADS, NA_DH)
    na_out = neighborhood_attention(nq.reshape(nshape), nk.reshape(nshape), nv.reshape(nshape), na_rpb).astype(hn.dtype)
    return jnp.concatenate([ret_out, na_out], axis=-1) @ w_out

def ssd_mixer(hn, w_in, conv_w, conv_b, dt_bias, a_log, d_skip, norm_g, w_out):
    f32 = jnp.float32
    bsz, s, _ = hn.shape
    proj = hn @ w_in
    z, xbc, dt_raw = jnp.split(proj, [SSD_INNER, SSD_INNER + SSD_XBC], axis=-1)
    xbc = jax.nn.silu(depthwise_conv_centered(xbc, conv_w, conv_b))
    xs, bm, cm = jnp.split(xbc, [SSD_INNER, SSD_INNER + SSD_GROUPS * SSD_STATE], axis=-1)
    dt = jax.nn.softplus(dt_raw.astype(f32).reshape(bsz, s, 2, SSD_HEADS) + dt_bias.astype(f32))
    A = -jnp.exp(a_log.astype(f32))
    log_a = dt * A
    grp = (bsz, s, SSD_GROUPS, SSD_HPG)
    xh = xs.astype(f32).reshape(bsz, s, SSD_GROUPS, SSD_HPG, SSD_HEADDIM)
    v_f = xh * dt[:, :, 0].reshape(grp)[..., None]
    v_b = xh * dt[:, :, 1].reshape(grp)[..., None]
    qc = cm.reshape(bsz, s, SSD_GROUPS, SSD_STATE)
    kb = bm.reshape(bsz, s, SSD_GROUPS, SSD_STATE)
    y = bidir_scan(qc, kb, v_f, v_b, log_a[:, :, 0].reshape(grp), log_a[:, :, 1].reshape(grp))
    y = y + xh * d_skip.astype(f32).reshape(SSD_GROUPS, SSD_HPG)[..., None]
    y = y.reshape(bsz, s, SSD_INNER) * jax.nn.silu(z.astype(f32))
    yg = y.reshape(bsz, s, SSD_GROUPS, SSD_INNER // SSD_GROUPS)
    yg = yg * lax.rsqrt(jnp.mean(yg * yg, axis=-1, keepdims=True) + EPS)
    y = yg.reshape(bsz, s, SSD_INNER) * norm_g.astype(f32)
    return y.astype(hn.dtype) @ w_out

def conv_geglu_ffn(hn, w_up, conv_w, conv_b, w_down):
    u = depthwise_conv_centered(hn @ w_up, conv_w, conv_b)
    gate, val = jnp.split(u, 2, axis=-1)
    return (jax.nn.gelu(gate, approximate=True) * val) @ w_down

def first_inputs(seed: int = 0) -> dict:
    key = jax.random.key(seed)
    ks = jax.random.split(key, 24)
    f32 = jnp.float32

    def nrm(k, shape, scale):
        return jax.random.normal(k, shape, f32) * scale

    def gain(k, shape):
        return 1.0 + 0.05 * jax.random.normal(k, shape, f32)

    x = nrm(ks[0], (BATCH, SEQ, D_MODEL), 1.0)
    norm_mix_pre = gain(ks[1], (DEPTH, D_MODEL))
    norm_mix_post = gain(ks[2], (DEPTH, D_MODEL))
    norm_ffn_pre = gain(ks[3], (DEPTH, D_MODEL))
    norm_ffn_post = gain(ks[4], (DEPTH, D_MODEL))
    ab_w_in = nrm(ks[5], (N_EVEN, D_MODEL, AB_IN_DIM), D_MODEL ** -0.5)
    gamma0 = 1.0 - 2.0 ** (-5.0 - jnp.arange(RET_HEADS, dtype=f32))
    ab_ret_decay_logit = (jnp.log(gamma0) - jnp.log1p(-gamma0))[None, None, :] + nrm(ks[6], (N_EVEN, 2, RET_HEADS), 0.05)
    ab_ret_gn_g = gain(ks[7], (N_EVEN, RET_WIDTH))
    ab_na_rpb = nrm(ks[8], (N_EVEN, NA_HEADS, 2 * NA_WIN_R - 1, 2 * NA_WIN_C - 1), 0.1)
    ab_w_out = nrm(ks[9], (N_EVEN, RET_WIDTH + NA_WIDTH, D_MODEL), (RET_WIDTH + NA_WIDTH) ** -0.5)
    c_w_in = nrm(ks[10], (N_ODD, D_MODEL, SSD_IN_DIM), D_MODEL ** -0.5)
    c_conv_w = nrm(ks[11], (N_ODD, SSD_CONV, SSD_XBC), SSD_CONV ** -0.5)
    c_conv_b = nrm(ks[12], (N_ODD, SSD_XBC), 0.02)
    dt0 = jnp.exp(jax.random.uniform(ks[13], (N_ODD, 2, SSD_HEADS), f32, math.log(1e-3), math.log(1e-1)))
    c_dt_bias = dt0 + jnp.log(-jnp.expm1(-dt0))
    c_a_log = jnp.log(jax.random.uniform(ks[14], (N_ODD, 2, SSD_HEADS), f32, 1.0, 16.0))
    c_d_skip = 1.0 + 0.1 * jax.random.normal(ks[15], (N_ODD, SSD_HEADS), f32)
    c_norm_g = gain(ks[16], (N_ODD, SSD_INNER))
    c_w_out = nrm(ks[17], (N_ODD, SSD_INNER, D_MODEL), SSD_INNER ** -0.5)
    ffn_w_up = nrm(ks[18], (DEPTH, D_MODEL, 2 * FFN_DIM), D_MODEL ** -0.5)
    ffn_conv_w = nrm(ks[19], (DEPTH, FFN_CONV, 2 * FFN_DIM), FFN_CONV ** -0.5)
    ffn_conv_b = nrm(ks[20], (DEPTH, 2 * FFN_DIM), 0.02)
    ffn_w_down = nrm(ks[21], (DEPTH, FFN_DIM, D_MODEL), FFN_DIM ** -0.5)
    return {'x': x, 'norm_mix_pre': norm_mix_pre, 'norm_mix_post': norm_mix_post,
            'norm_ffn_pre': norm_ffn_pre, 'norm_ffn_post': norm_ffn_post,
            'ab_w_in': ab_w_in, 'ab_ret_decay_logit': ab_ret_decay_logit, 'ab_ret_gn_g': ab_ret_gn_g,
            'ab_na_rpb': ab_na_rpb, 'ab_w_out': ab_w_out,
            'c_w_in': c_w_in, 'c_conv_w': c_conv_w, 'c_conv_b': c_conv_b, 'c_dt_bias': c_dt_bias,
            'c_a_log': c_a_log, 'c_d_skip': c_d_skip, 'c_norm_g': c_norm_g, 'c_w_out': c_w_out,
            'ffn_w_up': ffn_w_up, 'ffn_conv_w': ffn_conv_w, 'ffn_conv_b': ffn_conv_b, 'ffn_w_down': ffn_w_down}

def first_block(x, norm_mix_pre, norm_mix_post, norm_ffn_pre, norm_ffn_post,
              ab_w_in, ab_ret_decay_logit, ab_ret_gn_g, ab_na_rpb, ab_w_out,
              c_w_in, c_conv_w, c_conv_b, c_dt_bias, c_a_log, c_d_skip, c_norm_g, c_w_out,
              ffn_w_up, ffn_conv_w, ffn_conv_b, ffn_w_down):
    for layer in range(DEPTH):
        i = layer // 2
        hn = rms_norm(x, norm_mix_pre[layer])
        if layer % 2 == 0:
            m = retention_na_mixer(hn, ab_w_in[i], ab_ret_decay_logit[i], ab_ret_gn_g[i], ab_na_rpb[i], ab_w_out[i])
        else:
            m = ssd_mixer(hn, c_w_in[i], c_conv_w[i], c_conv_b[i], c_dt_bias[i], c_a_log[i],
                          c_d_skip[i], c_norm_g[i], c_w_out[i])
        x = x + rms_norm(m, norm_mix_post[layer])
        f = conv_geglu_ffn(rms_norm(x, norm_ffn_pre[layer]), ffn_w_up[layer], ffn_conv_w[layer],
                           ffn_conv_b[layer], ffn_w_down[layer])
        x = x + rms_norm(f, norm_ffn_post[layer])
    return x


DEPTH_2 = 1

HEAD_DIM = 64
MOBA_HEADS = 8
NSA_HEADS = 8
NSA_GROUPS = 2
NSA_HPG = NSA_HEADS // NSA_GROUPS
N_HEADS_TOTAL = MOBA_HEADS + NSA_HEADS
MOBA_WIDTH = MOBA_HEADS * HEAD_DIM
NSA_WIDTH = NSA_HEADS * HEAD_DIM
NSA_KV_WIDTH = NSA_GROUPS * HEAD_DIM
MOBA_BLOCK = 256
MOBA_TOPK = 3
CMP_LEN = 32
CMP_STRIDE = 16
CMP_HIDDEN = 256
SEL_BLOCK = 64
SEL_TOPN = 16
WINDOW = 512
NUM_BUCKETS = 32
MAX_DISTANCE = 1024
Q_CHUNK = 64
NEG = -1e30
BIG = 1e30
SPLIT_SIZES = (MOBA_WIDTH, MOBA_WIDTH, MOBA_WIDTH, MOBA_WIDTH, NSA_WIDTH, NSA_KV_WIDTH, NSA_KV_WIDTH, NSA_KV_WIDTH, NSA_KV_WIDTH, NSA_KV_WIDTH, NSA_KV_WIDTH, 3 * NSA_HEADS, NSA_WIDTH, 2 * D_MODEL)
IN_WIDTH = sum(SPLIT_SIZES)


def rms_norm_2(x, g):
    xf = x.astype(jnp.float32)
    y = xf * lax.rsqrt(jnp.mean(xf * xf, axis=-1, keepdims=True) + EPS)
    return (y * g.astype(jnp.float32)).astype(x.dtype)

def t5_bucket(dist):
    n = jnp.maximum(dist, 0)
    max_exact = NUM_BUCKETS // 2
    nf = jnp.maximum(n, max_exact).astype(jnp.float32)
    large = max_exact + (jnp.log(nf / max_exact) / math.log(MAX_DISTANCE / max_exact) * (NUM_BUCKETS - max_exact)).astype(jnp.int32)
    return jnp.where(n < max_exact, n, jnp.minimum(large, NUM_BUCKETS - 1))

def moba_mixer(q, k, v, bias_tab):
    B, S, H, Dh = q.shape
    scale = 1.0 / math.sqrt(Dh)
    nb = -(-S // MOBA_BLOCK)
    pad = nb * MOBA_BLOCK - S
    padw = ((0, 0), (0, pad), (0, 0), (0, 0))
    kb = jnp.pad(k, padw).reshape(B, nb, MOBA_BLOCK, H, Dh).transpose(0, 3, 1, 2, 4)
    vb = jnp.pad(v, padw).reshape(B, nb, MOBA_BLOCK, H, Dh).transpose(0, 3, 1, 2, 4)
    qh = q.transpose(0, 2, 1, 3)
    kmean = jnp.mean(kb.astype(jnp.float32), axis=3)
    score = jnp.einsum('bhsd,bhjd->bhsj', qh.astype(jnp.float32), kmean)
    qblk = jnp.arange(S)[:, None] // MOBA_BLOCK
    blk = jnp.arange(nb)[None, :]
    score = jnp.where(blk == qblk, BIG, jnp.where(blk < qblk, score, NEG))
    _, sel = lax.top_k(score, min(MOBA_TOPK + 1, nb))
    bi = jnp.arange(B)[:, None, None, None]
    hi = jnp.arange(H)[None, :, None, None]
    offs = jnp.arange(MOBA_BLOCK)

    def one_chunk(c):
        t0 = c * Q_CHUNK
        tq = t0 + jnp.arange(Q_CHUNK)
        qc = lax.dynamic_slice_in_dim(qh, t0, Q_CHUNK, axis=2)
        sc = lax.dynamic_slice_in_dim(sel, t0, Q_CHUNK, axis=2)
        kg = kb[bi, hi, sc]
        vg = vb[bi, hi, sc]
        logits = jnp.einsum('bhqd,bhqnkd->bhqnk', qc, kg).astype(jnp.float32) * scale
        dist = tq[:, None, None] - (sc[..., None] * MOBA_BLOCK + offs)
        bias = bias_tab[hi[..., None], t5_bucket(dist)]
        logits = jnp.where(dist >= 0, logits + bias, NEG)
        p = jax.nn.softmax(logits.reshape(B, H, Q_CHUNK, -1), axis=-1).astype(v.dtype)
        return jnp.einsum('bhqm,bhqmd->bhqd', p, vg.reshape(B, H, Q_CHUNK, -1, Dh))

    out = lax.map(one_chunk, jnp.arange(S // Q_CHUNK))
    return out.transpose(1, 0, 3, 2, 4).reshape(B, S, H * Dh)

def compress(kv, pos, w1, w2):
    B, S, G, Dh = kv.shape
    nc = (S - CMP_LEN) // CMP_STRIDE + 1
    idx = np.arange(nc)[:, None] * CMP_STRIDE + np.arange(CMP_LEN)[None, :]
    win = kv[:, idx] + pos[None, None, :, None, :]
    win = win.transpose(0, 1, 3, 2, 4).reshape(B, nc, G, CMP_LEN * Dh)
    return jax.nn.gelu(win @ w1) @ w2

def nsa_mixer(q, k_cmp, v_cmp, k_sel, v_sel, k_win, v_win, branch_gate, bias_tab):
    B, S, H, Dh = q.shape
    G = NSA_GROUPS
    HPG = H // G
    scale = 1.0 / math.sqrt(Dh)
    qg = q.reshape(B, S, G, HPG, Dh).transpose(0, 2, 3, 1, 4)
    nc = k_cmp.shape[1]
    tpos = jnp.arange(S)
    lc = jnp.einsum('bghsd,bcgd->bghsc', qg, k_cmp).astype(jnp.float32) * scale
    cend = jnp.arange(nc) * CMP_STRIDE + CMP_LEN - 1
    cvalid = cend[None, :] <= tpos[:, None]
    p_cmp = jax.nn.softmax(jnp.where(cvalid, lc, NEG), axis=-1) * cvalid
    o_cmp = jnp.einsum('bghsc,bcgd->bghsd', p_cmp.astype(v_cmp.dtype), v_cmp)
    nsel = S // SEL_BLOCK
    cs = np.arange(nc) * CMP_STRIDE
    bs = np.arange(nsel) * SEL_BLOCK
    ov = ((cs[None, :] < bs[:, None] + SEL_BLOCK) & (cs[None, :] + CMP_LEN > bs[:, None])).astype(np.float32)
    imp = jnp.einsum('bghsc,jc->bgsj', p_cmp, jnp.asarray(ov))
    qblk = tpos[:, None] // SEL_BLOCK
    blk = jnp.arange(nsel)[None, :]
    imp = jnp.where((blk == qblk) | (blk == 0), BIG, jnp.where(blk < qblk, imp, NEG))
    _, sel = lax.top_k(imp, min(SEL_TOPN, nsel))
    ksb = k_sel.reshape(B, nsel, SEL_BLOCK, G, Dh).transpose(0, 3, 1, 2, 4)
    vsb = v_sel.reshape(B, nsel, SEL_BLOCK, G, Dh).transpose(0, 3, 1, 2, 4)
    padw = ((0, 0), (WINDOW, 0), (0, 0), (0, 0))
    kwp = jnp.pad(k_win, padw).transpose(0, 2, 1, 3)
    vwp = jnp.pad(v_win, padw).transpose(0, 2, 1, 3)
    tab_g = bias_tab.reshape(G, HPG, NUM_BUCKETS)
    bi = jnp.arange(B)[:, None, None, None]
    gi = jnp.arange(G)[None, :, None, None]
    g6 = jnp.arange(G)[None, :, None, None, None, None]
    h6 = jnp.arange(HPG)[None, None, :, None, None, None]
    offs = jnp.arange(SEL_BLOCK)

    def one_chunk(c):
        t0 = c * Q_CHUNK
        tq = t0 + jnp.arange(Q_CHUNK)
        qc = lax.dynamic_slice_in_dim(qg, t0, Q_CHUNK, axis=3)
        sc = lax.dynamic_slice_in_dim(sel, t0, Q_CHUNK, axis=2)
        kg = ksb[bi, gi, sc]
        vg = vsb[bi, gi, sc]
        ls = jnp.einsum('bghqd,bgqnkd->bghqnk', qc, kg).astype(jnp.float32) * scale
        dist = tq[:, None, None] - (sc[..., None] * SEL_BLOCK + offs)
        bias = tab_g[g6, h6, t5_bucket(dist)[:, :, None]]
        ls = jnp.where(dist[:, :, None] >= 0, ls + bias, NEG)
        ps = jax.nn.softmax(ls.reshape(B, G, HPG, Q_CHUNK, -1), axis=-1).astype(v_sel.dtype)
        o_sel = jnp.einsum('bghqm,bgqmd->bghqd', ps, vg.reshape(B, G, Q_CHUNK, -1, Dh))
        kwc = lax.dynamic_slice_in_dim(kwp, t0, Q_CHUNK + WINDOW, axis=2)
        vwc = lax.dynamic_slice_in_dim(vwp, t0, Q_CHUNK + WINDOW, axis=2)
        kpos = t0 - WINDOW + jnp.arange(Q_CHUNK + WINDOW)
        dw = tq[:, None] - kpos[None, :]
        wvalid = (dw >= 0) & (dw < WINDOW) & (kpos[None, :] >= 0)
        lw = jnp.einsum('bghqd,bgkd->bghqk', qc, kwc).astype(jnp.float32) * scale + tab_g[:, :, t5_bucket(dw)]
        pw = jax.nn.softmax(jnp.where(wvalid, lw, NEG), axis=-1).astype(v_win.dtype)
        o_win = jnp.einsum('bghqk,bgkd->bghqd', pw, vwc)
        return o_sel, o_win

    o_sel, o_win = lax.map(one_chunk, jnp.arange(S // Q_CHUNK))
    o_sel = o_sel.transpose(1, 2, 3, 0, 4, 5).reshape(B, G, HPG, S, Dh)
    o_win = o_win.transpose(1, 2, 3, 0, 4, 5).reshape(B, G, HPG, S, Dh)
    g = jax.nn.sigmoid(branch_gate.astype(jnp.float32)).astype(q.dtype)
    g = g.reshape(B, S, G, HPG, 3).transpose(0, 2, 3, 1, 4)
    o = g[..., 0:1] * o_cmp + g[..., 1:2] * o_sel + g[..., 2:3] * o_win
    return o.transpose(0, 3, 1, 2, 4).reshape(B, S, H * Dh)

def second_inputs(seed: int = 0) -> dict:
    key = jax.random.key(seed)
    ks = jax.random.split(key, 19)

    def normal(k, shape, s):
        return jax.random.normal(k, shape, jnp.float32) * s

    def gain(k, shape):
        return 1.0 + 0.1 * jax.random.normal(k, shape, jnp.float32)

    L = DEPTH_2
    flat = CMP_LEN * HEAD_DIM
    return {
        'x': normal(ks[0], (BATCH, SEQ, D_MODEL), 1.0),
        'norm_w': gain(ks[1], (L, D_MODEL)),
        'w_in': normal(ks[2], (L, D_MODEL, IN_WIDTH), D_MODEL ** -0.5),
        'q_norm_a': gain(ks[3], (L, HEAD_DIM)),
        'k_norm_a': gain(ks[4], (L, HEAD_DIM)),
        'q_norm_b': gain(ks[5], (L, HEAD_DIM)),
        'k_norm_cmp': gain(ks[6], (L, HEAD_DIM)),
        'k_norm_sel': gain(ks[7], (L, HEAD_DIM)),
        'k_norm_win': gain(ks[8], (L, HEAD_DIM)),
        'cmp_pos_k': normal(ks[9], (L, CMP_LEN, HEAD_DIM), 0.1),
        'cmp_w1_k': normal(ks[10], (L, flat, CMP_HIDDEN), flat ** -0.5),
        'cmp_w2_k': normal(ks[11], (L, CMP_HIDDEN, HEAD_DIM), CMP_HIDDEN ** -0.5),
        'cmp_pos_v': normal(ks[12], (L, CMP_LEN, HEAD_DIM), 0.1),
        'cmp_w1_v': normal(ks[13], (L, flat, CMP_HIDDEN), flat ** -0.5),
        'cmp_w2_v': normal(ks[14], (L, CMP_HIDDEN, HEAD_DIM), CMP_HIDDEN ** -0.5),
        'rel_bias': normal(ks[15], (NUM_BUCKETS, N_HEADS_TOTAL), 0.5),
        'w_branch_a': normal(ks[16], (L, MOBA_WIDTH, D_MODEL), MOBA_WIDTH ** -0.5),
        'w_branch_b': normal(ks[17], (L, NSA_WIDTH, D_MODEL), NSA_WIDTH ** -0.5),
        'w_out': normal(ks[18], (L, D_MODEL, D_MODEL), D_MODEL ** -0.5),
    }

def second_block(x, norm_w, w_in, q_norm_a, k_norm_a, q_norm_b, k_norm_cmp, k_norm_sel, k_norm_win,
              cmp_pos_k, cmp_w1_k, cmp_w2_k, cmp_pos_v, cmp_w1_v, cmp_w2_v, rel_bias,
              w_branch_a, w_branch_b, w_out):
    B, S, _ = x.shape
    split_points = [int(p) for p in np.cumsum(SPLIT_SIZES)[:-1]]
    bias_tab = rel_bias.T
    bias_a = bias_tab[:MOBA_HEADS]
    bias_b = bias_tab[MOBA_HEADS:]

    def heads(t):
        return t.reshape(B, S, -1, HEAD_DIM)

    for l in range(DEPTH_2):
        h = rms_norm_2(x, norm_w[l])
        proj = h @ w_in[l]
        (q_a, k_a, v_a, z_a, q_b, kc, vc, ksl, vsl, kwn, vwn, gate_b, z_b, gate_m) = jnp.split(proj, split_points, axis=-1)
        o_a = moba_mixer(rms_norm_2(heads(q_a), q_norm_a[l]), rms_norm_2(heads(k_a), k_norm_a[l]), heads(v_a), bias_a)
        k_cmp = rms_norm_2(compress(heads(kc), cmp_pos_k[l], cmp_w1_k[l], cmp_w2_k[l]), k_norm_cmp[l])
        v_cmp = compress(heads(vc), cmp_pos_v[l], cmp_w1_v[l], cmp_w2_v[l])
        o_b = nsa_mixer(rms_norm_2(heads(q_b), q_norm_b[l]), k_cmp, v_cmp,
                        rms_norm_2(heads(ksl), k_norm_sel[l]), heads(vsl),
                        rms_norm_2(heads(kwn), k_norm_win[l]), heads(vwn),
                        gate_b.reshape(B, S, NSA_HEADS, 3), bias_b)
        y_a = o_a * jax.nn.silu(z_a)
        y_b = o_b * jax.nn.silu(z_b)
        g_m = jax.nn.sigmoid(gate_m)
        merged = g_m[..., :D_MODEL] * (y_a @ w_branch_a[l]) + g_m[..., D_MODEL:] * (y_b @ w_branch_b[l])
        x = x + merged @ w_out[l]
    return x


def setup_inputs(seed=0):
    out = dict(first_inputs(seed))
    for name, value in second_inputs(seed + 1).items():
        if name != "x":
            out[name + "_2"] = value
    return out


def reference(
    x, norm_mix_pre, norm_mix_post, norm_ffn_pre, norm_ffn_post, ab_w_in, ab_ret_decay_logit,
    ab_ret_gn_g, ab_na_rpb, ab_w_out, c_w_in, c_conv_w, c_conv_b, c_dt_bias, c_a_log, c_d_skip,
    c_norm_g, c_w_out, ffn_w_up, ffn_conv_w, ffn_conv_b, ffn_w_down, norm_w_2, w_in_2,
    q_norm_a_2, k_norm_a_2, q_norm_b_2, k_norm_cmp_2, k_norm_sel_2, k_norm_win_2, cmp_pos_k_2,
    cmp_w1_k_2, cmp_w2_k_2, cmp_pos_v_2, cmp_w1_v_2, cmp_w2_v_2, rel_bias_2, w_branch_a_2,
    w_branch_b_2, w_out_2,
):
    x = first_block(
        x, norm_mix_pre, norm_mix_post, norm_ffn_pre, norm_ffn_post, ab_w_in,
        ab_ret_decay_logit, ab_ret_gn_g, ab_na_rpb, ab_w_out, c_w_in, c_conv_w, c_conv_b,
        c_dt_bias, c_a_log, c_d_skip, c_norm_g, c_w_out, ffn_w_up, ffn_conv_w, ffn_conv_b,
        ffn_w_down,
    )
    return second_block(
        x, norm_w_2, w_in_2, q_norm_a_2, k_norm_a_2, q_norm_b_2, k_norm_cmp_2, k_norm_sel_2,
        k_norm_win_2, cmp_pos_k_2, cmp_w1_k_2, cmp_w2_k_2, cmp_pos_v_2, cmp_w1_v_2, cmp_w2_v_2,
        rel_bias_2, w_branch_a_2, w_branch_b_2, w_out_2,
    )


_drawn_inputs = setup_inputs


def setup_inputs(seed=0):
    import zlib

    import numpy as np

    out = dict(_drawn_inputs(seed))
    spreads = {}
    factors = {'c_conv_b': 3.436,
     'norm_w_2': 5.67,
     'q_norm_a_2': 8.0,
     'k_norm_a_2': 8.0,
     'q_norm_b_2': 8.0,
     'k_norm_cmp_2': 8.0,
     'k_norm_sel_2': 8.0,
     'k_norm_win_2': 8.0,
     'cmp_pos_k_2': 8.0,
     'cmp_w1_k_2': 4.325,
     'cmp_w2_k_2': 4.534,
     'cmp_pos_v_2': 8.0,
     'rel_bias_2': 3.754}
    for name, (base, spread) in spreads.items():
        noise = np.random.default_rng([zlib.crc32(name.encode()), seed]).standard_normal(out[name].shape)
        drawn = base * np.exp(spread * noise) if base else spread * noise
        out[name] = jnp.asarray(drawn.astype(out[name].dtype))
    for name, factor in factors.items():
        out[name] = (out[name] * factor).astype(out[name].dtype)
    return out
```

```python
from contextlib import ExitStack

import numpy as np

import concourse.bass as bass
from concourse import mybir

ALU = mybir.AluOpType
ACT = mybir.ActivationFunctionType
F32 = mybir.dt.float32
F32R = mybir.dt.float32r
AXX = mybir.AxisListType.X

P = 128
S = 256
NT = S // P
D = 1024
KD = D // P
EPS = 1e-6
NEG = -1e30
DH = 64
NH = 8
FF = 2816
FI = FF // 256
SI = 2048
SG = 4
SHG = 8
XBC = SI + 2 * SG * P
CL, CS, NCMP = 32, 16, 15
GW = 64
NRAW, NHI, NLO = 4, 3, 3
SLOT = 2048


class Counts:

    def __init__(self, nc, ctx, known):
        self.nc, self.ctx, self.known = nc, ctx, known
        self.sems, self.count, self.marks = {}, {}, {}

    def sem(self, family):
        if family not in self.sems:
            self.sems[family] = self.ctx.enter_context(self.nc.semaphore(family))
            self.count[family] = 0
        return self.sems[family]

    def done(self, family, key=0, by=1):
        s = self.sem(family)
        self.count[family] += by
        assert (family, key) not in self.marks or by == 16, (family, key)
        self.marks[(family, key)] = self.count[family]
        return s, by

    def at(self, family, key=0):
        s = self.sem(family)
        if self.known is None:
            return s, max(1, self.marks.get((family, key), 1))
        return s, self.known[(family, key)]


def bc(ap, axis, n):
    a = ap.unsqueeze(axis)
    shape = list(a.shape)
    shape[axis] = n
    return a.to_broadcast(shape)


def shape_constants():
    i = np.arange(P)
    ident = np.eye(P)
    u, t = i[:, None], i[None, :]
    le, gt, lt, ge = (u <= t), (u > t), (u < t), (u >= t)
    half = DH // 2
    inv = (1.0 / (np.float32(10000.0) ** (np.arange(half, dtype=np.float32) / np.float32(half)))).astype(np.float32)
    ang = (np.arange(S, dtype=np.float32)[:, None] * inv[None, :]).astype(np.float32).astype(np.float64)
    cos = np.concatenate([np.cos(ang), np.cos(ang)], 1).reshape(NT, P, DH).transpose(1, 0, 2).reshape(P, -1)
    sin = np.concatenate([-np.sin(ang), np.sin(ang)], 1).reshape(NT, P, DH).transpose(1, 0, 2).reshape(P, -1)
    s_all = (np.arange(NT)[None, :, None] * P + i[:, None, None])
    dist = np.arange(S)[None, None, :] - s_all
    pf, pb = np.maximum(dist, 0).reshape(P, -1), np.maximum(-dist, 0).reshape(P, -1)
    qc = i % GW
    kc = np.arange(GW)
    c0 = np.clip(qc - 8, 0, GW - 16)[:, None]
    nm = np.where((kc[None] >= c0) & (kc[None] < c0 + 16), 0.0, NEG)
    tok = (np.arange(NT)[None, :, None] * P + i[:, None, None])
    cend = np.arange(16)[None, None, :] * CS + CL - 1
    cv = (cend <= tok) & (np.arange(16)[None, None, :] < NCMP)
    cneg = np.where(cv, 0.0, NEG).reshape(P, -1)
    blk = (i[:, None] // 16 == np.arange(8)[None, :])
    parts = [("ident", ident), ("le", le), ("gt", gt), ("lt", lt), ("ge", ge), ("cos", cos), ("sin", sin),
             ("nm", nm), ("cneg", cneg), ("cval", cv.reshape(P, -1)), ("blk", blk)]
    at, n = {}, 0
    for name, a in parts:
        at[name] = (n, n + a.shape[1])
        n += a.shape[1]
    table = np.concatenate([a.astype(np.float32) for _, a in parts], 1)
    pfb = np.concatenate([pf, pb], 1).astype(np.float32)
    dd = 255 - np.arange(384)
    n_ = np.maximum(dd, 0)
    nf = np.maximum(n_, 16).astype(np.float32)
    large = 16 + (np.log(nf / np.float32(16)) / np.float32(np.log(64.0)) * np.float32(16)).astype(np.int32)
    bucket = np.where(n_ < 16, n_, np.minimum(large, 31))
    onehot = ((np.arange(32)[:, None] == bucket[None, :]) & (dd[None, :] >= 0)).astype(np.float32)
    negs = np.tile(np.where(dd >= 0, 0.0, NEG)[None, :], (16, 1)).astype(np.float32)
    return at, table, pfb, onehot, negs


CONST_AT, CONST_TABLE, CONST_PFB, CONST_ONEHOT, CONST_NEGS = shape_constants()
NCONST = CONST_TABLE.shape[1]


def vector_rows(I):
    r = lambda ap: ap.rearrange("(k p) -> k p", p=P)
    rows = []
    for l in range(2):
        rows.append((f"mix{l}", r(I["norm_mix_pre"][l])))
        rows.append((f"ffn{l}", r(I["norm_ffn_pre"][l])))
    rows.append(("sec", r(I["norm_w_2"][0])))
    rows.append(("gn", r(I["ab_ret_gn_g"][0])))
    rows.append(("ssdn", r(I["c_norm_g"][0])))
    rows.append(("posk", I["cmp_pos_k_2"][0].rearrange("(j r) d -> j (r d)", r=2)))
    rows.append(("posv", I["cmp_pos_v_2"][0].rearrange("(j r) d -> j (r d)", r=2)))
    for k in range(5):
        rows.append((f"cw{k}", r(I["c_conv_w"][0, k])))
    rows.append(("cb", r(I["c_conv_b"][0])))
    for l in range(2):
        for k in range(3):
            rows.append((f"fw{l}{k}", r(I["ffn_conv_w"][l, k])))
        rows.append((f"fb{l}", r(I["ffn_conv_b"][l])))
    return rows


def build(nc, I, out, known):
    ctx = ExitStack()
    with ctx:
        C = Counts(nc, ctx, known)
        done, at = C.done, C.at

        def sb(name, shape, dt=F32):
            return ctx.enter_context(nc.sbuf_tensor(name, shape, dt))

        PS = ctx.enter_context(nc.psum_tensor("PS", [P, 8, 512], F32))
        x = sb("x", [P, NT, D])
        hn = sb("hn", [P, NT, D])
        Th = sb("Th", [P, 16, S], F32R)
        Tl = sb("Tl", [P, 16, S], F32R)
        aTh = sb("aTh", [P, 2, 2, S], F32R)
        aTl = sb("aTl", [P, 2, 2, S], F32R)
        raw = [sb(f"raw{i}", [P, SLOT]) for i in range(NRAW)]
        whi = [sb(f"whi{i}", [P, SLOT], F32R) for i in range(NHI)]
        wlo = [sb(f"wlo{i}", [P, SLOT], F32R) for i in range(NLO)]
        gpost = sb("gpost", [P, D])
        cst = sb("cst", [P, NCONST])
        rows = vector_rows(I)
        col_at, n = {}, 0
        for name, ap in rows:
            k = ap.shape[0]
            if n % P + k > P:
                n += P - n % P
            col_at[name] = n
            n += k
        NR = -(-(n + 1) // P)
        qn = NR * P
        cols = sb("cols", [P, NR * P + 8])
        st = sb("st", [P, 160])
        eps = sb("eps", [P, 1])
        A = sb("arena", [P, 15000])

        def cc(name):
            a, b = CONST_AT[name]
            return cst[:, a:b]

        ident = cc("ident")

        def col(name, j=0):
            c = col_at[name] + j
            return cols[:, c:c + 1]

        slots, slot_no = [], {}

        def add(name, parts, width):
            slot_no[name] = len(slots)
            slots.append((parts, width))

        def wide(name, w, k0, c0, nk, nc_):
            add(name, [((nk, nc_, 0, nc_), w[k0 * P:(k0 + nk) * P, c0:c0 + nc_])], nk * nc_)

        def tm(name, w, c0, k0=0):
            for hf in range(2):
                wide((name, hf), w, k0 + 4 * hf, c0, 4, 512)

        def fm(name, w, c0, k0=0, j=0):
            wide((name, j), w, k0, c0, 8, 256)

        def dn(name, w, n, k0=0):
            for j in range(n):
                wide((name, j), w, k0 + 2 * j, 0, 2, 1024)

        def ffn_slots(l):
            up, down = I["ffn_w_up"][l], I["ffn_w_down"][l]
            for i in range(FI + 1):
                if i < FI:
                    wide(("G", l, i), up, 0, 256 * i, 8, 256)
                    wide(("V", l, i), up, 0, FF + 256 * i, 8, 256)
                if i >= 1:
                    wide(("D", l, i - 1), down, 2 * (i - 1), 0, 2, 1024)

        win = I["ab_w_in"][0]
        tm("rq", win, 0)
        tm("rk", win, 512)
        tm("rv", win, 1024)
        for j in range(2):
            fm("nq", win, 2048 + 256 * j, j=j)
        for j in range(2):
            fm("nk", win, 2560 + 256 * j, j=j)
        tm("nv", win, 3072)
        tm("rg", win, 1536)
        dn("mo0", I["ab_w_out"][0], 4)
        ffn_slots(0)
        cwin = I["c_w_in"][0]
        wide(("dt", 0), cwin, 0, SI + XBC, 8, 64)
        for g in range(SG):
            tm(("z", g), cwin, 512 * g)
            for j in range(2):
                fm(("xs", g), cwin, SI + 512 * g + 256 * j, j=j)
            add((("bc", g), 0), [((8, 256, 128 * m, 128 * m + 128),
                                  cwin[:, 2 * SI + 512 * m + P * g:2 * SI + 512 * m + P * (g + 1)]) for m in range(2)],
                SLOT)
        dn("mo1", I["c_w_out"][0], 8)
        ffn_slots(1)
        w2 = I["w_in_2"][0]
        KV = 2560
        tm("qa", w2, 0)
        tm("ka", w2, 512)
        tm("va", w2, 1024)
        tm("qb", w2, 2048)
        for n, nm in enumerate(("kc", "vc")):
            add((nm, 0), [((8, 256, 128 * g + 64 * r, 128 * g + 64 * r + 64),
                           w2[:, KV + 128 * n + 64 * g:KV + 128 * n + 64 * g + 64])
                          for g in range(2) for r in range(2)], SLOT)
        tm("ksv", w2, KV + 256)
        wide(("gb", 0), w2, 0, KV + 768, 8, 24)
        tm("za", w2, 1536)
        tm("zb", w2, KV + 792)
        for nm in ("k", "v"):
            for j in range(2):
                fm("w1" + nm, I["cmp_w1_" + nm + "_2"][0], 0, k0=8 * j, j=j)
        GM = KV + 792 + 512
        for n in range(2):
            tm(("GA", n), w2, GM + 512 * n)
            tm(("GB", n), w2, GM + D + 512 * n)
            wide((("YA", n), 0), I["w_branch_a_2"][0], 0, 512 * n, 4, 512)
            wide((("YB", n), 0), I["w_branch_b_2"][0], 0, 512 * n, 4, 512)
        dn("fo", I["w_out_2"][0], 4)
        NS = len(slots)

        def view(a, *shape):
            n = int(np.prod(shape))
            v = A[:, a:a + n]
            if len(shape) == 2:
                v = v.rearrange("p (a b) -> p a b", a=shape[0])
            elif len(shape) == 3:
                v = v.rearrange("p (a b c) -> p a b c", a=shape[0], b=shape[1])
            return v

        rqk = [view(1024 * i, NT, 512) for i in range(2)]
        nabias = view(0, NH, 6 * GW)
        rv, rg, nv = (view(3072 + 1024 * i, NT, 512) for i in range(3))
        rqT, rkT, nqT, nkT = (view(6144 + 1024 * i, 4, S) for i in range(4))
        pfb = view(10240, 2, 512)
        dcy = [view(11264 + 512 * i, 512) for i in range(2)]
        msc = [view(12288 + 512 * i, 512) for i in range(2)]
        spxs = {"ret": view(13400, 8, 16), "ssd": view(8448, 8, 128)}
        lg = A[:, 14500:14516]
        brow = A[:, 14516:14532]
        zt = [view(1024 * i, NT, 512) for i in range(2)]
        xs = [view(2048 + 1024 * i, NT, 512) for i in range(2)]
        bct = [view(4096 + 512 * i, 2, S) for i in range(2)]
        btm = view(5120, NT, P)
        vfb = view(5376, 2, NT, 512)
        vt = view(7424, 2, 512)
        am = [view(8448 + 512 * i, 4, P) for i in range(2)]
        ee = [view(9472 + 512 * i, 4, P) for i in range(2)]
        cvb = view(10496, 6, S)
        qk = view(12032, 2, NT, P)
        stt = view(12544, 2, 512)
        dtt = view(13568, 12, 64)
        ssx = view(14336, 0 or 1, 512)
        qaT, kaT, qbT = (view(1024 * i, 4, S) for i in range(3))
        va, za, zb = (view(3072 + 1024 * i, NT, 512) for i in range(3))
        kswT = view(6144, 4, S)
        vsw = view(7168, NT, 2, P)
        tb = view(7680, NH, S)
        sqb = view(9728, NT, 512)
        XC = [view(10752 + 512 * i, 16, 32) for i in range(2)]
        sc = [view(10752 + 512 * i, NT, S) for i in range(2)]
        pt = [view(11776 + 512 * i, 4, P) for i in range(2)]
        hid = view(12800, 2, 2, 32)
        hidr = view(12928, 2, P)
        vbd = view(13184, 8, DH)
        kcm = view(13696, 2, P)
        kcT = view(13952, 32)
        w2c = view(13984, 2, 2, DH)
        gb = view(14240, NT, 24)
        cpr = view(14300, NT, P)
        cpt = view(14560, NT, P)
        sg = [view(1024 * i, NT, 512) for i in range(2)]
        fac = [view(1024 * i, 4, S) for i in range(2)]
        fpr = [view(2048 + 512 * i, 2, S) for i in range(2)]
        rowb = view(0, NR + 1, P)
        oneh = A[0:32, 1024:1408]
        negs = A[0:16, 1408:1792]
        relb = A[0:32, 1792:1808]
        t5r = A[0:16, 13600:13984]

        chain = {}

        def link(eng, name, ins):
            chain[name] = chain.get(name, 0) + 1
            ins.then_inc(*done(name + "_chain", chain[name]))
            eng.wait_ge(*at(name + "_chain", chain[name]))

        def read(key):
            by_scalar = known is None or ("read_a", key) in known
            return at("read_a" if by_scalar else "read_v", key)

        toe = nc.dram_tensor("t5_rows", [16, P, 384], F32, kind="Internal").ap()
        narep = nc.dram_tensor("na_rows", [NH, GW, 465], F32, kind="Internal").ap()
        block = ctx.enter_context(nc.Block())

        @block.sync
        def _(sp):
            sp.dma_start(x[:, :, :], I["x"][0].rearrange("(t p) d -> p t d", p=P)).then_inc(*done("load_x", 0, 16))
            for n, (parts, width) in enumerate(slots):
                if n >= NRAW:
                    sp.wait_ge(*at("w_lo", n - NRAW))
                for (nk, nc_, a, b), src in parts:
                    dst = raw[n % NRAW][:, 0:nk * nc_].rearrange("p (k c) -> p k c", k=nk)[:, :, a:b]
                    sp.dma_start(dst, src.rearrange("(k p) c -> p k c", p=P))\
                        .then_inc(*done(f"w_raw{n % NRAW}", n, 16))
            sp.wait_ge(*at("x", (5, NT - 1)))
            sp.dma_start(out[0].rearrange("(t p) d -> p t d", p=P), x[:, :, :]).then_inc(*done("stored", 0, 16))
            sp.wait_ge(*at("stored", 0))

        @block.gpsimd
        def _(pool):
            for n, (parts, width) in enumerate(slots):
                pool.wait_ge(*at("w_hi", n))
                if n >= NLO:
                    pool.wait_ge(*at("w_used", n - NLO))
                nc.gpsimd.tensor_tensor(wlo[n % NLO][:, 0:width], raw[n % NRAW][:, 0:width],
                                        whi[n % NHI][:, 0:width].bitcast(F32), ALU.subtract)\
                    .then_inc(*done("w_lo", n))

        @block.tensor
        def _(pe):
            mm = nc.tensor.matmul

            def three(o, wh, wl, ah, al, first, last, moving_w):
                if moving_w:
                    mm(o, ah, wh, start=first, stop=False)
                    mm(o, ah, wl, start=False, stop=False)
                    return mm(o, al, wh, start=False, stop=last)
                mm(o, wh, ah, start=first, stop=False)
                mm(o, wh, al, start=False, stop=False)
                return mm(o, wl, ah, start=False, stop=last)

            def slot_tm(name, b0, kt0, first, last, ncol=512, nk=4):
                n = slot_no[name]
                pe.wait_ge(*at("w_lo", n))
                h, l = whi[n % NHI], wlo[n % NLO]
                for k in range(nk):
                    for t in range(NT):
                        i = three(PS[:, b0 + t, 0:ncol], h[:, k * ncol:(k + 1) * ncol], l[:, k * ncol:(k + 1) * ncol],
                                  Th[:, kt0 + k, t * P:(t + 1) * P], Tl[:, kt0 + k, t * P:(t + 1) * P],
                                  first and k == 0, last and k == nk - 1, True)
                i.then_inc(*done("w_used", n))

            def block_tm(name, b0):
                slot_tm((name, 0), b0, 0, True, False)
                slot_tm((name, 1), b0, 4, False, True)

            def slot_fm(name, b):
                n = slot_no[name]
                pe.wait_ge(*at("w_lo", n))
                h, l = whi[n % NHI], wlo[n % NLO]
                for m in range(2):
                    for k in range(KD):
                        c = k * 256 + m * P
                        i = three(PS[:, b, m * S:(m + 1) * S], h[:, c:c + P], l[:, c:c + P], Th[:, k, :], Tl[:, k, :],
                                  k == 0, k == KD - 1, False)
                i.then_inc(*done("w_used", n))

            def slot_dn(name, ah, al, first, last):
                n = slot_no[name]
                pe.wait_ge(*at("w_lo", n))
                h, l = whi[n % NHI], wlo[n % NLO]
                for k in range(2):
                    for t in range(NT):
                        for hf in range(2):
                            c = k * D + hf * 512
                            i = three(PS[:, 4 + 2 * t + hf, :], h[:, c:c + 512], l[:, c:c + 512], ah(k, t), al(k, t),
                                      first and k == 0, last and k == 1, True)
                i.then_inc(*done("w_used", n))

            def tr(o, src, idn):
                return nc.tensor.transpose(o, src, idn)

            def to_T(name, src, nk, b0):
                for k in range(nk):
                    for t in range(NT):
                        i = tr(PS[:, b0 + k // 2, (k % 2) * S + t * P:(k % 2) * S + (t + 1) * P],
                               src[:, t, k * P:(k + 1) * P], ident)
                    i.then_inc(*done("turned", (name, k)))

            def norm_T(l):
                pe.wait_ge(*at("n_hn", (l, NT - 1)))
                to_T(("n", l), hn, KD, 0)
                pe.wait_ge(*at("T_lo", (("n", l), KD - 1)))

            def out_proj(name, n, kt_of):
                for j in range(n):
                    slot_dn((name, j), lambda k, t: Th[:, kt_of(2 * j + k), t * P:(t + 1) * P],
                            lambda k, t: Tl[:, kt_of(2 * j + k), t * P:(t + 1) * P], j == 0, j == n - 1)

            def ffn(l):
                for i in range(FI + 1):
                    if i < FI:
                        if i >= 2:
                            pe.wait_ge(*at("f_conv", (l, i - 2)))
                        slot_fm(("G", l, i), 2 * (i % 2))
                        slot_fm(("V", l, i), 2 * (i % 2) + 1)
                    if i >= 1:
                        pe.wait_ge(*at("f_alo", (l, i - 1)))
                        p = (i - 1) % 2
                        slot_dn(("D", l, i - 1), lambda k, t: aTh[:, p, k, t * P:(t + 1) * P],
                                lambda k, t: aTl[:, p, k, t * P:(t + 1) * P], i == 1, i == FI)

            pe.wait_ge(*at("load_cst"))
            pe.wait_ge(*at("load_rows"))
            for r in range(NR):
                i = tr(PS[:, r // 4, (r % 4) * P:(r % 4 + 1) * P], rowb[:, r, :], ident)
            i = tr(PS[:, 3, 0:8], rowb[0:8, NR, :], ident[0:8, 0:8])
            pe.wait_ge(*at("load_t5"))
            mm(PS[0:16, 2, 0:384], relb, oneh, start=True, stop=True).then_inc(*done("set_up"))
            pe.wait_ge(*at("t5_sum"))
            pe.wait_ge(*at("cols"))

            norm_T(0)
            block_tm("rq", 0)
            block_tm("rk", 2)
            pe.wait_ge(*read(("rq", 1)))
            block_tm("rv", 0)
            for a, nm in enumerate(("rq", "rk")):
                pe.wait_ge(*at("rope", (nm, 1)))
                to_T(nm, rqk[a], 4, 4 + 2 * a)
            pe.wait_ge(*read(("rk", 1)))
            slot_fm(("nq", 0), 2)
            slot_fm(("nq", 1), 3)
            pe.wait_ge(*at("rT", ("rq", 1)))
            pe.wait_ge(*at("rT", ("rk", 1)))

            def ret_scores(h):
                b, k = (h % 2) * DH, h // 2
                if h >= 2:
                    pe.wait_ge(*at("r_m", h - 2))
                for s in range(NT):
                    i = mm(PS[:, 4 + h % 2, s * S:(s + 1) * S], rkT[b:b + DH, k, s * P:(s + 1) * P],
                           rqT[b:b + DH, k, :], start=True, stop=True)
                i.then_inc(*done("r_s", h))

            def ret_out(h):
                pe.wait_ge(*at("r_m", h))
                if h == 0:
                    pe.wait_ge(*read(("rv", 1)))
                for t in range(NT):
                    for s in range(NT):
                        i = mm(PS[:, 6 + t, h * DH:(h + 1) * DH],
                               msc[h % 2][:, s * S + t * P:s * S + (t + 1) * P],
                               rv[:, s, h * DH:(h + 1) * DH], start=s == 0, stop=s == NT - 1)
                i.then_inc(*done("r_pv", h))

            for h in range(NH + 1):
                if h < NH:
                    ret_scores(h)
                if h >= 1:
                    ret_out(h - 1)
                if h == 3:
                    pe.wait_ge(*read(("rv", 1)))
                    slot_fm(("nk", 0), 0)
                    slot_fm(("nk", 1), 1)
            pe.wait_ge(*read(("nq", 1)))
            block_tm("nv", 2)
            pe.wait_ge(*read(("nk", 1)))
            block_tm("rg", 0)

            def attention(tag, heads, after):
                def scores(i):
                    q, k, _, causal = heads[i]
                    if i >= 2:
                        pe.wait_ge(*at("a_sc", (tag, i - 2)))
                    for t in range(NT):
                        nk = P if causal and t == 0 else S
                        n = mm(PS[:, 4 + i % 2, t * S:t * S + nk], q(t), k(nk), start=True, stop=True)
                    n.then_inc(*done("a_s", (tag, i)))

                def turn(i):
                    causal = heads[i][3]
                    pe.wait_ge(*at("a_exp", (tag, i)))
                    if i >= 1:
                        pe.wait_ge(*at("a_pt", (tag, i - 1)))
                    for t in range(NT):
                        for c in range(1 if causal and t == 0 else 2):
                            n = tr(PS[:, 6, (2 * t + c) * P:(2 * t + c + 1) * P], sc[i % 2][:, t, c * P:(c + 1) * P], ident)
                    n.then_inc(*done("a_t", (tag, i)))

                def values(i):
                    causal = heads[i][3]
                    pe.wait_ge(*at("a_pt", (tag, i)))
                    if i >= 1:
                        pe.wait_ge(*at("a_o", (tag, i - 1)))
                    for t in range(NT):
                        nc_ = 1 if causal and t == 0 else 2
                        for c in range(nc_):
                            a = (i % 4) * P + t * DH
                            n = mm(PS[:, 7, a:a + DH], pt[i % 2][:, 2 * t + c, :], heads[i][2](c),
                                   start=c == 0, stop=c == nc_ - 1)
                    n.then_inc(*done("a_v", (tag, i)))

                n = len(heads)
                for i in range(n + 2):
                    if i < n:
                        scores(i)
                    if 1 <= i <= n:
                        turn(i - 1)
                    if i >= 2:
                        values(i - 2)
                    after(i)

            def operands(h, qT, kT, kk, v, causal):
                b = (h % 2) * DH
                return (lambda t: qT[b:b + DH, h // 2, t * P:(t + 1) * P], lambda nk: kT[b:b + DH, kk, 0:nk], v, causal)

            pe.wait_ge(*read(("nv", 1)))
            pe.wait_ge(*read(("nk", 1)))
            pe.wait_ge(*at("gn_c", 1))
            attention("na", [operands(h, nqT, nkT, h // 2, lambda c, h=h: nv[:, c, h * DH:(h + 1) * DH], False)
                             for h in range(NH)], lambda i: None)
            pe.wait_ge(*at("y0"))
            pe.wait_ge(*at("a_o", ("na", NH - 1)))
            to_T("y0", hn, KD, 0)
            pe.wait_ge(*at("T_lo", ("y0", KD - 1)))
            out_proj("mo0", 4, lambda k: 8 + k)
            norm_T(1)
            ffn(0)
            norm_T(2)

            pe.wait_ge(*at("T_lo", (("n", 2), KD - 1)))
            slot_tm(("dt", 0), 0, 0, True, True, 64, 8)
            pe.wait_ge(*at("la"))
            for j, (m, c, dr) in enumerate((("gt", 0, 0), ("lt", 1, 1), ("le", 1, 0), ("ge", 0, 1))):
                i = mm(PS[:, 4, 32 * j:32 * j + 32], cc(m), dtt[:, 2 + c, 32 * dr:32 * dr + 32], start=True, stop=True)
            i.then_inc(*done("cums"))

            def ssd_slot(g, j):
                if j == 0:
                    if g >= 1:
                        pe.wait_ge(*read((("bc", g - 1), 0)))
                    slot_tm((("z", g), 0), 0, 0, True, False)
                elif j == 1:
                    slot_tm((("z", g), 1), 0, 4, False, True)
                elif j in (2, 3):
                    if g >= 1:
                        pe.wait_ge(*read((("xs", g - 1), j - 2)))
                    slot_fm((("xs", g), j - 2), j)
                else:
                    pe.wait_ge(*read((("z", g), 1)))
                    slot_fm((("bc", g), 0), 0)

            def ssd(g):
                fill = (lambda j: ssd_slot(g + 1, j)) if g + 1 < SG else (lambda j: None)
                pe.wait_ge(*at("cv", (g, 1)))
                if g == 0:
                    pe.wait_ge(*at("ex"))
                else:
                    pe.wait_ge(*at("T_lo", (("y", g - 1), 3)))
                for t in range(NT):
                    for j in range(4):
                        i = tr(PS[:, 4 + t, j * P:(j + 1) * P], cvb[:, j, t * P:(t + 1) * P], ident)
                i.then_inc(*done("s_xt", g))
                pe.wait_ge(*at("cv", (g, 2)))
                for c in range(NT):
                    tr(PS[:, 6, c * P:(c + 1) * P], bct[g % 2][:, 0, c * P:(c + 1) * P], ident)
                for c in range(NT):
                    i = mm(PS[:, 6, S + c * P:S + (c + 1) * P], bct[g % 2][:, 0, c * P:(c + 1) * P],
                           bct[g % 2][:, 1, c * P:(c + 1) * P], start=True, stop=True)
                i.then_inc(*done("s_bq", g))
                fill(0)
                pe.wait_ge(*at("s_v", g))
                for r in range(2):
                    i = mm(PS[:, 4 + r, :], btm[:, r, :], vt[:, r, :], start=True, stop=True)
                i.then_inc(*done("s_st", g))
                fill(1)
                pe.wait_ge(*at("s_ste", g))
                for r in range(2):
                    c = 1 - r
                    i = mm(PS[:, 4 + r, :], bct[g % 2][:, 1, c * P:(c + 1) * P], stt[:, r, :], start=True, stop=True)
                i.then_inc(*done("s_yi", g))
                pe.wait_ge(*at("s_yie", g))

                def seg(u):
                    c, r, hf = u // 4, (u // 2) % 2, u % 2
                    pe.wait_ge(*at("s_am", (g, u)))
                    if u >= 2:
                        pe.wait_ge(*at("s_e", (g, u - 2)))
                    mm(PS[:, 4 + u % 2, :], cc("gt" if r == 0 else "lt"), am[u % 2][:, :, :],
                       start=True, stop=True).then_inc(*done("s_l", (g, u)))

                def diag(u):
                    c, r, hf = u // 4, (u // 2) % 2, u % 2
                    pe.wait_ge(*at("s_m", (g, u)))
                    for k in range(4):
                        h = 4 * hf + k
                        i = mm(PS[:, 7 - c, h * DH:(h + 1) * DH], ee[u % 2][:, k, :], vfb[:, r, c, h * DH:(h + 1) * DH],
                               start=u % 4 == 0 and k == 0, stop=False, skip_group_check=True)
                    i.then_inc(*done("s_pv", (g, u)))

                for u in range(9):
                    if u < 8:
                        seg(u)
                    if u >= 1:
                        diag(u - 1)
                    if u in (2, 4, 6):
                        fill(2 + u // 2 - 1)
                pe.wait_ge(*at("s_y", g))
                yv = hn[:, :, (g % 2) * 512:(g % 2) * 512 + 512]
                to_T(("y", g), yv, 4, 4)
                if g == SG - 1:
                    pe.wait_ge(*at("T_lo", (("y", g), 3)))

            for j in range(5):
                if j == 0:
                    pe.wait_ge(*at("dt_in"))
                ssd_slot(0, j)
            for g in range(SG):
                ssd(g)
            out_proj("mo1", 8, lambda k: (8 + k) % 16)
            norm_T(3)
            ffn(1)

            norm_T(4)
            block_tm("qa", 0)
            block_tm("ka", 2)

            def head_T(nm, a):
                pe.wait_ge(*read((nm, 1)))
                if a >= 2:
                    pe.wait_ge(*at("hT", (a - 2, 1)))
                to_T(nm, hn[:, :, 512 * (a % 2):512 * (a % 2) + 512], 4, 4 + 2 * (a % 2))

            pe.wait_ge(*read(("qa", 1)))
            block_tm("va", 0)
            head_T("qa", 0)
            head_T("ka", 1)
            block_tm("qb", 2)
            pe.wait_ge(*read(("va", 1)))
            slot_fm(("kc", 0), 0)
            slot_fm(("vc", 0), 1)
            head_T("qb", 2)
            block_tm("ksv", 2)
            pe.wait_ge(*read(("kc", 0)))
            pe.wait_ge(*read(("vc", 0)))
            slot_tm(("gb", 0), 0, 0, True, True, 24, 8)
            head_T("ksv", 3)
            pe.wait_ge(*read(("gb", 1)))
            block_tm("za", 0)
            block_tm("zb", 2)
            pe.wait_ge(*at("hT", (3, 1)))
            for a, nm in enumerate("kv"):
                pe.wait_ge(*at("x_lo", a))
                for j in range(2):
                    n = slot_no[("w1" + nm, j)]
                    pe.wait_ge(*at("w_lo", n))
                    h, l = whi[n % NHI], wlo[n % NLO]
                    for m in range(2):
                        for k in range(8):
                            c, kk = k * 256 + m * P, 8 * j + k
                            xh = Th[:, 8 + 2 * a:10 + 2 * a, :].rearrange("p a (b c) -> p (a b) c", c=32)[:, kk, :]
                            xl = Tl[:, 8 + 2 * a:10 + 2 * a, :].rearrange("p a (b c) -> p (a b) c", c=32)[:, kk, :]
                            i = three(PS[:, 4 + 2 * a + m, 0:32], h[:, c:c + P], l[:, c:c + P], xh, xl,
                                      kk == 0, kk == 15, False)
                    i.then_inc(*done("w_used", n))
            pe.wait_ge(*at("c_gelu", 0))
            pe.wait_ge(*at("load_w2"))
            for m in range(2):
                i = mm(PS[0:32, 4, 64:64 + DH], hid[:, 0, m, :], w2c[:, 0, m, :], start=m == 0, stop=m == 1)
            i.then_inc(*done("c_k"))
            pe.wait_ge(*at("c_rep"))
            for m in range(2):
                i = mm(PS[:, 5, 64:64 + DH], hidr[:, m, :], w2c[:, 1, m, :], start=m == 0, stop=m == 1)
            i.then_inc(*done("c_v"))
            pe.wait_ge(*at("c_kn"))
            tr(PS[:, 6, 0:32], kcm[0:32, 0, :], ident[0:32, 0:32]).then_inc(*done("c_kt"))
            pe.wait_ge(*at("c_kte"))
            pe.wait_ge(*at("c_vbd"))
            for t in range(NT):
                for h in range(NH):
                    b = (h % 2) * DH
                    a = 64 * t + 16 * (h // 2)
                    i = mm(PS[:, 4 + h % 2, a:a + 16], qbT[b:b + DH, h // 2, t * P:(t + 1) * P],
                           kcT[b:b + DH, 16 * (h // 4):16 * (h // 4) + 16], start=True, stop=True)
            i.then_inc(*done("c_s"))
            pe.wait_ge(*at("c_p"))
            for t in range(NT):
                i = tr(PS[:, 5, t * P:(t + 1) * P], cpr[:, t, :], ident)
            i.then_inc(*done("c_pt"))
            pe.wait_ge(*at("c_pte"))
            for t in range(NT):
                i = mm(PS[:, 6 + t, :], cpt[:, t, :], vbd[:, :, :], start=True, stop=True)
            i.then_inc(*done("c_o"))
            pe.wait_ge(*at("c_oe"))

            def g_blocks(n):
                for a, nm in enumerate(("GA", "GB")):
                    if n == 0:
                        pe.wait_ge(*read((("za", "zb")[a], 1)))
                    else:
                        pe.wait_ge(*read(((nm, n - 1), 1)))
                    block_tm((nm, n), 2 * a)

            def y_blocks(n):
                for a, nm in enumerate(("YA", "YB")):
                    if n:
                        pe.wait_ge(*at("mrg", (n - 1, a)))
                    slot_tm(((nm, n), 0), 4 + 2 * a, 8 + 4 * a, True, True)

            pe.wait_ge(*read(("va", 1)))
            attention("moba", [operands(h, qaT, kaT, h // 2, lambda c, h=h: va[:, c, h * DH:(h + 1) * DH], True)
                               for h in range(NH)], lambda i: None)
            pe.wait_ge(*at("a_o", ("moba", NH - 1)))
            attention("nsa", [operands(h, qbT, kswT, 2 * w + h // 4,
                                       lambda c, h=h, w=w: vsw[:, c, w, DH * (h // 4):DH * (h // 4) + DH], True)
                              for w in range(2) for h in range(NH)], lambda i: None)
            g_blocks(0)
            pe.wait_ge(*at("y2"))
            to_T("y2", hn, KD, 4)
            pe.wait_ge(*at("T_lo", ("y2", KD - 1)))
            y_blocks(0)
            g_blocks(1)
            y_blocks(1)
            pe.wait_ge(*at("mrg", (1, 1)))
            to_T("mrg", hn, KD, 0)
            pe.wait_ge(*at("T_lo", ("mrg", KD - 1)))
            out_proj("fo", 4, lambda k: k)

        @block.scalar
        def _(act):
            nxt = [0]

            def high(upto):
                while nxt[0] <= min(upto, NS - 1):
                    n = nxt[0]
                    parts, width = slots[n]
                    act.wait_ge(*at(f"w_raw{n % NRAW}", n))
                    if n >= NHI:
                        act.wait_ge(*at("w_used", n - NHI))
                    act.activation(whi[n % NHI][:, 0:width], raw[n % NRAW][:, 0:width], ACT.Copy)\
                        .then_inc(*done("w_hi", n))
                    nxt[0] += 1

            def used(name):
                n = slot_no[name]
                high(n + 2)
                act.wait_ge(*at("w_used", n))
                high(n + 3)

            def sqrt_of(key, o, i, width):
                act.activation(o, i, ACT.Sqrt, scale=1.0 / width, bias=eps[0:o.shape[0], 0:1]).then_inc(*done("root", key))

            def T_hi(name, nk, kt0, b0, gains):
                for k in range(nk):
                    if k % 2 == 0:
                        act.wait_ge(*at("turned", (name, k + 1)))
                    src = PS[:, b0 + k // 2, (k % 2) * S:(k % 2 + 1) * S]
                    g = gains(k)
                    act.activation(Th[:, kt0 + k, :], src, ACT.Identity, scale=1.0 if g is None else g)\
                        .then_inc(*done("T_hi", (name, k)))

            def norm(l, gain):
                act.wait_ge(*at("n_ss", l))
                sqrt_of(("n", l), st[:, 2:4], st[:, 0:2], D)
                T_hi(("n", l), KD, 0, 0, lambda k: col(gain, k))

            def post(l, last, vec):
                used(last)
                for j in range(4):
                    i = act.activation(hn[:, j // 2, (j % 2) * 512:(j % 2 + 1) * 512], PS[:, 4 + j, :], ACT.Square,
                                       accum_out=st[:, 4 + j:5 + j])
                i.then_inc(*done("p_ss", l))
                act.wait_ge(*at("p_sum", l))
                sqrt_of(("p", l), st[:, 10:12], st[:, 8:10], D)

            def load_gpost(l):
                src = (I["norm_mix_post"], I["norm_ffn_post"])[l % 2][l // 2:l // 2 + 1, :]
                act.dma_start(gpost[:, :], src.to_broadcast([P, D])).then_inc(*done("load_gpost", l, 16))

            def ffn(l):
                for i in range(FI + 1):
                    if i < FI:
                        for q in range(4):
                            if q % 2 == 0:
                                used(("GV"[q // 2], l, i))
                            if q == 0 and i >= 2:
                                act.wait_ge(*at("f_prod", (l, i - 2)))
                            j = (0, 1, 22, 23)[q] + 2 * i
                            act.activation(fac[i % 2][:, q, :],
                                           PS[:, 2 * (i % 2) + q // 2, (q % 2) * S:(q % 2 + 1) * S], ACT.Identity,
                                           scale=col(f"fw{l}1", j), bias=col(f"fb{l}", j)).then_inc(*done("f_ctr", (l, i, q)))
                        act.wait_ge(*at("f_cg", (l, i)))
                        act.activation(fac[i % 2][:, 0:2, :], fac[i % 2][:, 0:2, :], ACT.Gelu_apprx_tanh)\
                            .then_inc(*done("f_gelu", (l, i)))
                        if i >= 2:
                            act.wait_ge(*at("w_used", slot_no[("D", l, i - 2)]))
                        act.wait_ge(*at("f_prod", (l, i)))
                        act.activation(aTh[:, i % 2, :, :], fpr[i % 2][:, :, :], ACT.Copy).then_inc(*done("f_ahi", (l, i)))
                        high(slot_no[("V", l, i)] + 3)

            act.wait_ge(*at("rows_clear"))
            act.dma_start(cst[:, :], I["const_table"]).then_inc(*done("load_cst", 0, 16))
            for name, ap in rows:
                c = col_at[name]
                act.dma_start(rowb[c % P:c % P + ap.shape[0], c // P, :], ap).then_inc(*done("load_rows", 0, 16))
            for j, nm in enumerate(("q_norm_a_2", "k_norm_a_2", "q_norm_b_2", "k_norm_sel_2", "k_norm_win_2", "k_norm_cmp_2")):
                act.dma_start(rowb[j:j + 1, NR, :].rearrange("p (r d) -> p r d", r=2),
                              bc(I[nm], 1, 2)).then_inc(*done("load_rows", 0, 16))
            act.dma_start(oneh, I["const_onehot"]).then_inc(*done("load_t5", 0, 16))
            act.dma_start(negs, I["const_negs"]).then_inc(*done("load_t5", 0, 16))
            act.dma_start(relb, I["rel_bias_2"]).then_inc(*done("load_t5", 0, 16))
            act.dma_start(brow, I["ab_ret_decay_logit"].rearrange("a b c -> a (b c)").to_broadcast([P, 16]))\
                .then_inc(*done("load_dl", 0, 16))
            act.dma_start(narep, bc(I["ab_na_rpb"][0].rearrange("h a b -> h (a b)"), 1, GW)).then_inc(*done("na_rows", 0, 16))
            load_gpost(0)
            act.wait_ge(*at("set_up"))
            act.wait_ge(*at("eps"))
            for b in range((NR + 3) // 4):
                n = min(4, NR - 4 * b) * P
                i = act.activation(cols[:, 512 * b:512 * b + n], PS[:, b, 0:n], ACT.Copy)
            i.then_inc(*done("cols_act"))
            act.wait_ge(*at("t5_sum"))
            act.dma_start(toe, bc(t5r, 1, P)).then_inc(*done("t5_out", 0, 16))
            act.dma_start(pfb[:, :, :], I["const_pfb"].rearrange("p (a b) -> p a b", a=2)).then_inc(*done("load_pfb", 0, 16))

            def softplus(key, neg, n):
                spx = spxs[key]
                act.wait_ge(*at("sp_x", key))
                act.activation(spx[:, 1, 0:n], spx[:, 0, 0:n], ACT.Abs).then_inc(*done("sp_abs", key))
                act.wait_ge(*at("sp_abs", key))
                act.activation(spx[:, 2, 0:n], spx[:, 1, 0:n], ACT.Exp, scale=-1.0).then_inc(*done("sp_exp", key))
                act.wait_ge(*at("sp_u", key))
                act.activation(spx[:, 4, 0:n], spx[:, 3, 0:n], ACT.Ln).then_inc(*done("sp_ln", key))

            norm(0, "mix0")
            softplus("ret", True, 16)
            high(2)

            def copy_block(nm, dst, b0, scale=1.0, func=ACT.Copy):
                for t in range(NT):
                    if func == ACT.Copy:
                        i = act.activation(dst[:, t, :], PS[:, b0 + t, :], func, scale=scale)
                    else:
                        i = act.activation(dst[:, t, :], PS[:, b0 + t, :], func)
                    i.then_inc(*done("read_a", (nm, t)))

            def copy_fm(nm, dst, b0, scale=1.0):
                for j in range(2):
                    used((nm, j))
                    act.activation(dst[:, 2 * j:2 * j + 2, :], PS[:, b0 + j, :].rearrange("p (a b) -> p a b", a=2),
                                   ACT.Copy, scale=scale).then_inc(*done("read_a", (nm, j)))

            used(("rk", 1))
            high(slot_no[("rv", 0)] + 2)
            used(("rv", 1))
            copy_block("rv", rv, 0)
            for a, nm in enumerate(("rq", "rk")):
                for j in range(2):
                    act.wait_ge(*at("turned", (nm, 2 * j + 1)))
                    act.activation((rqT, rkT)[a][:, 2 * j:2 * j + 2, :],
                                   PS[:, 4 + 2 * a + j, :].rearrange("p (a b) -> p a b", a=2),
                                   ACT.Copy, scale=(1.0, DH ** -0.5)[a]).then_inc(*done("rT", (nm, j)))
            act.wait_ge(*at("na_rows"))
            act.wait_ge(*at("t5_out"))
            for h in range(NH):
                for q in range(2):
                    src = bass.AP(narep.tensor, h * GW * 465 + (5 - q) * 31 + 15, [[464, GW], [31, 6], [1, GW]])
                    act.dma_start(nabias[q * GW:(q + 1) * GW, h, :].rearrange("p (a b) -> p a b", a=6), src)\
                        .then_inc(*done("load_na", 0, 16))
            copy_fm("nq", nqT, 2, DH ** -0.5)
            for h in range(NH):
                act.wait_ge(*at("r_arg", h))
                act.activation(dcy[h % 2], dcy[h % 2], ACT.Exp).then_inc(*done("r_d", h))
                if h == 4:
                    copy_fm("nk", nkT, 0)
            used(("nv", 1))
            copy_block("nv", nv, 2)
            for t in range(NT):
                act.wait_ge(*at("gn_c", t))
                act.activation(A[:, 11264 + 512 * t:11776 + 512 * t], hn[:, t, 0:512], ACT.Square).then_inc(*done("gn_sq", t))
            act.wait_ge(*at("gn_ss"))
            sqrt_of("gn", st[:, 48:64], st[:, 32:48], DH)
            used(("rg", 1))
            copy_block("rg", rg, 0, func=ACT.Silu)

            def attention(tag, n, causal):
                for i in range(n + 1):
                    if i < n:
                        act.wait_ge(*at("a_nm", (tag, i)))
                        for t in range(NT):
                            nk = P if causal and t == 0 else S
                            e = act.activation(sc[i % 2][:, t, 0:nk], sc[i % 2][:, t, 0:nk], ACT.Exp,
                                               bias=st[:, 72 + 2 * (i % 4) + t:73 + 2 * (i % 4) + t],
                                               accum_out=st[:, 80 + 2 * (i % 4) + t:81 + 2 * (i % 4) + t])
                        e.then_inc(*done("a_exp", (tag, i)))
                    if i >= 1:
                        j = i - 1
                        act.wait_ge(*at("a_t", (tag, j)))
                        if j >= 2:
                            act.wait_ge(*at("a_v", (tag, j - 2)))
                        if causal:
                            act.activation(pt[j % 2][:, 0, :], PS[:, 6, 0:P], ACT.Copy)
                            e = act.activation(pt[j % 2][:, 2:4, :], PS[:, 6, S:2 * S].rearrange("p (a b) -> p a b", a=2), ACT.Copy)
                        else:
                            e = act.activation(pt[j % 2][:, :, :], PS[:, 6, :].rearrange("p (a b) -> p a b", a=4), ACT.Copy)
                        e.then_inc(*done("a_pt", (tag, j)))

            high(slot_no[("rg", 1)] + 3)
            attention("na", NH, False)
            T_hi("y0", KD, 8, 0, lambda k: col("gn", k) if k < 4 else None)
            post(0, ("mo0", 3), 0)
            norm(1, "ffn0")
            load_gpost(1)
            ffn(0)
            post(1, ("D", 0, FI - 1), 1)
            norm(2, "mix1")
            load_gpost(2)
            for r, (nm, w) in enumerate((("c_dt_bias", 64), ("c_a_log", 64))):
                act.dma_start(dtt[:, 4 + r, 0:w], I[nm].rearrange("a b c -> a (b c)").to_broadcast([P, w]))\
                    .then_inc(*done("load_ssd", 0, 16))
            act.dma_start(dtt[:, 6, 0:32], I["c_d_skip"].to_broadcast([P, 32])).then_inc(*done("load_ssd", 0, 16))
            used(("dt", 0))
            softplus("ssd", False, 128)
            act.wait_ge(*at("load_ssd"))
            act.activation(dtt[:, 5, :], dtt[:, 5, :], ACT.Exp).then_inc(*done("ssd_a"))
            act.wait_ge(*at("cums"))
            act.activation(dtt[:, 8:10, :], PS[:, 4, 0:128].rearrange("p (a b) -> p a b", a=2), ACT.Exp).then_inc(*done("ex"))

            def ssd_evac(g, j):
                if j == 1:
                    used((("z", g), 1))
                    if g >= 2:
                        act.wait_ge(*at("s_y", g - 2))
                    copy_block(("z", g), zt[g % 2], 0, func=ACT.Silu)
                elif j in (2, 3, 4):
                    used(((("xs", "xs", "bc")[j - 2], g), (0, 1, 0)[j - 2]))
                    if j == 2 and g >= 1:
                        act.wait_ge(*at("s_xt", g - 1))
                    b = (2, 3, 0)[j - 2]
                    for m in range(2):
                        ch = 4 * g + 2 * (j - 2) + m if j < 4 else 16 + 4 * m + g
                        q = 2 * (j - 2) + m
                        act.activation(cvb[:, q, :], PS[:, b, m * S:(m + 1) * S], ACT.Identity, scale=col("cw2", ch),
                                       bias=col("cb", ch)).then_inc(*done("c_ctr", (g, q)))
                    act.wait_ge(*at("c_cnv", (g, j - 2)))
                    if j < 4:
                        dst = cvb[:, 2 * (j - 2):2 * (j - 2) + 2, :]
                    else:
                        dst = bct[g % 2][:, :, :]
                    act.activation(dst, cvb[:, 2 * (j - 2):2 * (j - 2) + 2, :], ACT.Silu).then_inc(*done("cv", (g, j - 2)))

            def ssd(g):
                fill = (lambda j: ssd_evac(g + 1, j)) if g + 1 < SG else (lambda j: None)
                act.wait_ge(*at("s_xt", g))
                for t in range(NT):
                    i = act.activation(xs[g % 2][:, t, :], PS[:, 4 + t, :], ACT.Copy)
                i.then_inc(*done("s_xs", g))
                if g + 1 < SG:
                    high(slot_no[(("z", g + 1), 0)] + 2)
                act.wait_ge(*at("s_st", g))
                for r in range(2):
                    i = act.activation(stt[:, r, :], PS[:, 4 + r, :], ACT.Copy)
                i.then_inc(*done("s_ste", g))
                fill(1)
                for u in range(8):
                    act.wait_ge(*at("s_l", (g, u)))
                    if u >= 2:
                        act.wait_ge(*at("s_pv", (g, u - 2)))
                    act.activation(ee[u % 2][:, :, :], PS[:, 4 + u % 2, :].rearrange("p (a b) -> p a b", a=4), ACT.Exp)\
                        .then_inc(*done("s_e", (g, u)))
                    if u in (2, 4, 6):
                        fill(1 + u // 2)
                act.wait_ge(*at("s_ss", g))
                sqrt_of(("s", g), st[:, 98:100], st[:, 96:98], 512)
                T_hi(("y", g), 4, (8 + 4 * g) % 16, 4, lambda k: col("ssdn", 4 * g + k))

            for j in range(5):
                ssd_evac(0, j)
            for g in range(SG):
                ssd(g)
            post(2, ("mo1", 7), 2)
            norm(3, "ffn1")
            load_gpost(3)
            ffn(1)
            post(3, ("D", 1, FI - 1), 3)
            norm(4, "sec")

            def load_tb(k):
                for h in range(NH):
                    src = bass.AP(toe.tensor, (NH * k + h) * P * 384 + 127, [[383, P], [1, S]])
                    act.dma_start(tb[:, h, :], src).then_inc(*done("load_tb", k, 16))

            load_tb(0)
            for a, nm in enumerate("kv"):
                act.dma_start(w2c[:, a, :, :], I["cmp_w2_" + nm + "_2"][0].rearrange("(m p) d -> p m d", p=P))\
                    .then_inc(*done("load_w2", 0, 16))

            def head_norm(nm, b0):
                used((nm, 1))
                for t in range(NT):
                    if t == 0 and nm != "qa":
                        act.wait_ge(*at("q_ss", {"ka": "qa", "qb": "ka", "ksv": "qb"}[nm]))
                    act.activation(sqb[:, t, :], PS[:, b0 + t, :], ACT.Square).then_inc(*done("q_sq", (nm, t)))
                if nm == "ksv":
                    for t in range(NT):
                        v = PS[:, b0 + t, :].rearrange("p (w c d) -> p w c d", w=2, c=2)[:, :, 1, :]
                        act.activation(vsw[:, t, :, :], v, ACT.Copy).then_inc(*done("vsw", t))
                act.wait_ge(*at("q_ss", nm))
                sqrt_of(("q", nm), st[:, 120:136], st[:, 104:120], DH)

            def head_T(nm, a, dst, gains):
                for j in range(2):
                    act.wait_ge(*at("turned", (nm, 2 * j + 1)))
                    act.activation(dst[:, 2 * j:2 * j + 2, :], PS[:, 4 + 2 * (a % 2) + j, :].rearrange("p (a b) -> p a b", a=2),
                                   ACT.Identity, scale=cols[:, gains[j]:gains[j] + 1]).then_inc(*done("hT", (a, j)))

            head_norm("qa", 0)
            head_norm("ka", 2)
            used(("va", 1))
            copy_block("va", va, 0)
            head_T("qa", 0, qaT, (qn + 6, qn + 6))
            head_T("ka", 1, kaT, (qn + 1, qn + 1))
            head_norm("qb", 2)
            used(("vc", 0))
            head_T("qb", 2, qbT, (qn + 7, qn + 7))
            for a in range(2):
                act.wait_ge(*at("x_c", a))
                act.activation(Th[:, 8 + 2 * a:10 + 2 * a, :].rearrange("p a (b c) -> p (a b) c", c=32), XC[a][:, :, :],
                               ACT.Copy).then_inc(*done("x_hi", a))
            head_norm("ksv", 2)
            used(("gb", 0))
            for t in range(NT):
                act.activation(gb[:, t, :], PS[:, t, 0:24], ACT.Sigmoid).then_inc(*done("read_a", ("gb", t)))
            head_T("ksv", 3, kswT, (qn + 3, qn + 4))
            used(("za", 1))
            copy_block("za", za, 0, func=ACT.Silu)
            used(("zb", 1))
            copy_block("zb", zb, 2, func=ACT.Silu)
            for a, nm in enumerate("kv"):
                used(("w1" + nm, 1))
                act.activation(hid[:, a, :, :], PS[:, 4 + 2 * a:6 + 2 * a, 0:32], ACT.Gelu_apprx_tanh).then_inc(*done("c_gelu", a))
            act.wait_ge(*at("c_k"))
            act.activation(kcm[0:32, 1, 0:DH], PS[0:32, 4, 64:64 + DH], ACT.Square, accum_out=st[0:32, 12:13])\
                .then_inc(*done("c_kss"))
            act.wait_ge(*at("c_kss"))
            sqrt_of("ck", st[0:32, 13:14], st[0:32, 12:13], DH)
            act.wait_ge(*at("c_kt"))
            act.activation(kcT, PS[:, 6, 0:32], ACT.Identity, scale=cols[:, qn + 5:qn + 6]).then_inc(*done("c_kte"))
            act.wait_ge(*at("c_sub"))
            act.activation(cpr[:, :, :], cpr[:, :, :], ACT.Exp).then_inc(*done("c_exp"))
            act.wait_ge(*at("c_pt"))
            act.activation(cpt[:, :, :], PS[:, 5, 0:S].rearrange("p (a b) -> p a b", a=2), ACT.Copy).then_inc(*done("c_pte"))
            high(slot_no[("w1v", 1)] + 3)
            attention("moba", NH, True)
            act.wait_ge(*at("a_sc", ("moba", NH - 1)))
            load_tb(1)
            attention("nsa", 2 * NH, True)

            def g_evac(n):
                for a, nm in enumerate(("GA", "GB")):
                    used(((nm, n), 1))
                    if n:
                        act.wait_ge(*at("mrg", (n - 1, a)))
                    copy_block((nm, n), sg[a], 2 * a, func=ACT.Sigmoid)

            g_evac(0)
            T_hi("y2", KD, 8, 4, lambda k: None)
            high(slot_no[(("YB", 0), 0)] + 2)
            g_evac(1)
            high(slot_no[(("YB", 1), 0)] + 2)
            T_hi("mrg", KD, 0, 0, lambda k: None)
            used(("fo", 3))

        @block.vector
        def _(dve):
            tt, ts, stt3 = nc.vector.tensor_tensor, nc.vector.tensor_scalar, nc.vector.scalar_tensor_tensor
            lk = lambda ins: link(dve, "dve", ins)

            def T_lo(name, nk, kt0, b0, gains):
                for k in range(nk):
                    if k % 2 == 0:
                        dve.wait_ge(*at("T_hi", (name, k + 1)))
                    src = PS[:, b0 + k // 2, (k % 2) * S:(k % 2 + 1) * S]
                    g = gains(k)
                    stt3(out=Tl[:, kt0 + k, :], in0=src, scalar=1.0 if g is None else g,
                         in1=Th[:, kt0 + k, :].bitcast(F32), op0=ALU.mult, op1=ALU.subtract)\
                        .then_inc(*done("T_lo", (name, k)))

            def norm(l, gain):
                for t in range(NT):
                    i = nc.vector.tensor_tensor_reduce(out=hn[:, t, :], in0=x[:, t, :], in1=x[:, t, :], scale=1.0,
                                                       scalar=0.0, op0=ALU.mult, op1=ALU.add, accum_out=st[:, t:t + 1])
                i.then_inc(*done("n_ss", l))
                dve.wait_ge(*at("root", ("n", l)))
                lk(nc.vector.reciprocal(st[:, 0:2], st[:, 2:4]))
                for t in range(NT):
                    ts(hn[:, t, :], x[:, t, :], st[:, t:t + 1], None, ALU.mult).then_inc(*done("n_hn", (l, t)))
                T_lo(("n", l), KD, 0, 0, lambda k: col(gain, k))

            def post(l):
                dve.wait_ge(*at("p_ss", l))
                tt(st[:, 8:10], st[:, 4:8:2], st[:, 5:8:2], ALU.add).then_inc(*done("p_sum", l))
                dve.wait_ge(*at("root", ("p", l)))
                lk(nc.vector.reciprocal(st[:, 8:10], st[:, 10:12]))
                dve.wait_ge(*at("load_gpost", l))
                for t in range(NT):
                    for hf in range(2):
                        i = stt3(out=hn[:, t, hf * 512:(hf + 1) * 512], in0=PS[:, 4 + 2 * t + hf, :], scalar=st[:, 8 + t:9 + t],
                                 in1=gpost[:, hf * 512:(hf + 1) * 512], op0=ALU.mult, op1=ALU.mult)
                lk(i)
                for t in range(NT):
                    lk(tt(x[:, t, :], x[:, t, :], hn[:, t, :], ALU.add))

            def taps(dst, src, ws, shift):
                n = S - abs(shift)
                a, b = (-shift, 0) if shift < 0 else (0, shift)
                return stt3(out=dst[:, a:a + n], in0=src[:, b:b + n], scalar=ws, in1=dst[:, a:a + n], op0=ALU.mult, op1=ALU.add)

            def ffn(l):
                for i in range(FI):
                    p = i % 2
                    bank = lambda q: PS[:, 2 * p + q // 2, (q % 2) * S:(q % 2 + 1) * S]
                    j = lambda q: (0, 1, 22, 23)[q] + 2 * i
                    for hv in range(2):
                        dve.wait_ge(*at("f_ctr", (l, i, 2 * hv + 1)))
                        for q in (2 * hv, 2 * hv + 1):
                            o = taps(fac[p][:, q, :], bank(q), col(f"fw{l}0", j(q)), -1)
                        lk(o)
                        for q in (2 * hv, 2 * hv + 1):
                            o = taps(fac[p][:, q, :], bank(q), col(f"fw{l}2", j(q)), 1)
                        o.then_inc(*done(("f_cg", "f_conv")[hv], (l, i)))
                    dve.wait_ge(*at("f_gelu", (l, i)))
                    dve.wait_ge(*at("f_conv", (l, i)))
                    if i >= 2:
                        dve.wait_ge(*at("f_ahi", (l, i - 2)))
                    tt(fpr[p][:, :, :], fac[p][:, 0:2, :], fac[p][:, 2:4, :], ALU.mult).then_inc(*done("f_prod", (l, i)))
                    dve.wait_ge(*at("f_ahi", (l, i)))
                    if i >= 2:
                        dve.wait_ge(*at("w_used", slot_no[("D", l, i - 2)]))
                    tt(aTl[:, p, :, :], fpr[p][:, :, :], aTh[:, p, :, :].bitcast(F32), ALU.subtract).then_inc(*done("f_alo", (l, i)))

            def softplus(key, n, dst):
                w = lambda k: spxs[key][:, k, 0:n]
                dve.wait_ge(*at("sp_exp", key))
                ts(w(3), w(2), 1.0, None, ALU.add).then_inc(*done("sp_u", key))
                dve.wait_ge(*at("sp_u", key))
                lk(ts(w(5), w(3), -1.0, None, ALU.add))
                lk(ts(w(6), w(5), 0.0, None, ALU.is_equal))
                lk(tt(w(5), w(5), w(6), ALU.add))
                lk(nc.vector.reciprocal(w(7), w(5)))
                dve.wait_ge(*at("sp_ln", key))
                lk(tt(w(7), w(7), w(4), ALU.mult))
                lk(tt(w(7), w(7), w(6), ALU.add))
                lk(tt(w(7), w(7), w(2), ALU.mult))
                lk(stt3(out=dst, in0=w(0), scalar=0.0, in1=w(7), op0=ALU.max, op1=ALU.add))

            nc.vector.memset(eps[:, :], EPS).then_inc(*done("eps"))
            nc.vector.memset(rowb[:, :, :], 0.0).then_inc(*done("rows_clear"))
            dve.wait_ge(*at("set_up"))
            lk(nc.vector.tensor_copy(cols[:, qn:qn + 6], PS[:, 3, 0:6]))
            lk(ts(cols[:, qn + 6:qn + 8], cols[:, qn:qn + 3:2], DH ** -0.5, None, ALU.mult))
            dve.wait_ge(*at("load_t5"))
            tt(t5r, PS[0:16, 2, 0:384], negs, ALU.add).then_inc(*done("t5_sum"))
            dve.wait_ge(*at("cols_act"))
            dve.wait_ge(*at("t5_sum"))
            nc.vector.memset(st[:, :], 0.0).then_inc(*done("cols"))
            dve.wait_ge(*at("cols"))
            dve.wait_ge(*at("load_x"))
            norm(0, "mix0")
            dve.wait_ge(*at("load_dl"))
            ts(spxs["ret"][:, 0, 0:16], brow, -1.0, None, ALU.mult).then_inc(*done("sp_x", "ret"))
            dve.wait_ge(*at("sp_x", "ret"))
            softplus("ret", 16, lg)
            lk(ts(lg, lg, -1.0, None, ALU.mult))

            def rope(nm, a, b0):
                dve.wait_ge(*at("w_used", slot_no[(nm, 1)]))
                for t in range(NT):
                    src = PS[:, b0 + t, :]
                    o, tmp = rqk[a][:, t, :], hn[:, t, 512 * a:512 * a + 512]
                    h3 = lambda v: v.rearrange("p (h d) -> p h d", h=NH)
                    cosb = bc(cc("cos")[:, DH * t:DH * (t + 1)], 1, NH)
                    tt(h3(o), h3(src), cosb, ALU.mult)
                    for hf in range(2):
                        sn = bc(cc("sin")[:, DH * t + 32 * hf:DH * t + 32 * hf + 32], 1, NH)
                        i = tt(h3(tmp)[:, :, 32 * hf:32 * hf + 32], h3(src)[:, :, 32 * (1 - hf):32 * (1 - hf) + 32], sn, ALU.mult)
                    i.then_inc(*done("read_v", (nm, t)))
                    dve.wait_ge(*read((nm, t)))
                    tt(o, o, tmp, ALU.add).then_inc(*done("rope", (nm, t)))

            rope("rq", 0, 0)
            rope("rk", 1, 2)
            dve.wait_ge(*at("load_pfb"))

            def decay(h):
                if h >= 2:
                    dve.wait_ge(*at("r_m", h - 2))
                lk(ts(dcy[h % 2], pfb[:, 1, :], lg[:, 8 + h:9 + h], None, ALU.mult))
                stt3(out=dcy[h % 2], in0=pfb[:, 0, :], scalar=lg[:, h:h + 1], in1=dcy[h % 2], op0=ALU.mult, op1=ALU.add)\
                    .then_inc(*done("r_arg", h))

            decay(0)
            decay(1)
            for h in range(NH):
                dve.wait_ge(*at("r_s", h))
                dve.wait_ge(*at("r_d", h))
                if h >= 2:
                    dve.wait_ge(*at("r_pv", h - 2))
                tt(msc[h % 2], PS[:, 4 + h % 2, :], dcy[h % 2], ALU.mult).then_inc(*done("r_m", h))
                if h + 2 < NH:
                    decay(h + 2)
            dve.wait_ge(*at("r_pv", NH - 1))
            h3 = lambda v: v.rearrange("p (h d) -> p h d", h=NH)
            for t in range(NT):
                i = nc.vector.tensor_reduce(st[:, 16 + 8 * t:24 + 8 * t], h3(PS[:, 6 + t, :]), AXX, ALU.add)
            lk(i)
            for t in range(NT):
                stt3(out=h3(hn[:, t, 0:512]), in0=bc(st[:, 16 + 8 * t:24 + 8 * t], 2, DH), scalar=-1.0 / DH,
                     in1=h3(PS[:, 6 + t, :]), op0=ALU.mult, op1=ALU.add).then_inc(*done("gn_c", t))
            for t in range(NT):
                dve.wait_ge(*at("gn_sq", t))
                i = nc.vector.tensor_reduce(st[:, 32 + 8 * t:40 + 8 * t], h3(A[:, 11264 + 512 * t:11776 + 512 * t]), AXX, ALU.add)
            i.then_inc(*done("gn_ss"))
            dve.wait_ge(*at("root", "gn"))
            lk(nc.vector.reciprocal(st[:, 32:48], st[:, 48:64]))
            for t in range(NT):
                i = tt(h3(hn[:, t, 0:512]), h3(hn[:, t, 0:512]), bc(st[:, 32 + 8 * t:40 + 8 * t], 2, DH), ALU.mult)
            lk(i)
            dve.wait_ge(*read(("rg", 1)))
            for t in range(NT):
                i = tt(hn[:, t, 0:512], hn[:, t, 0:512], rg[:, t, :], ALU.mult)
            i.then_inc(*done("y0"))
            dve.wait_ge(*at("load_na"))
            for h in range(NH):
                v = nabias[:, h, :].rearrange("p (a b) -> p a b", a=6)
                i = tt(v, v, bc(cc("nm"), 1, 6), ALU.add)
            lk(i)

            def attention(tag, n, bias, causal, write):
                def finish(j):
                    dve.wait_ge(*at("a_v", (tag, j)))
                    s = 80 + 2 * (j % 4)
                    lk(nc.vector.reciprocal(st[:, s + 8:s + 10], st[:, s:s + 2]))
                    write(j, st[:, s + 8:s + 10], PS[:, 7, (j % 4) * P:(j % 4 + 1) * P].rearrange("p (t d) -> p t d", t=NT))\
                        .then_inc(*done("a_o", (tag, j)))

                for i in range(n + 2):
                    if i < n:
                        dve.wait_ge(*at("a_s", (tag, i)))
                        if i >= 2:
                            dve.wait_ge(*at("a_t", (tag, i - 2)))
                        for t in range(NT):
                            nk = P if causal and t == 0 else S
                            o = nc.vector.tensor_tensor_reduce(
                                out=sc[i % 2][:, t, 0:nk], in0=PS[:, 4 + i % 2, t * S:t * S + nk], in1=bias(i, t),
                                scale=1.0, scalar=-3e38, op0=ALU.add, op1=ALU.max,
                                accum_out=st[:, 64 + 2 * (i % 4) + t:65 + 2 * (i % 4) + t])
                        o.then_inc(*done("a_sc", (tag, i)))
                        dve.wait_ge(*at("a_sc", (tag, i)))
                        ts(st[:, 72 + 2 * (i % 4):74 + 2 * (i % 4)], st[:, 64 + 2 * (i % 4):66 + 2 * (i % 4)], -1.0, None,
                           ALU.mult).then_inc(*done("a_nm", (tag, i)))
                    if i >= 2:
                        finish(i - 2)

            def na_write(j, rc, o):
                return tt(hn[:, :, 512 + DH * j:512 + DH * (j + 1)], o, bc(rc, 2, DH), ALU.mult)

            attention("na", NH, lambda i, t: nabias[:, i, 128 - 128 * t:384 - 128 * t], False, na_write)
            T_lo("y0", KD, 8, 0, lambda k: col("gn", k) if k < 4 else None)
            post(0)
            norm(1, "ffn0")
            ffn(0)
            post(1)
            norm(2, "mix1")

            dve.wait_ge(*at("load_ssd"))
            dve.wait_ge(*at("w_used", slot_no[("dt", 0)]))
            for t in range(NT):
                i = tt(spxs["ssd"][:, 0, 64 * t:64 * t + 64], PS[:, t, 0:64], dtt[:, 4, :], ALU.add)
            i.then_inc(*done("sp_x", "ssd"))
            dve.wait_ge(*at("sp_x", "ssd"))
            nc.vector.memset(ssx[:, 0, 0:1], 0.0).then_inc(*done("dt_in"))
            softplus("ssd", 128, dtt[:, 0:2, :].rearrange("p a b -> p (a b)"))
            dve.wait_ge(*at("ssd_a"))
            stt3(out=dtt[:, 2:4, :], in0=dtt[:, 0:2, :], scalar=-1.0, in1=bc(dtt[:, 5, :], 1, 2), op0=ALU.mult, op1=ALU.mult)\
                .then_inc(*done("la"))
            dve.wait_ge(*at("la"))

            def ssd_conv(g, j):
                b = (2, 3, 0)[j]
                ch = lambda m: 4 * g + 2 * j + m if j < 2 else 16 + 4 * m + g
                dve.wait_ge(*at("c_ctr", (g, 2 * j + 1)))
                for k in (0, 1, 3, 4):
                    for m in range(2):
                        i = taps(cvb[:, 2 * j + m, :], PS[:, b, m * S:(m + 1) * S], col(f"cw{k}", ch(m)), k - 2)
                    if k < 4:
                        lk(i)
                i.then_inc(*done("c_cnv", (g, j)))
                dve.wait_ge(*at("c_cnv", (g, j)))
                nc.vector.memset(ssx[:, 0, 1:2], 0.0).then_inc(*done("read_v", ((("xs", "xs", "bc")[j], g), (0, 1, 0)[j])))

            def hb(v, n=8):
                return v.rearrange("p (h d) -> p h d", h=n)

            def decay_rows(g, u):
                c, r, hf = u // 4, (u // 2) % 2, u % 2
                if u >= 2:
                    dve.wait_ge(*at("s_l", (g, u - 2)))
                a0 = 32 * r + 8 * g + 4 * hf
                tt(am[u % 2][:, :, :], bc(cc("le" if r == 0 else "ge"), 1, 4), bc(dtt[:, 2 + c, a0:a0 + 4], 2, P), ALU.mult)\
                    .then_inc(*done("s_am", (g, u)))

            def ssd(g):
                fill = (lambda j: ssd_conv(g + 1, j)) if g + 1 < SG else (lambda j: None)
                X = xs[g % 2]
                y = hn[:, :, (g % 2) * 512:(g % 2) * 512 + 512]
                if g == 0:
                    dve.wait_ge(*at("ex"))
                dve.wait_ge(*at("s_bq", g))
                nc.vector.tensor_copy(btm[:, :, :], PS[:, 6, 0:S].rearrange("p (a b) -> p a b", a=2))
                pq = PS[:, 6, S:2 * S].rearrange("p (a b) -> p a b", a=2)
                tt(qk[:, 0, :, :], pq, bc(cc("le"), 1, 2), ALU.mult)
                lk(tt(qk[:, 1, :, :], pq, bc(cc("gt"), 1, 2), ALU.mult))
                dve.wait_ge(*at("s_xs", g))
                for r in range(2):
                    for t in range(NT):
                        i = tt(hb(vfb[:, r, t, :]), hb(X[:, t, :]),
                               bc(dtt[:, t, 32 * r + 8 * g:32 * r + 8 * g + 8], 2, DH), ALU.mult)
                lk(i)
                exv = dtt[:, 8:10, :].rearrange("p a b -> p (a b)")
                for r in range(2):
                    i = tt(hb(vt[:, r, :]), hb(vfb[:, r, r, :]), bc(exv[:, 32 * r + 8 * g:32 * r + 8 * g + 8], 2, DH), ALU.mult)
                i.then_inc(*done("s_v", g))
                decay_rows(g, 0)
                decay_rows(g, 1)
                if g >= 2:
                    dve.wait_ge(*at("turned", (("y", g - 2), 3)))
                dve.wait_ge(*at("s_yi", g))
                for r in range(2):
                    i = tt(hb(y[:, 1 - r, :]), hb(PS[:, 4 + r, :]),
                           bc(exv[:, 64 + 32 * r + 8 * g:64 + 32 * r + 8 * g + 8], 2, DH), ALU.mult)
                i.then_inc(*done("s_yie", g))
                dve.wait_ge(*at("s_yie", g))
                for u in range(8):
                    c, r, hf = u // 4, (u // 2) % 2, u % 2
                    dve.wait_ge(*at("s_e", (g, u)))
                    tt(ee[u % 2][:, :, :], ee[u % 2][:, :, :], bc(qk[:, r, c, :], 1, 4), ALU.mult).then_inc(*done("s_m", (g, u)))
                    if u + 2 < 8:
                        decay_rows(g, u + 2)
                    if u in (2, 4, 6):
                        fill(u // 2 - 1)
                dve.wait_ge(*at("s_pv", (g, 7)))
                for c in range(NT):
                    tt(y[:, c, :], y[:, c, :], PS[:, 7 - c, :], ALU.add)
                    i = tt(hb(X[:, c, :]), hb(X[:, c, :]), bc(dtt[:, 6, 8 * g:8 * g + 8], 2, DH), ALU.mult)
                lk(i)
                for c in range(NT):
                    i = tt(y[:, c, :], y[:, c, :], X[:, c, :], ALU.add)
                lk(i)
                dve.wait_ge(*read((("z", g), 1)))
                for c in range(NT):
                    i = tt(y[:, c, :], y[:, c, :], zt[g % 2][:, c, :], ALU.mult)
                lk(i)
                for c in range(NT):
                    i = nc.vector.tensor_tensor_reduce(out=X[:, c, :], in0=y[:, c, :], in1=y[:, c, :], scale=1.0, scalar=0.0,
                                                       op0=ALU.mult, op1=ALU.add, accum_out=st[:, 96 + c:97 + c])
                i.then_inc(*done("s_ss", g))
                dve.wait_ge(*at("root", ("s", g)))
                lk(nc.vector.reciprocal(st[:, 100:102], st[:, 98:100]))
                for c in range(NT):
                    i = ts(y[:, c, :], y[:, c, :], st[:, 100 + c:101 + c], None, ALU.mult)
                i.then_inc(*done("s_y", g))
                T_lo(("y", g), 4, (8 + 4 * g) % 16, 4, lambda k: col("ssdn", 4 * g + k))

            for j in range(3):
                ssd_conv(0, j)
            for g in range(SG):
                ssd(g)
            post(2)
            norm(3, "ffn1")
            ffn(1)
            post(3)
            norm(4, "sec")

            def head_norm(nm, a, b0):
                for t in range(NT):
                    dve.wait_ge(*at("q_sq", (nm, t)))
                    i = nc.vector.tensor_reduce(st[:, 104 + 8 * t:112 + 8 * t], h3(sqb[:, t, :]), AXX, ALU.add)
                i.then_inc(*done("q_ss", nm))
                dve.wait_ge(*at("root", ("q", nm)))
                lk(nc.vector.reciprocal(st[:, 136:152], st[:, 120:136]))
                if a >= 2:
                    dve.wait_ge(*at("turned", (("qa", "ka")[a - 2], 3)))
                for t in range(NT):
                    o = hn[:, t, 512 * (a % 2):512 * (a % 2) + 512]
                    if nm != "ksv":
                        i = tt(h3(o), h3(PS[:, b0 + t, :]), bc(st[:, 136 + 8 * t:144 + 8 * t], 2, DH), ALU.mult)
                    else:
                        for w in range(2):
                            for r in range(2):
                                i = tt(o[:, 256 * w:256 * w + 256].rearrange("p (g r d) -> p g r d", g=2, r=2)[:, :, r, :],
                                       PS[:, b0 + t, 256 * w:256 * w + 128].rearrange("p (g d) -> p g d", g=2),
                                       bc(st[:, 136 + 8 * t + 4 * w:138 + 8 * t + 4 * w], 2, DH), ALU.mult)
                    i.then_inc(*done("read_v", (nm, t)))

            head_norm("qa", 0, 0)
            head_norm("ka", 1, 2)
            head_norm("qb", 2, 2)

            def windows(a, b):
                lk(nc.vector.memset(XC[a][:, :, :], 0.0))
                pos = cols[:, col_at[("posk", "posv")[a]]:col_at[("posk", "posv")[a]] + 16]
                for g in range(2):
                    for r in range(2):
                        base = PS[64 * r:64 * r + 64, b, g * S + r:g * S + r + 1]
                        src = bass.AP(base.tensor, base.offset, [list(base.ap[0]), [2, 16], [16, NCMP]])
                        i = tt(XC[a][64 * r:64 * r + 64, :, 16 * g:16 * g + NCMP], src,
                               bc(pos[64 * r:64 * r + 64, :], 2, NCMP), ALU.add)
                i.then_inc(*done("read_v", (("kc", "vc")[a], 0)))
                dve.wait_ge(*read((("kc", "vc")[a], 0)))

            dve.wait_ge(*at("w_used", slot_no[("vc", 0)]))
            windows(0, 0)
            windows(1, 1)
            for a in range(2):
                nc.vector.memset(st[:, 152 + a:153 + a], 0.0).then_inc(*done("x_c", a))
                dve.wait_ge(*at("x_hi", a))
                tt(Tl[:, 8 + 2 * a:10 + 2 * a, :].rearrange("p a (b c) -> p (a b) c", c=32), XC[a][:, :, :],
                   Th[:, 8 + 2 * a:10 + 2 * a, :].rearrange("p a (b c) -> p (a b) c", c=32).bitcast(F32), ALU.subtract)\
                    .then_inc(*done("x_lo", a))
            head_norm("ksv", 3, 2)
            dve.wait_ge(*at("c_gelu", 1))
            for m in range(2):
                i = nc.vector.tensor_copy(hidr[:, m, :].rearrange("p (g h c) -> p g h c", g=2, h=4),
                                          bc(hid[:, 1, m, :].rearrange("p (g c) -> p g c", g=2), 2, 4))
            i.then_inc(*done("c_rep"))
            dve.wait_ge(*at("root", "ck"))
            lk(nc.vector.reciprocal(st[0:32, 14:15], st[0:32, 13:14]))
            for r in range(2):
                i = ts(kcm[0:32, 0, DH * r:DH * r + DH], PS[0:32, 4, 64:64 + DH], st[0:32, 14:15], None, ALU.mult)
            i.then_inc(*done("c_kn"))
            dve.wait_ge(*at("c_v"))
            tt(vbd[:, :, :], bc(PS[:, 5, 64:64 + DH], 1, 8), bc(cc("blk"), 2, DH), ALU.mult).then_inc(*done("c_vbd"))
            dve.wait_ge(*at("c_s"))
            for t in range(NT):
                for r in range(2):
                    i = tt(cpr[:, t, :].rearrange("p (h r c) -> p h r c", h=4, r=2)[:, :, r, :],
                           PS[:, 4 + r, 64 * t:64 * t + 64].rearrange("p (h c) -> p h c", h=4),
                           bc(cc("cneg")[:, 16 * t:16 * t + 16], 1, 4), ALU.add)
            lk(i)
            c3 = cpr[:, :, :].rearrange("p t (h c) -> p (t h) c", h=NH)
            lk(nc.vector.tensor_reduce(st[:, 104:120], c3, AXX, ALU.max))
            tt(c3, c3, bc(st[:, 104:120], 2, 16), ALU.subtract).then_inc(*done("c_sub"))
            dve.wait_ge(*at("c_exp"))
            lk(nc.vector.tensor_reduce(st[:, 120:136], c3, AXX, ALU.add))
            for t in range(NT):
                v = cpr[:, t, :].rearrange("p (h c) -> p h c", h=NH)
                i = tt(v, v, bc(cc("cval")[:, 16 * t:16 * t + 16], 1, NH), ALU.mult)
            i.then_inc(*done("c_p"))
            lk(nc.vector.reciprocal(st[:, 136:152], st[:, 120:136]))
            dve.wait_ge(*read(("gb", 1)))
            gates = lambda k: gb[:, :, :].rearrange("p t (h k) -> p t h k", k=3)[:, :, :, k]
            c8 = st[:, 136:152].rearrange("p (t h) -> p t h", t=NT)
            lk(tt(c8, c8, gates(0), ALU.mult))
            dve.wait_ge(*at("c_o"))
            for t in range(NT):
                i = tt(h3(hn[:, t, 512:D]), h3(PS[:, 6 + t, :]), bc(st[:, 136 + 8 * t:144 + 8 * t], 2, DH), ALU.mult)
            i.then_inc(*done("c_oe"))
            dve.wait_ge(*at("c_oe"))
            dve.wait_ge(*at("load_tb", 0))

            def moba_write(j, rc, o):
                return tt(hn[:, :, DH * j:DH * (j + 1)], o, bc(rc, 2, DH), ALU.mult)

            def nsa_write(j, rc, o):
                w, h = j // NH, j % NH
                lk(tt(rc, rc, gates(1 + w)[:, :, h], ALU.mult))
                for t in range(NT):
                    ob = hn[:, t, 512 + DH * h:512 + DH * (h + 1)]
                    i = stt3(out=ob, in0=o[:, t, :], scalar=rc[:, t:t + 1], in1=ob, op0=ALU.mult, op1=ALU.add)
                return i

            tbias = lambda i, t: tb[:, i % NH, P:S] if t == 0 else tb[:, i % NH, :]
            attention("moba", NH, tbias, True, moba_write)
            dve.wait_ge(*at("load_tb", 1))
            attention("nsa", 2 * NH, tbias, True, nsa_write)
            dve.wait_ge(*at("a_o", ("nsa", 2 * NH - 1)))
            dve.wait_ge(*read(("zb", 1)))
            for t in range(NT):
                tt(hn[:, t, 0:512], hn[:, t, 0:512], za[:, t, :], ALU.mult)
                i = tt(hn[:, t, 512:D], hn[:, t, 512:D], zb[:, t, :], ALU.mult)
            i.then_inc(*done("y2"))
            T_lo("y2", KD, 8, 4, lambda k: None)
            for n in range(2):
                for a, nm in enumerate(("YA", "YB")):
                    dve.wait_ge(*read(((("GA", "GB")[a], n), 1)))
                    dve.wait_ge(*at("w_used", slot_no[((nm, n), 0)]))
                    for t in range(NT):
                        o = hn[:, t, 512 * n:512 * n + 512]
                        i = tt(o if a == 0 else sg[1][:, t, :], sg[a][:, t, :], PS[:, 4 + 2 * a + t, :], ALU.mult)
                    lk(i)
                    if a == 1:
                        for t in range(NT):
                            o = hn[:, t, 512 * n:512 * n + 512]
                            i = tt(o, o, sg[1][:, t, :], ALU.add)
                        lk(i)
                    nc.vector.memset(st[:, 154:155], 0.0).then_inc(*done("mrg", (n, a)))
            T_lo("mrg", KD, 0, 0, lambda k: None)
            dve.wait_ge(*at("w_used", slot_no[("fo", 3)]))
            for t in range(NT):
                for hf in range(2):
                    o = x[:, t, 512 * hf:512 * hf + 512]
                    i = tt(o, o, PS[:, 4 + 2 * t + hf, :], ALU.add)
            i.then_inc(*done("x", (5, NT - 1)))
        return C.marks


_INS = ["x", "norm_mix_pre", "norm_mix_post", "norm_ffn_pre", "norm_ffn_post", "ab_w_in", "ab_ret_decay_logit",
        "ab_ret_gn_g", "ab_na_rpb", "ab_w_out", "c_w_in", "c_conv_w", "c_conv_b", "c_dt_bias", "c_a_log", "c_d_skip",
        "c_norm_g", "c_w_out", "ffn_w_up", "ffn_conv_w", "ffn_conv_b", "ffn_w_down", "norm_w_2", "w_in_2",
        "q_norm_a_2", "k_norm_a_2", "q_norm_b_2", "k_norm_cmp_2", "k_norm_sel_2", "k_norm_win_2", "cmp_pos_k_2",
        "cmp_w1_k_2", "cmp_w2_k_2", "cmp_pos_v_2", "cmp_w1_v_2", "cmp_w2_v_2", "rel_bias_2", "w_branch_a_2",
        "w_branch_b_2", "w_out_2"]


def kernel(**inputs):
    import numpy as _np
    import concourse.bacc as _bacc
    from concourse import mybir as _mybir
    from concourse.bass_utils import run_bass_kernel_spmd as _run

    arrays = {f"in_{n}_dram": _np.ascontiguousarray(inputs[n]) for n in _INS}
    for n, a in (("const_table", CONST_TABLE), ("const_pfb", CONST_PFB), ("const_onehot", CONST_ONEHOT),
                 ("const_negs", CONST_NEGS)):
        arrays[f"in_{n}_dram"] = a
    known = None
    for _ in range(2):
        nc = _bacc.Bacc("TRN2", target_bir_lowering=False, num_devices=1)
        handles = {name[3:-5]: nc.dram_tensor(name, a.shape, _mybir.dt.from_np(a.dtype), kind="ExternalInput").ap()
                   for name, a in arrays.items()}
        out = nc.dram_tensor("out_0_dram", (1, S, D), _mybir.dt.float32, kind="ExternalOutput").ap()
        known = build(nc, handles, out, known)
    r = _run(nc, [arrays], core_ids=[0])
    return r.results[0]["out_0_dram"]
```

```python
from contextlib import ExitStack

import numpy as np

import concourse.bass as bass
from concourse import mybir

ALU = mybir.AluOpType
ACT = mybir.ActivationFunctionType
F32 = mybir.dt.float32
F32R = mybir.dt.float32r
AXX = mybir.AxisListType.X

P = 128
S = 256
NT = S // P
D = 1024
KD = D // P
EPS = 1e-6
NEG = -1e30
DH = 64
NH = 8
FF = 2816
FI = FF // 256
SI = 2048
SG = 4
SHG = 8
XBC = SI + 2 * SG * P
CL, CS, NCMP = 32, 16, 15
GW = 64
NRAW, NHI, NLO = 4, 3, 3
SLOT = 2048


class Counts:

    def __init__(self, nc, ctx, known):
        self.nc, self.ctx, self.known = nc, ctx, known
        self.sems, self.count, self.marks = {}, {}, {}

    def sem(self, family):
        if family not in self.sems:
            self.sems[family] = self.ctx.enter_context(self.nc.semaphore(family))
            self.count[family] = 0
        return self.sems[family]

    def done(self, family, key=0, by=1):
        s = self.sem(family)
        self.count[family] += by
        assert (family, key) not in self.marks or by == 16, (family, key)
        self.marks[(family, key)] = self.count[family]
        return s, by

    def at(self, family, key=0):
        s = self.sem(family)
        if self.known is None:
            return s, max(1, self.marks.get((family, key), 1))
        return s, self.known[(family, key)]


def bc(ap, axis, n):
    a = ap.unsqueeze(axis)
    shape = list(a.shape)
    shape[axis] = n
    return a.to_broadcast(shape)


def shape_constants():
    i = np.arange(P)
    ident = np.eye(P)
    u, t = i[:, None], i[None, :]
    le, gt, lt, ge = (u <= t), (u > t), (u < t), (u >= t)
    half = DH // 2
    inv = (1.0 / (np.float32(10000.0) ** (np.arange(half, dtype=np.float32) / np.float32(half)))).astype(np.float32)
    ang = (np.arange(S, dtype=np.float32)[:, None] * inv[None, :]).astype(np.float32).astype(np.float64)
    cos = np.concatenate([np.cos(ang), np.cos(ang)], 1).reshape(NT, P, DH).transpose(1, 0, 2).reshape(P, -1)
    sin = np.concatenate([-np.sin(ang), np.sin(ang)], 1).reshape(NT, P, DH).transpose(1, 0, 2).reshape(P, -1)
    s_all = (np.arange(NT)[None, :, None] * P + i[:, None, None])
    dist = np.arange(S)[None, None, :] - s_all
    pf, pb = np.maximum(dist, 0).reshape(P, -1), np.maximum(-dist, 0).reshape(P, -1)
    qc = i % GW
    kc = np.arange(GW)
    c0 = np.clip(qc - 8, 0, GW - 16)[:, None]
    nm = np.where((kc[None] >= c0) & (kc[None] < c0 + 16), 0.0, NEG)
    tok = (np.arange(NT)[None, :, None] * P + i[:, None, None])
    cend = np.arange(16)[None, None, :] * CS + CL - 1
    cv = (cend <= tok) & (np.arange(16)[None, None, :] < NCMP)
    cneg = np.where(cv, 0.0, NEG).reshape(P, -1)
    blk = (i[:, None] // 16 == np.arange(8)[None, :])
    parts = [("ident", ident), ("le", le), ("gt", gt), ("lt", lt), ("ge", ge), ("cos", cos), ("sin", sin),
             ("nm", nm), ("cneg", cneg), ("cval", cv.reshape(P, -1)), ("blk", blk)]
    at, n = {}, 0
    for name, a in parts:
        at[name] = (n, n + a.shape[1])
        n += a.shape[1]
    table = np.concatenate([a.astype(np.float32) for _, a in parts], 1)
    pfb = np.concatenate([pf, pb], 1).astype(np.float32)
    dd = 255 - np.arange(384)
    n_ = np.maximum(dd, 0)
    nf = np.maximum(n_, 16).astype(np.float32)
    large = 16 + (np.log(nf / np.float32(16)) / np.float32(np.log(64.0)) * np.float32(16)).astype(np.int32)
    bucket = np.where(n_ < 16, n_, np.minimum(large, 31))
    onehot = ((np.arange(32)[:, None] == bucket[None, :]) & (dd[None, :] >= 0)).astype(np.float32)
    negs = np.tile(np.where(dd >= 0, 0.0, NEG)[None, :], (16, 1)).astype(np.float32)
    return at, table, pfb, onehot, negs


CONST_AT, CONST_TABLE, CONST_PFB, CONST_ONEHOT, CONST_NEGS = shape_constants()
NCONST = CONST_TABLE.shape[1]


def vector_rows(I):
    r = lambda ap: ap.rearrange("(k p) -> k p", p=P)
    rows = []
    rows.append(("mix1", r(I["norm_mix_pre"][1])))
    for l in range(2):
        rows.append((f"ffn{l}", r(I["norm_ffn_pre"][l])))
    rows.append(("sec", r(I["norm_w_2"][0])))
    rows.append(("gn", r(I["ab_ret_gn_g"][0])))
    rows.append(("ssdn", r(I["c_norm_g"][0])))
    rows.append(("posk", I["cmp_pos_k_2"][0].rearrange("(j r) d -> j (r d)", r=2)))
    rows.append(("posv", I["cmp_pos_v_2"][0].rearrange("(j r) d -> j (r d)", r=2)))
    for k in range(5):
        rows.append((f"cw{k}", r(I["c_conv_w"][0, k])))
    rows.append(("cb", r(I["c_conv_b"][0])))
    for l in range(2):
        for k in range(3):
            rows.append((f"fw{l}{k}", r(I["ffn_conv_w"][l, k])))
        rows.append((f"fb{l}", r(I["ffn_conv_b"][l])))
    return rows


def build(nc, I, out, known):
    ctx = ExitStack()
    with ctx:
        C = Counts(nc, ctx, known)
        done, at = C.done, C.at

        def sb(name, shape, dt=F32):
            return ctx.enter_context(nc.sbuf_tensor(name, shape, dt))

        PS = ctx.enter_context(nc.psum_tensor("PS", [P, 8, 512], F32))
        x = sb("x", [P, NT, D])
        hn = sb("hn", [P, NT, D])
        Th = sb("Th", [P, 16, S], F32R)
        Tl = sb("Tl", [P, 16, S], F32R)
        aTh = sb("aTh", [P, 2, 2, S], F32R)
        aTl = sb("aTl", [P, 2, 2, S], F32R)
        raw = [sb(f"raw{i}", [P, SLOT]) for i in range(NRAW)]
        whi = [sb(f"whi{i}", [P, SLOT], F32R) for i in range(NHI)]
        wlo = [sb(f"wlo{i}", [P, SLOT], F32R) for i in range(NLO)]
        gpost = sb("gpost", [P, D])
        cst = sb("cst", [P, NCONST])
        rows = vector_rows(I)
        col_at, n = {}, 0
        for name, ap in rows:
            k = ap.shape[0]
            if n % P + k > P:
                n += P - n % P
            col_at[name] = n
            n += k
        NR = -(-(n + 1) // P)
        qn = NR * P
        cols = sb("cols", [P, NR * P + 16])
        col_at["mix0"] = NR * P + 8
        st = sb("st", [P, 160])
        eps = sb("eps", [P, 1])
        sqj = sb("sqj", [P, 512])
        A = sb("arena", [P, 14800])

        def cc(name):
            a, b = CONST_AT[name]
            return cst[:, a:b]

        ident = cc("ident")

        def col(name, j=0):
            c = col_at[name] + j
            return cols[:, c:c + 1]

        slots, slot_no = [], {}

        def add(name, parts, width):
            slot_no[name] = len(slots)
            slots.append((parts, width))

        def wide(name, w, k0, c0, nk, nc_):
            add(name, [((nk, nc_, 0, nc_), w[k0 * P:(k0 + nk) * P, c0:c0 + nc_])], nk * nc_)

        def tm(name, w, c0, k0=0):
            for hf in range(2):
                wide((name, hf), w, k0 + 4 * hf, c0, 4, 512)

        def fm(name, w, c0, k0=0, j=0):
            wide((name, j), w, k0, c0, 8, 256)

        def dn(name, w, n, k0=0):
            for j in range(n):
                wide((name, j), w, k0 + 2 * j, 0, 2, 1024)

        def ffn_slots(l):
            up, down = I["ffn_w_up"][l], I["ffn_w_down"][l]
            for i in range(FI + 1):
                if i < FI:
                    wide(("G", l, i), up, 0, 256 * i, 8, 256)
                    wide(("V", l, i), up, 0, FF + 256 * i, 8, 256)
                if i >= 1:
                    wide(("D", l, i - 1), down, 2 * (i - 1), 0, 2, 1024)

        win = I["ab_w_in"][0]
        tm("rq", win, 0)
        tm("rk", win, 512)
        tm("rv", win, 1024)
        for j in range(2):
            fm("nq", win, 2048 + 256 * j, j=j)
        for j in range(2):
            fm("nk", win, 2560 + 256 * j, j=j)
        tm("nv", win, 3072)
        tm("rg", win, 1536)
        dn("mo0", I["ab_w_out"][0], 4)
        ffn_slots(0)
        cwin = I["c_w_in"][0]
        wide(("dt", 0), cwin, 0, SI + XBC, 8, 64)
        for g in range(SG):
            add((("bc", g), 0), [((8, 256, 128 * m, 128 * m + 128),
                                  cwin[:, 2 * SI + 512 * m + P * g:2 * SI + 512 * m + P * (g + 1)]) for m in range(2)],
                SLOT)
            for j in range(2):
                fm(("xs", g), cwin, SI + 512 * g + 256 * j, j=j)
            tm(("z", g), cwin, 512 * g)
        dn("mo1", I["c_w_out"][0], 8)
        ffn_slots(1)
        w2 = I["w_in_2"][0]
        KV = 2560
        tm("qa", w2, 0)
        tm("ka", w2, 512)
        tm("va", w2, 1024)
        tm("qb", w2, 2048)
        for n, nm in enumerate(("kc", "vc")):
            add((nm, 0), [((8, 256, 128 * g + 64 * r, 128 * g + 64 * r + 64),
                           w2[:, KV + 128 * n + 64 * g:KV + 128 * n + 64 * g + 64])
                          for g in range(2) for r in range(2)], SLOT)
        tm("ksv", w2, KV + 256)
        wide(("gb", 0), w2, 0, KV + 768, 8, 24)
        tm("za", w2, 1536)
        tm("zb", w2, KV + 792)
        for nm in ("k", "v"):
            for j in range(2):
                fm("w1" + nm, I["cmp_w1_" + nm + "_2"][0], 0, k0=8 * j, j=j)
        GM = KV + 792 + 512
        for n in range(2):
            tm(("GA", n), w2, GM + 512 * n)
            tm(("GB", n), w2, GM + D + 512 * n)
            wide((("YA", n), 0), I["w_branch_a_2"][0], 0, 512 * n, 4, 512)
            wide((("YB", n), 0), I["w_branch_b_2"][0], 0, 512 * n, 4, 512)
        dn("fo", I["w_out_2"][0], 4)
        NS = len(slots)

        by_vector = {slot_no[("D", l, i)] for l in range(2) for i in range(FI)}

        def view(a, *shape):
            n = int(np.prod(shape))
            v = A[:, a:a + n]
            if len(shape) == 2:
                v = v.rearrange("p (a b) -> p a b", a=shape[0])
            elif len(shape) == 3:
                v = v.rearrange("p (a b c) -> p a b c", a=shape[0], b=shape[1])
            return v

        rqk = [view(1024 * i, NT, 512) for i in range(2)]
        nabias = view(0, NH, 6 * GW)
        rv, rg, nv = (view(3072 + 1024 * i, NT, 512) for i in range(3))
        rqT, rkT, nqT, nkT = (view(6144 + 1024 * i, 4, S) for i in range(4))
        pfb = view(10240, 2, 512)
        dcy = [view(11264 + 512 * i, 512) for i in range(2)]
        msc = [view(12288 + 512 * i, 512) for i in range(2)]
        spxs = {"ret": view(13400, 8, 16), "ssd": view(8448, 8, 128)}
        lg = A[:, 14500:14516]
        brow = A[:, 14516:14532]
        zt = [view(1024 * i, NT, 512) for i in range(2)]
        xs = [view(2048 + 1024 * i, NT, 512) for i in range(2)]
        bct = [view(4096 + 512 * i, 2, S) for i in range(2)]
        btm = view(5120, NT, P)
        vfb = view(5376, 2, NT, 512)
        vt = view(7424, 2, 512)
        am = [view(8448 + 512 * i, 4, P) for i in range(2)]
        ee = [view(9472 + 512 * i, 4, P) for i in range(2)]
        cvb = view(10496, 6, S)
        qk = view(12032, 2, NT, P)
        stt = view(12544, 2, 512)
        dtt = view(13568, 12, 64)
        qaT, kaT, qbT = (view(1024 * i, 4, S) for i in range(3))
        va, za, zb = (view(3072 + 1024 * i, NT, 512) for i in range(3))
        kswT = view(6144, 4, S)
        vsw = view(7168, NT, 2, P)
        tb = view(7680, NH, S)
        sqb = view(9728, NT, 512)
        XC = [view(10752 + 512 * i, 16, 32) for i in range(2)]
        sc = [view(10752 + 512 * i, NT, S) for i in range(2)]
        pt = [view(11776 + 512 * i, 4, P) for i in range(2)]
        hid = view(12800, 2, 2, 32)
        hidr = view(12928, 2, P)
        vbd = view(13184, 8, DH)
        kcm = view(13696, 2, P)
        kcT = view(13952, 32)
        w2c = view(13984, 2, 2, DH)
        gb = view(14240, NT, 24)
        cpr = view(14288, NT, P)
        cpt = view(14544, NT, P)
        sg = [view(1024 * i, NT, 512) for i in range(2)]
        fac = [view(1024 * i, 4, S) for i in range(2)]
        fpr = [view(2048 + 512 * i, 2, S) for i in range(2)]
        rowb = view(6144, NR + 1, P)
        rowm = A[0:8, 7040:7168]
        oneh = A[0:32, 7168:7552]
        negs = A[0:16, 7552:7936]
        relb = A[0:32, 7936:7952]
        t5r = A[0:16, 13600:13984]

        chain = {}

        def link(eng, name, ins):
            chain[name] = chain.get(name, 0) + 1
            ins.then_inc(*done(name + "_chain", chain[name]))
            eng.wait_ge(*at(name + "_chain", chain[name]))

        def low(n):
            return at("w_lo_v" if n in by_vector else "w_lo", n)

        def read(key):
            by_scalar = known is None or ("read_a", key) in known
            return at("read_a" if by_scalar else "read_v", key)

        toe = nc.dram_tensor("t5_rows", [16, P, 384], F32, kind="Internal").ap()
        narep = nc.dram_tensor("na_rows", [NH, GW, 465], F32, kind="Internal").ap()
        block = ctx.enter_context(nc.Block())

        @block.sync
        def _(sp):
            def set_up_loads():
                sp.dma_start(cst[:, P:NCONST], I["const_table"][:, P:NCONST]).then_inc(*done("load_cst", 0, 16))
                sp.wait_ge(*at("rows_clear"))
                for name, ap in rows:
                    c = col_at[name]
                    sp.dma_start(rowb[c % P:c % P + ap.shape[0], c // P, :], ap).then_inc(*done("load_rows", 0, 16))
                for j, nm in enumerate(("q_norm_a_2", "k_norm_a_2", "q_norm_b_2", "k_norm_sel_2", "k_norm_win_2", "k_norm_cmp_2")):
                    sp.dma_start(rowb[j:j + 1, NR, :].rearrange("p (r d) -> p r d", r=2),
                                 bc(I[nm], 1, 2)).then_inc(*done("load_rows", 0, 16))
                sp.dma_start(oneh, I["const_onehot"]).then_inc(*done("load_t5", 0, 16))
                sp.dma_start(negs, I["const_negs"]).then_inc(*done("load_t5", 0, 16))
                sp.dma_start(relb, I["rel_bias_2"]).then_inc(*done("load_t5", 0, 16))
                sp.dma_start(brow, I["ab_ret_decay_logit"].rearrange("a b c -> a (b c)").to_broadcast([P, 16]))\
                    .then_inc(*done("load_dl", 0, 16))
                sp.dma_start(narep, bc(I["ab_na_rpb"][0].rearrange("h a b -> h (a b)"), 1, GW)).then_inc(*done("na_rows", 0, 16))

            for t in range(NT):
                sp.dma_start(x[:, t, :], I["x"][0, t * P:(t + 1) * P]).then_inc(*done(f"load_x{t}", 0, 16))
            for n, (parts, width) in enumerate(slots):
                if n == NRAW:
                    set_up_loads()
                if n >= NRAW:
                    sp.wait_ge(*low(n - NRAW))
                for (nk, nc_, a, b), src in parts:
                    dst = raw[n % NRAW][:, 0:nk * nc_].rearrange("p (k c) -> p k c", k=nk)[:, :, a:b]
                    sp.dma_start(dst, src.rearrange("(k p) c -> p k c", p=P))\
                        .then_inc(*done(f"w_raw{n % NRAW}", n, 16))
            sp.wait_ge(*at("x", (5, NT - 1)))
            sp.dma_start(out[0].rearrange("(t p) d -> p t d", p=P), x[:, :, :]).then_inc(*done("stored", 0, 16))
            sp.wait_ge(*at("stored", 0))

        @block.gpsimd
        def _(pool):
            for n, (parts, width) in enumerate(slots):
                if n in by_vector:
                    continue
                pool.wait_ge(*at("w_hi", n))
                if n >= NLO:
                    pool.wait_ge(*at("w_used", n - NLO))
                nc.gpsimd.tensor_tensor(wlo[n % NLO][:, 0:width], raw[n % NRAW][:, 0:width],
                                        whi[n % NHI][:, 0:width].bitcast(F32), ALU.subtract)\
                    .then_inc(*done("w_lo", n))

        @block.tensor
        def _(pe):
            mm = nc.tensor.matmul

            def three(o, wh, wl, ah, al, first, last, moving_w):
                if moving_w:
                    mm(o, ah, wh, start=first, stop=False)
                    mm(o, ah, wl, start=False, stop=False)
                    return mm(o, al, wh, start=False, stop=last)
                mm(o, wh, ah, start=first, stop=False)
                mm(o, wh, al, start=False, stop=False)
                return mm(o, wl, ah, start=False, stop=last)

            def slot_tm(name, b0, kt0, first, last, ncol=512, nk=4, fresh=None):
                n = slot_no[name]
                pe.wait_ge(*low(n))
                h, l = whi[n % NHI], wlo[n % NLO]
                for k in range(nk):
                    if fresh:
                        pe.wait_ge(*at("T_lo", (fresh, kt0 % KD + k)))
                    for t in range(NT):
                        i = three(PS[:, b0 + t, 0:ncol], h[:, k * ncol:(k + 1) * ncol], l[:, k * ncol:(k + 1) * ncol],
                                  Th[:, kt0 + k, t * P:(t + 1) * P], Tl[:, kt0 + k, t * P:(t + 1) * P],
                                  first and k == 0, last and k == nk - 1, True)
                i.then_inc(*done("w_used", n))

            def block_tm(name, b0, fresh=None):
                slot_tm((name, 0), b0, 0, True, False, fresh=fresh)
                slot_tm((name, 1), b0, 4, False, True, fresh=fresh)

            def slot_fm(name, b, fresh=None):
                n = slot_no[name]
                pe.wait_ge(*low(n))
                h, l = whi[n % NHI], wlo[n % NLO]
                for m in range(2):
                    for k in range(KD):
                        if fresh and m == 0:
                            pe.wait_ge(*at("T_lo", (fresh, k)))
                        c = k * 256 + m * P
                        i = three(PS[:, b, m * S:(m + 1) * S], h[:, c:c + P], l[:, c:c + P], Th[:, k, :], Tl[:, k, :],
                                  k == 0, k == KD - 1, False)
                i.then_inc(*done("w_used", n))

            def slot_dn(name, ah, al, first, last, b0=4):
                n = slot_no[name]
                pe.wait_ge(*low(n))
                h, l = whi[n % NHI], wlo[n % NLO]
                for k, t in ((0, 0), (1, 0), (0, 1), (1, 1)) if last else ((0, 0), (0, 1), (1, 0), (1, 1)):
                    for hf in range(2):
                        c = k * D + hf * 512
                        i = three(PS[:, b0 + 2 * t + hf, :], h[:, c:c + 512], l[:, c:c + 512], ah(k, t), al(k, t),
                                  first and k == 0, last and k == 1, True)
                    if last and (k, t) == (1, 0):
                        i.then_inc(*done("sum_0", n))
                i.then_inc(*done("w_used", n))

            def tr(o, src, idn):
                return nc.tensor.transpose(o, src, idn)

            def to_T(name, src, nk, b0):
                for k in range(nk):
                    for t in range(NT):
                        i = tr(PS[:, b0 + k // 2, (k % 2) * S + t * P:(k % 2) * S + (t + 1) * P],
                               src[:, t, k * P:(k + 1) * P], ident)
                    i.then_inc(*done("turned", (name, k)))

            def norm_T(l):
                pe.wait_ge(*at("n_hn", (l, NT - 1)))
                to_T(("n", l), hn, KD, 4)

            def out_proj(name, n, kt_of, fresh=None):
                for j in range(n):
                    if fresh:
                        pe.wait_ge(*at("T_lo", (fresh, 2 * j + 1)))
                    slot_dn((name, j), lambda k, t: Th[:, kt_of(2 * j + k), t * P:(t + 1) * P],
                            lambda k, t: Tl[:, kt_of(2 * j + k), t * P:(t + 1) * P], j == 0, j == n - 1)

            def ffn(l):
                for i in range(FI + 1):
                    if i < FI:
                        if i >= 2:
                            pe.wait_ge(*at("f_conv", (l, i - 2)))
                        slot_fm(("G", l, i), 2 * (i % 2), ("n", 2 * l + 1) if i == 0 else None)
                        if i == 0:
                            pe.wait_ge(*at("T_lo", (("n", 2 * l + 1), KD - 1)))
                        slot_fm(("V", l, i), 2 * (i % 2) + 1)
                    if i >= 1:
                        pe.wait_ge(*at("f_alo", (l, i - 1)))
                        p = (i - 1) % 2
                        slot_dn(("D", l, i - 1), lambda k, t: aTh[:, p, k, t * P:(t + 1) * P],
                                lambda k, t: aTl[:, p, k, t * P:(t + 1) * P], i == 1, i == FI)

            pe.wait_ge(*at("load_ident"))
            pe.wait_ge(*at("load_mix0"))
            tr(PS[:, 0, 0:8], rowm, ident[0:8, 0:8]).then_inc(*done("mix0_T"))
            norm_T(0)
            pe.wait_ge(*at("mix0_col"))
            block_tm("rq", 0, ("n", 0))
            pe.wait_ge(*at("load_rows"))
            for r in range(NR):
                i = tr(PS[:, 4 + r // 4, (r % 4) * P:(r % 4 + 1) * P], rowb[:, r, :], ident)
            i = tr(PS[:, 6, 0:8], rowb[0:8, NR, :], ident[0:8, 0:8])
            pe.wait_ge(*at("load_t5"))
            mm(PS[0:16, 7, 0:384], relb, oneh, start=True, stop=True).then_inc(*done("set_up"))
            block_tm("rk", 2)
            pe.wait_ge(*at("load_cst"))
            pe.wait_ge(*read(("rq", 1)))
            block_tm("rv", 0)
            pe.wait_ge(*at("cols_act"))
            pe.wait_ge(*at("cols"))
            for a, nm in enumerate(("rq", "rk")):
                pe.wait_ge(*at("rope", (nm, 1)))
                to_T(nm, rqk[a], 4, 4 + 2 * a)
            pe.wait_ge(*read(("rk", 1)))
            slot_fm(("nq", 0), 2)
            slot_fm(("nq", 1), 3)
            pe.wait_ge(*at("rT", ("rq", 1)))
            pe.wait_ge(*at("rT", ("rk", 1)))

            def ret_scores(h):
                b, k = (h % 2) * DH, h // 2
                if h >= 2:
                    pe.wait_ge(*at("r_m", h - 2))
                for s in range(NT):
                    i = mm(PS[:, 4 + h % 2, s * S:(s + 1) * S], rkT[b:b + DH, k, s * P:(s + 1) * P],
                           rqT[b:b + DH, k, :], start=True, stop=True)
                i.then_inc(*done("r_s", h))

            def ret_out(h):
                pe.wait_ge(*at("r_m", h))
                if h == 0:
                    pe.wait_ge(*read(("rv", 1)))
                for t in range(NT):
                    for s in range(NT):
                        i = mm(PS[:, 6 + t, h * DH:(h + 1) * DH],
                               msc[h % 2][:, s * S + t * P:s * S + (t + 1) * P],
                               rv[:, s, h * DH:(h + 1) * DH], start=s == 0, stop=s == NT - 1)
                i.then_inc(*done("r_pv", h))

            for h in range(NH + 1):
                if h < NH:
                    ret_scores(h)
                if h >= 1:
                    ret_out(h - 1)
                if h == 3:
                    pe.wait_ge(*read(("rv", 1)))
                    slot_fm(("nk", 0), 0)
                    slot_fm(("nk", 1), 1)
            pe.wait_ge(*read(("nq", 1)))
            block_tm("nv", 2)
            pe.wait_ge(*read(("nk", 1)))
            block_tm("rg", 0)

            def attention(tag, heads, after):
                def scores(i):
                    q, k, _, causal = heads[i]
                    if i >= 2:
                        pe.wait_ge(*at("a_sc", (tag, i - 2)))
                    for t in range(NT):
                        nk = P if causal and t == 0 else S
                        n = mm(PS[:, 4 + i % 2, t * S:t * S + nk], q(t), k(nk), start=True, stop=True)
                    n.then_inc(*done("a_s", (tag, i)))

                def turn(i):
                    causal = heads[i][3]
                    pe.wait_ge(*at("a_exp", (tag, i)))
                    if i >= 1:
                        pe.wait_ge(*at("a_pt", (tag, i - 1)))
                    for t in range(NT):
                        for c in range(1 if causal and t == 0 else 2):
                            n = tr(PS[:, 6, (2 * t + c) * P:(2 * t + c + 1) * P], sc[i % 2][:, t, c * P:(c + 1) * P], ident)
                    n.then_inc(*done("a_t", (tag, i)))

                def values(i):
                    causal = heads[i][3]
                    pe.wait_ge(*at("a_pt", (tag, i)))
                    if i >= 1:
                        pe.wait_ge(*at("a_o", (tag, i - 1)))
                    for t in range(NT):
                        nc_ = 1 if causal and t == 0 else 2
                        for c in range(nc_):
                            a = (i % 4) * P + t * DH
                            n = mm(PS[:, 7, a:a + DH], pt[i % 2][:, 2 * t + c, :], heads[i][2](c),
                                   start=c == 0, stop=c == nc_ - 1)
                    n.then_inc(*done("a_v", (tag, i)))

                n = len(heads)
                for i in range(n + 2):
                    if i < n:
                        scores(i)
                    if 1 <= i <= n:
                        turn(i - 1)
                    if i >= 2:
                        values(i - 2)
                    after(i)

            def operands(h, qT, kT, kk, v, causal):
                b = (h % 2) * DH
                return (lambda t: qT[b:b + DH, h // 2, t * P:(t + 1) * P], lambda nk: kT[b:b + DH, kk, 0:nk], v, causal)

            pe.wait_ge(*read(("nv", 1)))
            pe.wait_ge(*read(("nk", 1)))
            pe.wait_ge(*at("gn_c", 1))
            attention("na", [operands(h, nqT, nkT, h // 2, lambda c, h=h: nv[:, c, h * DH:(h + 1) * DH], False)
                             for h in range(NH)], lambda i: None)
            pe.wait_ge(*at("y0"))
            pe.wait_ge(*at("a_o", ("na", NH - 1)))
            to_T("y0", hn, KD, 0)
            out_proj("mo0", 4, lambda k: 8 + k, "y0")
            norm_T(1)
            ffn(0)
            norm_T(2)

            slot_tm(("dt", 0), 0, 0, True, True, 64, 8, fresh=("n", 2))

            def ssd_slot(g, j):
                if g == SG:
                    for j in (j, j + 1) if j == 4 else (j,):
                        ssd_out(j)
                elif j == 0:
                    if g >= 1:
                        pe.wait_ge(*at("c_cnv", (g - 1, 1)))
                    slot_fm((("bc", g), 0), 2)
                elif j == 1:
                    if g >= 1:
                        pe.wait_ge(*at("c_cnv", (g - 1, 0)))
                    slot_fm((("xs", g), 0), 3)
                elif j == 2:
                    pe.wait_ge(*at("c_cnv", (g, 2)))
                    slot_fm((("xs", g), 1), 2)
                elif j == 3:
                    pe.wait_ge(*(read((("z", g - 1), 1)) if g else at("sp_x", "ssd")))
                    slot_tm((("z", g), 0), 0, 0, True, False)
                else:
                    slot_tm((("z", g), 1), 0, 4, False, True)

            def ssd_out(j):
                if j == 0:
                    pe.wait_ge(*read((("z", SG - 1), 1)))
                    pe.wait_ge(*at("c_cnv", (SG - 1, 0)))
                    pe.wait_ge(*at("c_cnv", (SG - 1, 1)))
                kt = lambda k: (8 + 2 * j + k) % 16
                slot_dn(("mo1", j), lambda k, t: Th[:, kt(k), t * P:(t + 1) * P], lambda k, t: Tl[:, kt(k), t * P:(t + 1) * P],
                        j == 0, j == 7, 0)

            def ssd_turn(g):
                pe.wait_ge(*at("s_y", g))
                to_T(("y", g), hn[:, :, (g % 2) * 512:(g % 2) * 512 + 512], 4, 6)

            def ssd(g):
                fill = lambda j: ssd_slot(g + 1, j)
                pe.wait_ge(*at("cv", (g, 1)))
                if g == 0:
                    pe.wait_ge(*at("ex"))
                for t in range(NT):
                    for j in range(4):
                        i = tr(PS[:, 4 + t, j * P:(j + 1) * P], cvb[:, j, t * P:(t + 1) * P], ident)
                i.then_inc(*done("s_xt", g))
                if g:
                    pe.wait_ge(*at("s_add", g - 1))
                for c in range(NT):
                    tr(PS[:, 6, c * P:(c + 1) * P], bct[g % 2][:, 0, c * P:(c + 1) * P], ident)
                for c in range(NT):
                    i = mm(PS[:, 6, S + c * P:S + (c + 1) * P], bct[g % 2][:, 0, c * P:(c + 1) * P],
                           bct[g % 2][:, 1, c * P:(c + 1) * P], start=True, stop=True)
                i.then_inc(*done("s_bq", g))
                fill(0)
                pe.wait_ge(*at("s_v", g))
                for r in range(2):
                    i = mm(PS[:, 4 + r, :], btm[:, r, :], vt[:, r, :], start=True, stop=True)
                i.then_inc(*done("s_st", g))
                fill(1)
                pe.wait_ge(*at("s_ste", g))
                for r in range(2):
                    c = 1 - r
                    i = mm(PS[:, 4 + r, :], bct[g % 2][:, 1, c * P:(c + 1) * P], stt[:, r, :], start=True, stop=True)
                i.then_inc(*done("s_yi", g))
                if g:
                    ssd_turn(g - 1)
                fill(2)
                pe.wait_ge(*at("s_yie", g))
                if g:
                    pe.wait_ge(*at("T_lo", (("y", g - 1), 3)))

                def seg(u):
                    c, r, hf = u // 4, (u // 2) % 2, u % 2
                    pe.wait_ge(*at("s_am", (g, u)))
                    if u >= 2:
                        pe.wait_ge(*at("s_e", (g, u - 2)))
                    mm(PS[:, 4 + u % 2, :], cc("gt" if r == 0 else "lt"), am[u % 2][:, :, :],
                       start=True, stop=True).then_inc(*done("s_l", (g, u)))

                def diag(u):
                    c, r, hf = u // 4, (u // 2) % 2, u % 2
                    pe.wait_ge(*at("s_m", (g, u)))
                    for k in range(4):
                        h = 4 * hf + k
                        i = mm(PS[:, 7 - c, h * DH:(h + 1) * DH], ee[u % 2][:, k, :], vfb[:, r, c, h * DH:(h + 1) * DH],
                               start=u % 4 == 0 and k == 0, stop=False, skip_group_check=True)
                    i.then_inc(*done("s_pv", (g, u)))

                for u in range(9):
                    if u < 8:
                        seg(u)
                    if u >= 1:
                        diag(u - 1)
                    if u == 4:
                        fill(3)
                fill(4)

            for j in range(5):
                ssd_slot(0, j)
                if j == 2:
                    pe.wait_ge(*at("la"))
                    for k, (m, c, dr) in enumerate((("gt", 0, 0), ("lt", 1, 1), ("le", 1, 0), ("ge", 0, 1))):
                        i = mm(PS[:, 4, 32 * k:32 * k + 32], cc(m), dtt[:, 2 + c, 32 * dr:32 * dr + 32], start=True, stop=True)
                    i.then_inc(*done("cums"))
            for g in range(SG):
                ssd(g)
            pe.wait_ge(*at("s_add", SG - 1))
            ssd_turn(SG - 1)
            for j in (6, 7):
                pe.wait_ge(*at("T_lo", (("y", SG - 1), 2 * j - 11)))
                ssd_out(j)
            norm_T(3)
            ffn(1)

            norm_T(4)
            block_tm("qa", 0, ("n", 4))
            block_tm("ka", 2)

            def head_T(nm, a):
                pe.wait_ge(*read((nm, 1)))
                if a >= 2:
                    pe.wait_ge(*at("hT", (a - 2, 1)))
                to_T(nm, hn[:, :, 512 * (a % 2):512 * (a % 2) + 512], 4, 4 + 2 * (a % 2))

            pe.wait_ge(*read(("qa", 1)))
            block_tm("va", 0)
            head_T("qa", 0)
            head_T("ka", 1)
            block_tm("qb", 2)
            pe.wait_ge(*read(("va", 1)))
            slot_fm(("kc", 0), 0)
            slot_fm(("vc", 0), 1)
            head_T("qb", 2)
            block_tm("ksv", 2)
            pe.wait_ge(*read(("kc", 0)))
            pe.wait_ge(*read(("vc", 0)))
            slot_tm(("gb", 0), 0, 0, True, True, 24, 8)
            head_T("ksv", 3)
            pe.wait_ge(*read(("gb", 1)))
            block_tm("za", 0)
            block_tm("zb", 2)
            pe.wait_ge(*at("hT", (3, 1)))
            for a, nm in enumerate("kv"):
                pe.wait_ge(*at("x_lo", a))
                for j in range(2):
                    n = slot_no[("w1" + nm, j)]
                    pe.wait_ge(*low(n))
                    h, l = whi[n % NHI], wlo[n % NLO]
                    for m in range(2):
                        for k in range(8):
                            c, kk = k * 256 + m * P, 8 * j + k
                            xh = Th[:, 8 + 2 * a:10 + 2 * a, :].rearrange("p a (b c) -> p (a b) c", c=32)[:, kk, :]
                            xl = Tl[:, 8 + 2 * a:10 + 2 * a, :].rearrange("p a (b c) -> p (a b) c", c=32)[:, kk, :]
                            i = three(PS[:, 4 + 2 * a + m, 0:32], h[:, c:c + P], l[:, c:c + P], xh, xl,
                                      kk == 0, kk == 15, False)
                    i.then_inc(*done("w_used", n))
            pe.wait_ge(*at("c_gelu", 0))
            pe.wait_ge(*at("load_w2"))
            for m in range(2):
                i = mm(PS[0:32, 4, 64:64 + DH], hid[:, 0, m, :], w2c[:, 0, m, :], start=m == 0, stop=m == 1)
            i.then_inc(*done("c_k"))
            pe.wait_ge(*at("c_rep"))
            for m in range(2):
                i = mm(PS[:, 5, 64:64 + DH], hidr[:, m, :], w2c[:, 1, m, :], start=m == 0, stop=m == 1)
            i.then_inc(*done("c_v"))
            pe.wait_ge(*at("c_kn"))
            tr(PS[:, 6, 0:32], kcm[0:32, 0, :], ident[0:32, 0:32]).then_inc(*done("c_kt"))
            pe.wait_ge(*at("c_kte"))
            pe.wait_ge(*at("c_vbd"))
            for t in range(NT):
                for h in range(NH):
                    b = (h % 2) * DH
                    a = 64 * t + 16 * (h // 2)
                    i = mm(PS[:, 4 + h % 2, a:a + 16], qbT[b:b + DH, h // 2, t * P:(t + 1) * P],
                           kcT[b:b + DH, 16 * (h // 4):16 * (h // 4) + 16], start=True, stop=True)
            i.then_inc(*done("c_s"))
            pe.wait_ge(*at("c_p"))
            for t in range(NT):
                i = tr(PS[:, 5, t * P:(t + 1) * P], cpr[:, t, :], ident)
            i.then_inc(*done("c_pt"))
            pe.wait_ge(*at("c_pte"))
            for t in range(NT):
                i = mm(PS[:, 6 + t, :], cpt[:, t, :], vbd[:, :, :], start=True, stop=True)
            i.then_inc(*done("c_o"))
            pe.wait_ge(*at("c_oe"))

            def g_blocks(n):
                for a, nm in enumerate(("GA", "GB")):
                    if n == 0:
                        pe.wait_ge(*read((("za", "zb")[a], 1)))
                    else:
                        pe.wait_ge(*read(((nm, n - 1), 1)))
                    block_tm((nm, n), 2 * a)

            def y_blocks(n):
                for a, nm in enumerate(("YA", "YB")):
                    if n:
                        pe.wait_ge(*at("mrg_p", (n - 1, a)))
                    slot_tm(((nm, n), 0), 4 + 2 * a, 8 + 4 * a, True, True)

            pe.wait_ge(*read(("va", 1)))
            attention("moba", [operands(h, qaT, kaT, h // 2, lambda c, h=h: va[:, c, h * DH:(h + 1) * DH], True)
                               for h in range(NH)], lambda i: None)
            pe.wait_ge(*at("a_o", ("moba", NH - 1)))
            attention("nsa", [operands(h, qbT, kswT, 2 * w + h // 4,
                                       lambda c, h=h, w=w: vsw[:, c, w, DH * (h // 4):DH * (h // 4) + DH], True)
                              for w in range(2) for h in range(NH)], lambda i: None)
            g_blocks(0)
            pe.wait_ge(*at("y2"))
            to_T("y2", hn, KD, 4)
            pe.wait_ge(*at("T_lo", ("y2", KD - 1)))
            y_blocks(0)
            g_blocks(1)
            y_blocks(1)
            pe.wait_ge(*at("mrg", (1, 1)))
            to_T("mrg", hn, KD, 0)
            out_proj("fo", 4, lambda k: k, "mrg")

        @block.scalar
        def _(act):
            nxt = [0]

            def high(upto):
                while nxt[0] <= min(upto, NS - 1):
                    n = nxt[0]
                    parts, width = slots[n]
                    act.wait_ge(*at(f"w_raw{n % NRAW}", n))
                    if n >= NHI:
                        act.wait_ge(*at("w_used", n - NHI))
                    act.activation(whi[n % NHI][:, 0:width], raw[n % NRAW][:, 0:width], ACT.Copy)\
                        .then_inc(*done("w_hi", n))
                    nxt[0] += 1

            def used(name):
                n = slot_no[name]
                high(n + 2)
                act.wait_ge(*at("w_used", n))
                high(n + 3)

            def sqrt_of(key, o, i, width):
                act.activation(o, i, ACT.Sqrt, scale=1.0 / width, bias=eps[0:o.shape[0], 0:1]).then_inc(*done("root", key))

            def T_hi(name, nk, kt0, b0, gains):
                for k in range(nk):
                    if k % 2 == 0:
                        act.wait_ge(*at("turned", (name, k + 1)))
                    src = PS[:, b0 + k // 2, (k % 2) * S:(k % 2 + 1) * S]
                    g = gains(k)
                    act.activation(Th[:, kt0 + k, :], src, ACT.Identity, scale=1.0 if g is None else g)\
                        .then_inc(*done("T_hi", (name, k)))

            def norm(l, gain):
                for t in range(NT):
                    if l:
                        act.wait_ge(*at("x", (l - 1, t)))
                    else:
                        act.wait_ge(*at("eps"))
                        act.wait_ge(*at(f"load_x{t}"))
                    act.activation(hn[:, t, :], x[:, t, :], ACT.Square, accum_out=st[:, t:t + 1]).then_inc(*done("n_ss", (l, t)))
                    act.wait_ge(*at("n_ss", (l, t)))
                    sqrt_of(("n", l, t), st[:, 2 + t:3 + t], st[:, t:t + 1], D)
                if l == 0:
                    act.wait_ge(*at("mix0_T"))
                    act.activation(cols[:, col_at["mix0"]:col_at["mix0"] + 8], PS[:, 0, 0:8], ACT.Copy)\
                        .then_inc(*done("mix0_col"))
                    high(0)
                    act.wait_ge(*at("mix0_col"))
                T_hi(("n", l), KD, 0, 4, lambda k: col(gain, k))

            def post(l, last, b0=4):
                n = slot_no[last]
                high(n + 2)
                act.activation(st[:, 157:158], eps[:, 0:1], ACT.Sqrt)
                for t in range(NT):
                    act.wait_ge(*at(("sum_0", "w_used")[t], n))
                    for hf in range(2):
                        b = b0 + 2 * t + hf
                        if (t, hf) != (0, 0):
                            act.wait_ge(*at("p_ss", (l, (0, 0, 1)[2 * t + hf - 1], (0, 1, 0)[2 * t + hf - 1])))
                        c = 4 + 2 * t + hf
                        act.activation(sqj[:, :], PS[:, b, :], ACT.Square, accum_out=st[:, c:c + 1])\
                            .then_inc(*done("p_ss", (l, t, hf)))
                    act.wait_ge(*at("p_sum", (l, t)))
                    sqrt_of(("p", l, t), st[:, 10 + t:11 + t], st[:, 8 + t:9 + t], D)
                high(n + 3)

            def load_gpost(l):
                src = (I["norm_mix_post"], I["norm_ffn_post"])[l % 2][l // 2:l // 2 + 1, :]
                act.dma_start(gpost[:, :], src.to_broadcast([P, D])).then_inc(*done("load_gpost", l, 16))

            def ffn(l):
                for i in range(FI + 1):
                    if i < FI:
                        for q in range(4):
                            if q % 2 == 0:
                                used(("GV"[q // 2], l, i))
                            if q == 0 and i >= 2:
                                act.wait_ge(*at("f_prod", (l, i - 2)))
                            j = (0, 1, 22, 23)[q] + 2 * i
                            act.activation(fac[i % 2][:, q, :],
                                           PS[:, 2 * (i % 2) + q // 2, (q % 2) * S:(q % 2 + 1) * S], ACT.Identity,
                                           scale=col(f"fw{l}1", j), bias=col(f"fb{l}", j)).then_inc(*done("f_ctr", (l, i, q)))
                        act.wait_ge(*at("f_cg", (l, i)))
                        act.activation(fac[i % 2][:, 0:2, :], fac[i % 2][:, 0:2, :], ACT.Gelu_apprx_tanh)\
                            .then_inc(*done("f_gelu", (l, i)))
                        if i >= 2:
                            act.wait_ge(*at("w_used", slot_no[("D", l, i - 2)]))
                        act.wait_ge(*at("f_prod", (l, i)))
                        act.activation(aTh[:, i % 2, :, :], fpr[i % 2][:, :, :], ACT.Copy).then_inc(*done("f_ahi", (l, i)))
                        high(slot_no[("V", l, i)] + 3)

            act.dma_start(cst[:, 0:P], I["const_table"][:, 0:P]).then_inc(*done("load_ident", 0, 16))
            act.dma_start(rowm, I["norm_mix_pre"][0].rearrange("(k p) -> k p", p=P)).then_inc(*done("load_mix0", 0, 16))
            def set_up():
                act.wait_ge(*at("set_up"))
                for b in range((NR + 3) // 4):
                    n = min(4, NR - 4 * b) * P
                    i = act.activation(cols[:, 512 * b:512 * b + n], PS[:, 4 + b, 0:n], ACT.Copy)
                i.then_inc(*done("cols_act"))
                act.wait_ge(*at("t5_sum"))
                act.dma_start(toe, bc(t5r, 1, P)).then_inc(*done("t5_out", 0, 16))
                act.dma_start(pfb[:, :, :], I["const_pfb"].rearrange("p (a b) -> p a b", a=2)).then_inc(*done("load_pfb", 0, 16))

            def softplus(key, neg, n):
                spx = spxs[key]
                act.wait_ge(*at("sp_x", key))
                act.activation(spx[:, 1, 0:n], spx[:, 0, 0:n], ACT.Abs).then_inc(*done("sp_abs", key))
                act.wait_ge(*at("sp_abs", key))
                act.activation(spx[:, 2, 0:n], spx[:, 1, 0:n], ACT.Exp, scale=-1.0).then_inc(*done("sp_exp", key))
                act.wait_ge(*at("sp_u", key))
                act.activation(spx[:, 4, 0:n], spx[:, 3, 0:n], ACT.Ln).then_inc(*done("sp_ln", key))

            norm(0, "mix0")
            high(3)
            load_gpost(0)
            high(slot_no[("rk", 0)] + 1)
            set_up()
            softplus("ret", True, 16)

            def copy_block(nm, dst, b0, scale=1.0, func=ACT.Copy):
                for t in range(NT):
                    if func == ACT.Copy:
                        i = act.activation(dst[:, t, :], PS[:, b0 + t, :], func, scale=scale)
                    else:
                        i = act.activation(dst[:, t, :], PS[:, b0 + t, :], func)
                    i.then_inc(*done("read_a", (nm, t)))

            def copy_fm(nm, dst, b0, scale=1.0):
                for j in range(2):
                    used((nm, j))
                    act.activation(dst[:, 2 * j:2 * j + 2, :], PS[:, b0 + j, :].rearrange("p (a b) -> p a b", a=2),
                                   ACT.Copy, scale=scale).then_inc(*done("read_a", (nm, j)))

            used(("rk", 1))
            high(slot_no[("rv", 0)] + 2)
            used(("rv", 1))
            copy_block("rv", rv, 0)
            for a, nm in enumerate(("rq", "rk")):
                for j in range(2):
                    act.wait_ge(*at("turned", (nm, 2 * j + 1)))
                    act.activation((rqT, rkT)[a][:, 2 * j:2 * j + 2, :],
                                   PS[:, 4 + 2 * a + j, :].rearrange("p (a b) -> p a b", a=2),
                                   ACT.Copy, scale=(1.0, DH ** -0.5)[a]).then_inc(*done("rT", (nm, j)))
            act.wait_ge(*at("na_rows"))
            act.wait_ge(*at("t5_out"))
            for h in range(NH):
                for q in range(2):
                    src = bass.AP(narep.tensor, h * GW * 465 + (5 - q) * 31 + 15, [[464, GW], [31, 6], [1, GW]])
                    act.dma_start(nabias[q * GW:(q + 1) * GW, h, :].rearrange("p (a b) -> p a b", a=6), src)\
                        .then_inc(*done("load_na", 0, 16))
            copy_fm("nq", nqT, 2, DH ** -0.5)
            for h in range(NH):
                act.wait_ge(*at("r_arg", h))
                act.activation(dcy[h % 2], dcy[h % 2], ACT.Exp).then_inc(*done("r_d", h))
                if h == 4:
                    copy_fm("nk", nkT, 0)
            used(("nv", 1))
            copy_block("nv", nv, 2)
            for t in range(NT):
                act.wait_ge(*at("gn_c", t))
                act.activation(A[:, 11264 + 512 * t:11776 + 512 * t], hn[:, t, 0:512], ACT.Square).then_inc(*done("gn_sq", t))
            act.wait_ge(*at("gn_ss"))
            sqrt_of("gn", st[:, 48:64], st[:, 32:48], DH)
            used(("rg", 1))
            copy_block("rg", rg, 0, func=ACT.Silu)

            def attention(tag, n, causal):
                for i in range(n + 1):
                    if i < n:
                        act.wait_ge(*at("a_nm", (tag, i)))
                        for t in range(NT):
                            nk = P if causal and t == 0 else S
                            e = act.activation(sc[i % 2][:, t, 0:nk], sc[i % 2][:, t, 0:nk], ACT.Exp,
                                               bias=st[:, 72 + 2 * (i % 4) + t:73 + 2 * (i % 4) + t],
                                               accum_out=st[:, 80 + 2 * (i % 4) + t:81 + 2 * (i % 4) + t])
                        e.then_inc(*done("a_exp", (tag, i)))
                    if i >= 1:
                        j = i - 1
                        act.wait_ge(*at("a_t", (tag, j)))
                        if j >= 2:
                            act.wait_ge(*at("a_v", (tag, j - 2)))
                        if causal:
                            act.activation(pt[j % 2][:, 0, :], PS[:, 6, 0:P], ACT.Copy)
                            e = act.activation(pt[j % 2][:, 2:4, :], PS[:, 6, S:2 * S].rearrange("p (a b) -> p a b", a=2), ACT.Copy)
                        else:
                            e = act.activation(pt[j % 2][:, :, :], PS[:, 6, :].rearrange("p (a b) -> p a b", a=4), ACT.Copy)
                        e.then_inc(*done("a_pt", (tag, j)))

            high(slot_no[("rg", 1)] + 3)
            attention("na", NH, False)
            T_hi("y0", KD, 8, 0, lambda k: col("gn", k) if k < 4 else None)
            post(0, ("mo0", 3))
            norm(1, "ffn0")
            load_gpost(1)
            ffn(0)
            post(1, ("D", 0, FI - 1))
            norm(2, "mix1")
            load_gpost(2)
            for r, (nm, w) in enumerate((("c_dt_bias", 64), ("c_a_log", 64))):
                act.dma_start(dtt[:, 4 + r, 0:w], I[nm].rearrange("a b c -> a (b c)").to_broadcast([P, w]))\
                    .then_inc(*done("load_ssd", 0, 16))
            act.dma_start(dtt[:, 6, 0:32], I["c_d_skip"].to_broadcast([P, 32])).then_inc(*done("load_ssd", 0, 16))
            def ssd_centre(g, j):
                used(((("xs", g), j) if j < 2 else (("bc", g), 0)))
                for m in range(2):
                    ch = 4 * g + 2 * j + m if j < 2 else 16 + 4 * m + g
                    act.activation(cvb[:, 2 * j + m, :], PS[:, (3, 2, 2)[j], m * S:(m + 1) * S], ACT.Identity,
                                   scale=col("cw2", ch), bias=col("cb", ch)).then_inc(*done("c_ctr", (g, 2 * j + m)))

            def ssd_silu(g):
                for j in (2, 0, 1):
                    act.wait_ge(*at("c_cnv", (g, j)))
                    act.activation(cvb[:, 2 * j:2 * j + 2, :] if j < 2 else bct[g % 2][:, :, :], cvb[:, 2 * j:2 * j + 2, :],
                                   ACT.Silu).then_inc(*done("cv", (g, j)))

            def ssd(g):
                more = g + 1 < SG
                b = slot_no[(("bc", g + 1), 0)] if more else slot_no[("mo1", 0)]
                act.wait_ge(*at("s_xt", g))
                for t in range(NT):
                    i = act.activation(xs[g % 2][:, t, :], PS[:, 4 + t, :], ACT.Copy)
                i.then_inc(*done("s_xs", g))
                used((("z", g), 1))
                if g >= 2:
                    act.wait_ge(*at("s_ss", g - 2))
                copy_block(("z", g), zt[g % 2], 0, func=ACT.Silu)
                high(b + 1)
                if g:
                    act.wait_ge(*at("s_ss", g - 1))
                    sqrt_of(("s", g - 1), st[:, 98:100], st[:, 96:98], 512)
                act.wait_ge(*at("s_st", g))
                for r in range(2):
                    i = act.activation(stt[:, r, :], PS[:, 4 + r, :], ACT.Copy)
                i.then_inc(*done("s_ste", g))
                high(b + 2)
                if more:
                    ssd_centre(g + 1, 2)
                high(b + 3)
                if g:
                    T_hi(("y", g - 1), 4, (4 + 4 * g) % 16, 6, lambda k: col("ssdn", 4 * g - 4 + k))
                if more:
                    ssd_centre(g + 1, 0)
                high(b + 4)
                for u in range(8):
                    act.wait_ge(*at("s_l", (g, u)))
                    if u >= 2:
                        act.wait_ge(*at("s_pv", (g, u - 2)))
                    act.activation(ee[u % 2][:, :, :], PS[:, 4 + u % 2, :].rearrange("p (a b) -> p a b", a=4), ACT.Exp)\
                        .then_inc(*done("s_e", (g, u)))
                    if u == 1:
                        if more:
                            ssd_centre(g + 1, 1)
                        high(b + 5)
                    if u == 5:
                        high(b + 6)
                if more:
                    ssd_silu(g + 1)

            for j in (2, 0, 1):
                ssd_centre(0, j)
                if j == 0:
                    softplus("ssd", False, 128)
                    act.wait_ge(*at("load_ssd"))
                    act.activation(dtt[:, 5, :], dtt[:, 5, :], ACT.Exp).then_inc(*done("ssd_a"))
            act.wait_ge(*at("cums"))
            act.activation(dtt[:, 8:10, :], PS[:, 4, 0:128].rearrange("p (a b) -> p a b", a=2), ACT.Exp).then_inc(*done("ex"))
            ssd_silu(0)
            for g in range(SG):
                ssd(g)
            high(slot_no[("mo1", 7)])
            act.wait_ge(*at("s_ss", SG - 1))
            sqrt_of(("s", SG - 1), st[:, 98:100], st[:, 96:98], 512)
            T_hi(("y", SG - 1), 4, (4 + 4 * SG) % 16, 6, lambda k: col("ssdn", 4 * SG - 4 + k))
            post(2, ("mo1", 7), 0)
            norm(3, "ffn1")
            load_gpost(3)
            ffn(1)
            post(3, ("D", 1, FI - 1))
            norm(4, "sec")

            def load_tb(k):
                for h in range(NH):
                    src = bass.AP(toe.tensor, (NH * k + h) * P * 384 + 127, [[383, P], [1, S]])
                    act.dma_start(tb[:, h, :], src).then_inc(*done("load_tb", k, 16))

            load_tb(0)
            for a, nm in enumerate("kv"):
                act.dma_start(w2c[:, a, :, :], I["cmp_w2_" + nm + "_2"][0].rearrange("(m p) d -> p m d", p=P))\
                    .then_inc(*done("load_w2", 0, 16))

            def head_norm(nm, b0):
                used((nm, 1))
                for t in range(NT):
                    if t == 0 and nm != "qa":
                        act.wait_ge(*at("q_ss", {"ka": "qa", "qb": "ka", "ksv": "qb"}[nm]))
                    act.activation(sqb[:, t, :], PS[:, b0 + t, :], ACT.Square).then_inc(*done("q_sq", (nm, t)))
                if nm == "ksv":
                    for t in range(NT):
                        v = PS[:, b0 + t, :].rearrange("p (w c d) -> p w c d", w=2, c=2)[:, :, 1, :]
                        act.activation(vsw[:, t, :, :], v, ACT.Copy).then_inc(*done("vsw", t))
                act.wait_ge(*at("q_ss", nm))
                sqrt_of(("q", nm), st[:, 120:136], st[:, 104:120], DH)

            def head_T(nm, a, dst, gains):
                for j in range(2):
                    act.wait_ge(*at("turned", (nm, 2 * j + 1)))
                    act.activation(dst[:, 2 * j:2 * j + 2, :], PS[:, 4 + 2 * (a % 2) + j, :].rearrange("p (a b) -> p a b", a=2),
                                   ACT.Identity, scale=cols[:, gains[j]:gains[j] + 1]).then_inc(*done("hT", (a, j)))

            head_norm("qa", 0)
            head_norm("ka", 2)
            used(("va", 1))
            copy_block("va", va, 0)
            head_T("qa", 0, qaT, (qn + 6, qn + 6))
            head_T("ka", 1, kaT, (qn + 1, qn + 1))
            head_norm("qb", 2)
            used(("vc", 0))
            head_T("qb", 2, qbT, (qn + 7, qn + 7))
            for a in range(2):
                act.wait_ge(*read((("kc", "vc")[a], 0)))
                act.activation(Th[:, 8 + 2 * a:10 + 2 * a, :].rearrange("p a (b c) -> p (a b) c", c=32), XC[a][:, :, :],
                               ACT.Copy).then_inc(*done("x_hi", a))
            head_norm("ksv", 2)
            used(("gb", 0))
            for t in range(NT):
                act.activation(gb[:, t, :], PS[:, t, 0:24], ACT.Sigmoid).then_inc(*done("read_a", ("gb", t)))
            head_T("ksv", 3, kswT, (qn + 3, qn + 4))
            used(("za", 1))
            copy_block("za", za, 0, func=ACT.Silu)
            used(("zb", 1))
            copy_block("zb", zb, 2, func=ACT.Silu)
            for a, nm in enumerate("kv"):
                used(("w1" + nm, 1))
                act.activation(hid[:, a, :, :], PS[:, 4 + 2 * a:6 + 2 * a, 0:32], ACT.Gelu_apprx_tanh).then_inc(*done("c_gelu", a))
            act.wait_ge(*at("c_k"))
            act.activation(kcm[0:32, 1, 0:DH], PS[0:32, 4, 64:64 + DH], ACT.Square, accum_out=st[0:32, 12:13])\
                .then_inc(*done("c_kss"))
            act.wait_ge(*at("c_kss"))
            sqrt_of("ck", st[0:32, 13:14], st[0:32, 12:13], DH)
            act.wait_ge(*at("c_kt"))
            act.activation(kcT, PS[:, 6, 0:32], ACT.Identity, scale=cols[:, qn + 5:qn + 6]).then_inc(*done("c_kte"))
            act.wait_ge(*at("c_sub"))
            act.activation(cpr[:, :, :], cpr[:, :, :], ACT.Exp).then_inc(*done("c_exp"))
            act.wait_ge(*at("c_pt"))
            act.activation(cpt[:, :, :], PS[:, 5, 0:S].rearrange("p (a b) -> p a b", a=2), ACT.Copy).then_inc(*done("c_pte"))
            high(slot_no[("w1v", 1)] + 3)
            attention("moba", NH, True)
            act.wait_ge(*at("a_sc", ("moba", NH - 1)))
            load_tb(1)
            attention("nsa", 2 * NH, True)

            def g_evac(n):
                for a, nm in enumerate(("GA", "GB")):
                    used(((nm, n), 1))
                    if n:
                        act.wait_ge(*(at("mrg_p", (n - 1, 0)) if a == 0 else at("mrg", (n - 1, 1))))
                    copy_block((nm, n), sg[a], 2 * a, func=ACT.Sigmoid)

            g_evac(0)
            T_hi("y2", KD, 8, 4, lambda k: None)
            high(slot_no[(("YB", 0), 0)] + 2)
            g_evac(1)
            high(slot_no[(("YB", 1), 0)] + 2)
            T_hi("mrg", KD, 0, 0, lambda k: None)
            used(("fo", 3))

        @block.vector
        def _(dve):
            tt, ts, stt3 = nc.vector.tensor_tensor, nc.vector.tensor_scalar, nc.vector.scalar_tensor_tensor
            lk = lambda ins: link(dve, "dve", ins)

            def T_lo(name, nk, kt0, b0, gains):
                for k in range(nk):
                    if k % 2 == 0:
                        dve.wait_ge(*at("T_hi", (name, k + 1)))
                    src = PS[:, b0 + k // 2, (k % 2) * S:(k % 2 + 1) * S]
                    g = gains(k)
                    stt3(out=Tl[:, kt0 + k, :], in0=src, scalar=1.0 if g is None else g,
                         in1=Th[:, kt0 + k, :].bitcast(F32), op0=ALU.mult, op1=ALU.subtract)\
                        .then_inc(*done("T_lo", (name, k)))

            def norm(l, gain):
                for t in range(NT):
                    dve.wait_ge(*at("root", ("n", l, t)))
                    lk(nc.vector.reciprocal(st[:, t:t + 1], st[:, 2 + t:3 + t]))
                    ts(hn[:, t, :], x[:, t, :], st[:, t:t + 1], None, ALU.mult).then_inc(*done("n_hn", (l, t)))
                T_lo(("n", l), KD, 0, 4, lambda k: col(gain, k))

            def post(l, last, b0=4):
                dve.wait_ge(*at("load_gpost", l))
                for t in range(NT):
                    b, c, m = b0 + 2 * t, 4 + 2 * t, hn[:, t, :]
                    dve.wait_ge(*at("p_ss", (l, t, 0)))
                    tt(m[:, 0:512], PS[:, b, :], gpost[:, 0:512], ALU.mult)
                    dve.wait_ge(*at("p_ss", (l, t, 1)))
                    tt(st[:, 8 + t:9 + t], st[:, c:c + 1], st[:, c + 1:c + 2], ALU.add).then_inc(*done("p_sum", (l, t)))
                    lk(tt(m[:, 512:D], PS[:, b + 1, :], gpost[:, 512:D], ALU.mult))
                    dve.wait_ge(*at("root", ("p", l, t)))
                    lk(nc.vector.reciprocal(st[:, 14 + t:15 + t], st[:, 10 + t:11 + t]))
                    stt3(out=x[:, t, :], in0=m, scalar=st[:, 14 + t:15 + t], in1=x[:, t, :], op0=ALU.mult, op1=ALU.add)\
                        .then_inc(*done("x", (l, t)))

            def taps(dst, src, ws, shift):
                n = S - abs(shift)
                a, b = (-shift, 0) if shift < 0 else (0, shift)
                return stt3(out=dst[:, a:a + n], in0=src[:, b:b + n], scalar=ws, in1=dst[:, a:a + n], op0=ALU.mult, op1=ALU.add)

            def ffn(l):
                for i in range(FI):
                    p = i % 2
                    bank = lambda q: PS[:, 2 * p + q // 2, (q % 2) * S:(q % 2 + 1) * S]
                    j = lambda q: (0, 1, 22, 23)[q] + 2 * i
                    for hv in range(2):
                        dve.wait_ge(*at("f_ctr", (l, i, 2 * hv + 1)))
                        for q in (2 * hv, 2 * hv + 1):
                            o = taps(fac[p][:, q, :], bank(q), col(f"fw{l}0", j(q)), -1)
                        lk(o)
                        for q in (2 * hv, 2 * hv + 1):
                            o = taps(fac[p][:, q, :], bank(q), col(f"fw{l}2", j(q)), 1)
                        o.then_inc(*done(("f_cg", "f_conv")[hv], (l, i)))
                    dve.wait_ge(*at("f_gelu", (l, i)))
                    dve.wait_ge(*at("f_conv", (l, i)))
                    if i >= 2:
                        dve.wait_ge(*at("f_ahi", (l, i - 2)))
                    tt(fpr[p][:, :, :], fac[p][:, 0:2, :], fac[p][:, 2:4, :], ALU.mult).then_inc(*done("f_prod", (l, i)))
                    dve.wait_ge(*at("f_ahi", (l, i)))
                    if i >= 2:
                        dve.wait_ge(*at("w_used", slot_no[("D", l, i - 2)]))
                    tt(aTl[:, p, :, :], fpr[p][:, :, :], aTh[:, p, :, :].bitcast(F32), ALU.subtract).then_inc(*done("f_alo", (l, i)))
                    n = slot_no[("D", l, i)]
                    dve.wait_ge(*at("w_hi", n))
                    dve.wait_ge(*at("w_used", n - NLO))
                    tt(wlo[n % NLO][:, :], raw[n % NRAW][:, :], whi[n % NHI][:, :].bitcast(F32), ALU.subtract)\
                        .then_inc(*done("w_lo_v", n))

            def softplus(key, n, dst):
                w = lambda k: spxs[key][:, k, 0:n]
                dve.wait_ge(*at("sp_exp", key))
                ts(w(3), w(2), 1.0, None, ALU.add).then_inc(*done("sp_u", key))
                dve.wait_ge(*at("sp_u", key))
                lk(ts(w(5), w(3), -1.0, None, ALU.add))
                lk(ts(w(6), w(5), 0.0, None, ALU.is_equal))
                lk(tt(w(5), w(5), w(6), ALU.add))
                lk(nc.vector.reciprocal(w(7), w(5)))
                dve.wait_ge(*at("sp_ln", key))
                lk(tt(w(7), w(7), w(4), ALU.mult))
                lk(tt(w(7), w(7), w(6), ALU.add))
                lk(tt(w(7), w(7), w(2), ALU.mult))
                lk(stt3(out=dst, in0=w(0), scalar=0.0, in1=w(7), op0=ALU.max, op1=ALU.add))

            nc.vector.memset(st[:, :], 0.0)
            nc.vector.memset(eps[:, :], EPS).then_inc(*done("eps"))
            nc.vector.memset(rowb[:, :, :], 0.0).then_inc(*done("rows_clear"))
            dve.wait_ge(*at("eps"))
            for t in range(NT):
                dve.wait_ge(*at(f"load_x{t}"))
            norm(0, "mix0")
            dve.wait_ge(*at("set_up"))
            lk(nc.vector.tensor_copy(cols[:, qn:qn + 6], PS[:, 6, 0:6]))
            tt(t5r, PS[0:16, 7, 0:384], negs, ALU.add).then_inc(*done("t5_sum"))
            ts(cols[:, qn + 6:qn + 8], cols[:, qn:qn + 3:2], DH ** -0.5, None, ALU.mult).then_inc(*done("cols"))
            dve.wait_ge(*at("load_dl"))
            ts(spxs["ret"][:, 0, 0:16], brow, -1.0, None, ALU.mult).then_inc(*done("sp_x", "ret"))
            dve.wait_ge(*at("sp_x", "ret"))
            softplus("ret", 16, lg)
            lk(ts(lg, lg, -1.0, None, ALU.mult))

            def rope(nm, a, b0):
                dve.wait_ge(*at("w_used", slot_no[(nm, 1)]))
                for t in range(NT):
                    src = PS[:, b0 + t, :]
                    o, tmp = rqk[a][:, t, :], hn[:, t, 512 * a:512 * a + 512]
                    h3 = lambda v: v.rearrange("p (h d) -> p h d", h=NH)
                    cosb = bc(cc("cos")[:, DH * t:DH * (t + 1)], 1, NH)
                    tt(h3(o), h3(src), cosb, ALU.mult)
                    for hf in range(2):
                        sn = bc(cc("sin")[:, DH * t + 32 * hf:DH * t + 32 * hf + 32], 1, NH)
                        i = tt(h3(tmp)[:, :, 32 * hf:32 * hf + 32], h3(src)[:, :, 32 * (1 - hf):32 * (1 - hf) + 32], sn, ALU.mult)
                    i.then_inc(*done("read_v", (nm, t)))
                    dve.wait_ge(*read((nm, t)))
                    tt(o, o, tmp, ALU.add).then_inc(*done("rope", (nm, t)))

            dve.wait_ge(*at("load_cst"))
            rope("rq", 0, 0)
            rope("rk", 1, 2)
            dve.wait_ge(*at("load_pfb"))

            def decay(h):
                if h >= 2:
                    dve.wait_ge(*at("r_m", h - 2))
                lk(ts(dcy[h % 2], pfb[:, 1, :], lg[:, 8 + h:9 + h], None, ALU.mult))
                stt3(out=dcy[h % 2], in0=pfb[:, 0, :], scalar=lg[:, h:h + 1], in1=dcy[h % 2], op0=ALU.mult, op1=ALU.add)\
                    .then_inc(*done("r_arg", h))

            decay(0)
            decay(1)
            for h in range(NH):
                dve.wait_ge(*at("r_s", h))
                dve.wait_ge(*at("r_d", h))
                if h >= 2:
                    dve.wait_ge(*at("r_pv", h - 2))
                tt(msc[h % 2], PS[:, 4 + h % 2, :], dcy[h % 2], ALU.mult).then_inc(*done("r_m", h))
                if h + 2 < NH:
                    decay(h + 2)
            dve.wait_ge(*at("r_pv", NH - 1))
            h3 = lambda v: v.rearrange("p (h d) -> p h d", h=NH)
            for t in range(NT):
                i = nc.vector.tensor_reduce(st[:, 16 + 8 * t:24 + 8 * t], h3(PS[:, 6 + t, :]), AXX, ALU.add)
            lk(i)
            for t in range(NT):
                stt3(out=h3(hn[:, t, 0:512]), in0=bc(st[:, 16 + 8 * t:24 + 8 * t], 2, DH), scalar=-1.0 / DH,
                     in1=h3(PS[:, 6 + t, :]), op0=ALU.mult, op1=ALU.add).then_inc(*done("gn_c", t))
            for t in range(NT):
                dve.wait_ge(*at("gn_sq", t))
                i = nc.vector.tensor_reduce(st[:, 32 + 8 * t:40 + 8 * t], h3(A[:, 11264 + 512 * t:11776 + 512 * t]), AXX, ALU.add)
            i.then_inc(*done("gn_ss"))
            dve.wait_ge(*at("root", "gn"))
            lk(nc.vector.reciprocal(st[:, 32:48], st[:, 48:64]))
            for t in range(NT):
                i = tt(h3(hn[:, t, 0:512]), h3(hn[:, t, 0:512]), bc(st[:, 32 + 8 * t:40 + 8 * t], 2, DH), ALU.mult)
            lk(i)
            dve.wait_ge(*read(("rg", 1)))
            for t in range(NT):
                i = tt(hn[:, t, 0:512], hn[:, t, 0:512], rg[:, t, :], ALU.mult)
            i.then_inc(*done("y0"))
            dve.wait_ge(*at("load_na"))
            for h in range(NH):
                v = nabias[:, h, :].rearrange("p (a b) -> p a b", a=6)
                i = tt(v, v, bc(cc("nm"), 1, 6), ALU.add)
            lk(i)

            def attention(tag, n, bias, causal, write):
                def finish(j):
                    dve.wait_ge(*at("a_v", (tag, j)))
                    s = 80 + 2 * (j % 4)
                    lk(nc.vector.reciprocal(st[:, s + 8:s + 10], st[:, s:s + 2]))
                    write(j, st[:, s + 8:s + 10], PS[:, 7, (j % 4) * P:(j % 4 + 1) * P].rearrange("p (t d) -> p t d", t=NT))\
                        .then_inc(*done("a_o", (tag, j)))

                for i in range(n + 2):
                    if i < n:
                        dve.wait_ge(*at("a_s", (tag, i)))
                        if i >= 2:
                            dve.wait_ge(*at("a_t", (tag, i - 2)))
                        for t in range(NT):
                            nk = P if causal and t == 0 else S
                            o = nc.vector.tensor_tensor_reduce(
                                out=sc[i % 2][:, t, 0:nk], in0=PS[:, 4 + i % 2, t * S:t * S + nk], in1=bias(i, t),
                                scale=1.0, scalar=-3e38, op0=ALU.add, op1=ALU.max,
                                accum_out=st[:, 64 + 2 * (i % 4) + t:65 + 2 * (i % 4) + t])
                        o.then_inc(*done("a_sc", (tag, i)))
                        dve.wait_ge(*at("a_sc", (tag, i)))
                        ts(st[:, 72 + 2 * (i % 4):74 + 2 * (i % 4)], st[:, 64 + 2 * (i % 4):66 + 2 * (i % 4)], -1.0, None,
                           ALU.mult).then_inc(*done("a_nm", (tag, i)))
                    if i >= 2:
                        finish(i - 2)

            def na_write(j, rc, o):
                return tt(hn[:, :, 512 + DH * j:512 + DH * (j + 1)], o, bc(rc, 2, DH), ALU.mult)

            attention("na", NH, lambda i, t: nabias[:, i, 128 - 128 * t:384 - 128 * t], False, na_write)
            T_lo("y0", KD, 8, 0, lambda k: col("gn", k) if k < 4 else None)
            post(0, ("mo0", 3))
            norm(1, "ffn0")
            ffn(0)
            post(1, ("D", 0, FI - 1))
            norm(2, "mix1")

            dve.wait_ge(*at("load_ssd"))
            dve.wait_ge(*at("w_used", slot_no[("dt", 0)]))
            for t in range(NT):
                i = tt(spxs["ssd"][:, 0, 64 * t:64 * t + 64], PS[:, t, 0:64], dtt[:, 4, :], ALU.add)
            i.then_inc(*done("sp_x", "ssd"))

            def ssd_conv(g, j):
                b = (3, 2, 2)[j]
                ch = lambda m: 4 * g + 2 * j + m if j < 2 else 16 + 4 * m + g
                dve.wait_ge(*at("c_ctr", (g, 2 * j + 1)))
                for k in (0, 1, 3, 4):
                    for m in range(2):
                        i = taps(cvb[:, 2 * j + m, :], PS[:, b, m * S:(m + 1) * S], col(f"cw{k}", ch(m)), k - 2)
                    if k < 4:
                        lk(i)
                i.then_inc(*done("c_cnv", (g, j)))

            def hb(v, n=8):
                return v.rearrange("p (h d) -> p h d", h=n)

            def decay_rows(g, u):
                c, r, hf = u // 4, (u // 2) % 2, u % 2
                if u >= 2:
                    dve.wait_ge(*at("s_l", (g, u - 2)))
                a0 = 32 * r + 8 * g + 4 * hf
                tt(am[u % 2][:, :, :], bc(cc("le" if r == 0 else "ge"), 1, 4), bc(dtt[:, 2 + c, a0:a0 + 4], 2, P), ALU.mult)\
                    .then_inc(*done("s_am", (g, u)))

            exv = dtt[:, 8:10, :].rearrange("p a b -> p (a b)")

            def ssd_scale(g):
                y = hn[:, :, (g % 2) * 512:(g % 2) * 512 + 512]
                dve.wait_ge(*at("root", ("s", g)))
                lk(nc.vector.reciprocal(st[:, 100:102], st[:, 98:100]))
                for c in range(NT):
                    i = ts(y[:, c, :], y[:, c, :], st[:, 100 + c:101 + c], None, ALU.mult)
                i.then_inc(*done("s_y", g))

            def ssd(g):
                more = g + 1 < SG
                X = xs[g % 2]
                y = hn[:, :, (g % 2) * 512:(g % 2) * 512 + 512]
                dve.wait_ge(*at("s_bq", g))
                nc.vector.tensor_copy(btm[:, :, :], PS[:, 6, 0:S].rearrange("p (a b) -> p a b", a=2))
                pq = PS[:, 6, S:2 * S].rearrange("p (a b) -> p a b", a=2)
                tt(qk[:, 0, :, :], pq, bc(cc("le"), 1, 2), ALU.mult)
                lk(tt(qk[:, 1, :, :], pq, bc(cc("gt"), 1, 2), ALU.mult))
                if g == 0:
                    dve.wait_ge(*at("ex"))
                dve.wait_ge(*at("s_xs", g))
                for r in range(2):
                    for t in range(NT):
                        i = tt(hb(vfb[:, r, t, :]), hb(X[:, t, :]),
                               bc(dtt[:, t, 32 * r + 8 * g:32 * r + 8 * g + 8], 2, DH), ALU.mult)
                lk(i)
                for r in range(2):
                    i = tt(hb(vt[:, r, :]), hb(vfb[:, r, r, :]), bc(exv[:, 32 * r + 8 * g:32 * r + 8 * g + 8], 2, DH), ALU.mult)
                i.then_inc(*done("s_v", g))
                if g:
                    ssd_scale(g - 1)
                if more:
                    ssd_conv(g + 1, 2)
                if g >= 2:
                    dve.wait_ge(*at("turned", (("y", g - 2), 3)))
                dve.wait_ge(*at("s_yi", g))
                for r in range(2):
                    i = tt(hb(y[:, 1 - r, :]), hb(PS[:, 4 + r, :]),
                           bc(exv[:, 64 + 32 * r + 8 * g:64 + 32 * r + 8 * g + 8], 2, DH), ALU.mult)
                i.then_inc(*done("s_yie", g))
                decay_rows(g, 0)
                decay_rows(g, 1)
                if g:
                    T_lo(("y", g - 1), 4, (4 + 4 * g) % 16, 6, lambda k: col("ssdn", 4 * g - 4 + k))
                if more:
                    ssd_conv(g + 1, 0)
                for u in range(8):
                    c, r, hf = u // 4, (u // 2) % 2, u % 2
                    dve.wait_ge(*at("s_e", (g, u)))
                    tt(ee[u % 2][:, :, :], ee[u % 2][:, :, :], bc(qk[:, r, c, :], 1, 4), ALU.mult).then_inc(*done("s_m", (g, u)))
                    if u + 2 < 8:
                        decay_rows(g, u + 2)
                    if u == 4 and more:
                        ssd_conv(g + 1, 1)
                dve.wait_ge(*at("s_pv", (g, 7)))
                dve.wait_ge(*at("s_yie", g))
                for c in range(NT):
                    i = tt(y[:, c, :], y[:, c, :], PS[:, 7 - c, :], ALU.add)
                i.then_inc(*done("s_add", g))
                for c in range(NT):
                    i = tt(hb(X[:, c, :]), hb(X[:, c, :]), bc(dtt[:, 6, 8 * g:8 * g + 8], 2, DH), ALU.mult)
                lk(i)
                dve.wait_ge(*at("s_add", g))
                for c in range(NT):
                    i = tt(y[:, c, :], y[:, c, :], X[:, c, :], ALU.add)
                lk(i)
                dve.wait_ge(*read((("z", g), 1)))
                for c in range(NT):
                    i = tt(y[:, c, :], y[:, c, :], zt[g % 2][:, c, :], ALU.mult)
                lk(i)
                for c in range(NT):
                    i = nc.vector.tensor_tensor_reduce(out=X[:, c, :], in0=y[:, c, :], in1=y[:, c, :], scale=1.0, scalar=0.0,
                                                       op0=ALU.mult, op1=ALU.add, accum_out=st[:, 96 + c:97 + c])
                i.then_inc(*done("s_ss", g))

            ssd_conv(0, 2)
            softplus("ssd", 128, dtt[:, 0:2, :].rearrange("p a b -> p (a b)"))
            dve.wait_ge(*at("ssd_a"))
            stt3(out=dtt[:, 2:4, :], in0=dtt[:, 0:2, :], scalar=-1.0, in1=bc(dtt[:, 5, :], 1, 2), op0=ALU.mult, op1=ALU.mult)\
                .then_inc(*done("la"))
            ssd_conv(0, 0)
            ssd_conv(0, 1)
            for g in range(SG):
                ssd(g)
            ssd_scale(SG - 1)
            T_lo(("y", SG - 1), 4, (4 + 4 * SG) % 16, 6, lambda k: col("ssdn", 4 * SG - 4 + k))
            post(2, ("mo1", 7), 0)
            norm(3, "ffn1")
            ffn(1)
            post(3, ("D", 1, FI - 1))
            norm(4, "sec")

            def head_norm(nm, a, b0):
                for t in range(NT):
                    dve.wait_ge(*at("q_sq", (nm, t)))
                    i = nc.vector.tensor_reduce(st[:, 104 + 8 * t:112 + 8 * t], h3(sqb[:, t, :]), AXX, ALU.add)
                i.then_inc(*done("q_ss", nm))
                dve.wait_ge(*at("root", ("q", nm)))
                lk(nc.vector.reciprocal(st[:, 136:152], st[:, 120:136]))
                if a >= 2:
                    dve.wait_ge(*at("turned", (("qa", "ka")[a - 2], 3)))
                for t in range(NT):
                    o = hn[:, t, 512 * (a % 2):512 * (a % 2) + 512]
                    if nm != "ksv":
                        i = tt(h3(o), h3(PS[:, b0 + t, :]), bc(st[:, 136 + 8 * t:144 + 8 * t], 2, DH), ALU.mult)
                    else:
                        for w in range(2):
                            for r in range(2):
                                i = tt(o[:, 256 * w:256 * w + 256].rearrange("p (g r d) -> p g r d", g=2, r=2)[:, :, r, :],
                                       PS[:, b0 + t, 256 * w:256 * w + 128].rearrange("p (g d) -> p g d", g=2),
                                       bc(st[:, 136 + 8 * t + 4 * w:138 + 8 * t + 4 * w], 2, DH), ALU.mult)
                    i.then_inc(*done("read_v", (nm, t)))

            head_norm("qa", 0, 0)
            head_norm("ka", 1, 2)
            head_norm("qb", 2, 2)

            def windows(a, b):
                lk(nc.vector.memset(XC[a][:, :, :], 0.0))
                pos = cols[:, col_at[("posk", "posv")[a]]:col_at[("posk", "posv")[a]] + 16]
                for g in range(2):
                    for r in range(2):
                        base = PS[64 * r:64 * r + 64, b, g * S + r:g * S + r + 1]
                        src = bass.AP(base.tensor, base.offset, [list(base.ap[0]), [2, 16], [16, NCMP]])
                        i = tt(XC[a][64 * r:64 * r + 64, :, 16 * g:16 * g + NCMP], src,
                               bc(pos[64 * r:64 * r + 64, :], 2, NCMP), ALU.add)
                i.then_inc(*done("read_v", (("kc", "vc")[a], 0)))
                dve.wait_ge(*read((("kc", "vc")[a], 0)))

            dve.wait_ge(*at("w_used", slot_no[("vc", 0)]))
            windows(0, 0)
            windows(1, 1)
            for a in range(2):
                dve.wait_ge(*at("x_hi", a))
                tt(Tl[:, 8 + 2 * a:10 + 2 * a, :].rearrange("p a (b c) -> p (a b) c", c=32), XC[a][:, :, :],
                   Th[:, 8 + 2 * a:10 + 2 * a, :].rearrange("p a (b c) -> p (a b) c", c=32).bitcast(F32), ALU.subtract)\
                    .then_inc(*done("x_lo", a))
            head_norm("ksv", 3, 2)
            dve.wait_ge(*at("c_gelu", 1))
            for m in range(2):
                i = nc.vector.tensor_copy(hidr[:, m, :].rearrange("p (g h c) -> p g h c", g=2, h=4),
                                          bc(hid[:, 1, m, :].rearrange("p (g c) -> p g c", g=2), 2, 4))
            i.then_inc(*done("c_rep"))
            dve.wait_ge(*at("root", "ck"))
            lk(nc.vector.reciprocal(st[0:32, 14:15], st[0:32, 13:14]))
            for r in range(2):
                i = ts(kcm[0:32, 0, DH * r:DH * r + DH], PS[0:32, 4, 64:64 + DH], st[0:32, 14:15], None, ALU.mult)
            i.then_inc(*done("c_kn"))
            dve.wait_ge(*at("c_v"))
            tt(vbd[:, :, :], bc(PS[:, 5, 64:64 + DH], 1, 8), bc(cc("blk"), 2, DH), ALU.mult).then_inc(*done("c_vbd"))
            dve.wait_ge(*at("c_s"))
            for t in range(NT):
                for r in range(2):
                    i = tt(cpr[:, t, :].rearrange("p (h r c) -> p h r c", h=4, r=2)[:, :, r, :],
                           PS[:, 4 + r, 64 * t:64 * t + 64].rearrange("p (h c) -> p h c", h=4),
                           bc(cc("cneg")[:, 16 * t:16 * t + 16], 1, 4), ALU.add)
            lk(i)
            c3 = cpr[:, :, :].rearrange("p t (h c) -> p (t h) c", h=NH)
            lk(nc.vector.tensor_reduce(st[:, 104:120], c3, AXX, ALU.max))
            tt(c3, c3, bc(st[:, 104:120], 2, 16), ALU.subtract).then_inc(*done("c_sub"))
            dve.wait_ge(*at("c_exp"))
            lk(nc.vector.tensor_reduce(st[:, 120:136], c3, AXX, ALU.add))
            for t in range(NT):
                v = cpr[:, t, :].rearrange("p (h c) -> p h c", h=NH)
                i = tt(v, v, bc(cc("cval")[:, 16 * t:16 * t + 16], 1, NH), ALU.mult)
            i.then_inc(*done("c_p"))
            lk(nc.vector.reciprocal(st[:, 136:152], st[:, 120:136]))
            dve.wait_ge(*read(("gb", 1)))
            gates = lambda k: gb[:, :, :].rearrange("p t (h k) -> p t h k", k=3)[:, :, :, k]
            c8 = st[:, 136:152].rearrange("p (t h) -> p t h", t=NT)
            lk(tt(c8, c8, gates(0), ALU.mult))
            dve.wait_ge(*at("c_o"))
            for t in range(NT):
                i = tt(h3(hn[:, t, 512:D]), h3(PS[:, 6 + t, :]), bc(st[:, 136 + 8 * t:144 + 8 * t], 2, DH), ALU.mult)
            i.then_inc(*done("c_oe"))
            dve.wait_ge(*at("c_oe"))
            dve.wait_ge(*at("load_tb", 0))

            def moba_write(j, rc, o):
                return tt(hn[:, :, DH * j:DH * (j + 1)], o, bc(rc, 2, DH), ALU.mult)

            def nsa_write(j, rc, o):
                w, h = j // NH, j % NH
                lk(tt(rc, rc, gates(1 + w)[:, :, h], ALU.mult))
                for t in range(NT):
                    ob = hn[:, t, 512 + DH * h:512 + DH * (h + 1)]
                    i = stt3(out=ob, in0=o[:, t, :], scalar=rc[:, t:t + 1], in1=ob, op0=ALU.mult, op1=ALU.add)
                return i

            tbias = lambda i, t: tb[:, i % NH, P:S] if t == 0 else tb[:, i % NH, :]
            attention("moba", NH, tbias, True, moba_write)
            dve.wait_ge(*at("load_tb", 1))
            attention("nsa", 2 * NH, tbias, True, nsa_write)
            dve.wait_ge(*at("a_o", ("nsa", 2 * NH - 1)))
            dve.wait_ge(*read(("zb", 1)))
            for t in range(NT):
                tt(hn[:, t, 0:512], hn[:, t, 0:512], za[:, t, :], ALU.mult)
                i = tt(hn[:, t, 512:D], hn[:, t, 512:D], zb[:, t, :], ALU.mult)
            i.then_inc(*done("y2"))
            T_lo("y2", KD, 8, 4, lambda k: None)
            for n in range(2):
                for a, nm in enumerate(("YA", "YB")):
                    dve.wait_ge(*read(((("GA", "GB")[a], n), 1)))
                    dve.wait_ge(*at("w_used", slot_no[((nm, n), 0)]))
                    for t in range(NT):
                        o = hn[:, t, 512 * n:512 * n + 512]
                        i = tt(o if a == 0 else sg[1][:, t, :], sg[a][:, t, :], PS[:, 4 + 2 * a + t, :], ALU.mult)
                    i.then_inc(*done("mrg_p", (n, a)))
                    if a == 1:
                        dve.wait_ge(*at("mrg_p", (n, 1)))
                        for t in range(NT):
                            o = hn[:, t, 512 * n:512 * n + 512]
                            i = tt(o, o, sg[1][:, t, :], ALU.add)
                        i.then_inc(*done("mrg", (n, 1)))
            T_lo("mrg", KD, 0, 0, lambda k: None)
            dve.wait_ge(*at("w_used", slot_no[("fo", 3)]))
            for t in range(NT):
                for hf in range(2):
                    o = x[:, t, 512 * hf:512 * hf + 512]
                    i = tt(o, o, PS[:, 4 + 2 * t + hf, :], ALU.add)
            i.then_inc(*done("x", (5, NT - 1)))
        return C.marks


_INS = ["x", "norm_mix_pre", "norm_mix_post", "norm_ffn_pre", "norm_ffn_post", "ab_w_in", "ab_ret_decay_logit",
        "ab_ret_gn_g", "ab_na_rpb", "ab_w_out", "c_w_in", "c_conv_w", "c_conv_b", "c_dt_bias", "c_a_log", "c_d_skip",
        "c_norm_g", "c_w_out", "ffn_w_up", "ffn_conv_w", "ffn_conv_b", "ffn_w_down", "norm_w_2", "w_in_2",
        "q_norm_a_2", "k_norm_a_2", "q_norm_b_2", "k_norm_cmp_2", "k_norm_sel_2", "k_norm_win_2", "cmp_pos_k_2",
        "cmp_w1_k_2", "cmp_w2_k_2", "cmp_pos_v_2", "cmp_w1_v_2", "cmp_w2_v_2", "rel_bias_2", "w_branch_a_2",
        "w_branch_b_2", "w_out_2"]


def kernel(**inputs):
    import numpy as _np
    import concourse.bacc as _bacc
    from concourse import mybir as _mybir
    from concourse.bass_utils import run_bass_kernel_spmd as _run

    arrays = {f"in_{n}_dram": _np.ascontiguousarray(inputs[n]) for n in _INS}
    for n, a in (("const_table", CONST_TABLE), ("const_pfb", CONST_PFB), ("const_onehot", CONST_ONEHOT),
                 ("const_negs", CONST_NEGS)):
        arrays[f"in_{n}_dram"] = a
    known = None
    for _ in range(2):
        nc = _bacc.Bacc("TRN2", target_bir_lowering=False, num_devices=1)
        handles = {name[3:-5]: nc.dram_tensor(name, a.shape, _mybir.dt.from_np(a.dtype), kind="ExternalInput").ap()
                   for name, a in arrays.items()}
        out = nc.dram_tensor("out_0_dram", (1, S, D), _mybir.dt.float32, kind="ExternalOutput").ap()
        known = build(nc, handles, out, known)
    r = _run(nc, [arrays], core_ids=[0])
    return r.results[0]["out_0_dram"]
```

```python
from contextlib import ExitStack

import numpy as np

import concourse.bass as bass
from concourse import mybir

ALU = mybir.AluOpType
ACT = mybir.ActivationFunctionType
F32 = mybir.dt.float32
F32R = mybir.dt.float32r
AXX = mybir.AxisListType.X

P = 128
S = 256
NT = S // P
D = 1024
KD = D // P
EPS = 1e-6
NEG = -1e30
DH = 64
NH = 8
FF = 2816
FI = FF // 256
SI = 2048
SG = 4
SHG = 8
XBC = SI + 2 * SG * P
CL, CS, NCMP = 32, 16, 15
GW = 64
NRAW, NHI, NLO = 4, 3, 3
SLOT = 2048


class Counts:

    def __init__(self, nc, ctx, known):
        self.nc, self.ctx, self.known = nc, ctx, known
        self.sems, self.count, self.marks = {}, {}, {}

    def sem(self, family):
        if family not in self.sems:
            self.sems[family] = self.ctx.enter_context(self.nc.semaphore(family))
            self.count[family] = 0
        return self.sems[family]

    def done(self, family, key=0, by=1):
        s = self.sem(family)
        self.count[family] += by
        assert (family, key) not in self.marks or by == 16, (family, key)
        self.marks[(family, key)] = self.count[family]
        return s, by

    def at(self, family, key=0):
        s = self.sem(family)
        if self.known is None:
            return s, max(1, self.marks.get((family, key), 1))
        return s, self.known[(family, key)]


def bc(ap, axis, n):
    a = ap.unsqueeze(axis)
    shape = list(a.shape)
    shape[axis] = n
    return a.to_broadcast(shape)


def shape_constants():
    i = np.arange(P)
    ident = np.eye(P)
    u, t = i[:, None], i[None, :]
    le, gt, lt, ge = (u <= t), (u > t), (u < t), (u >= t)
    half = DH // 2
    inv = (1.0 / (np.float32(10000.0) ** (np.arange(half, dtype=np.float32) / np.float32(half)))).astype(np.float32)
    ang = (np.arange(S, dtype=np.float32)[:, None] * inv[None, :]).astype(np.float32).astype(np.float64)
    cos = np.concatenate([np.cos(ang), np.cos(ang)], 1).reshape(NT, P, DH).transpose(1, 0, 2).reshape(P, -1)
    sin = np.concatenate([-np.sin(ang), np.sin(ang)], 1).reshape(NT, P, DH).transpose(1, 0, 2).reshape(P, -1)
    s_all = (np.arange(NT)[None, :, None] * P + i[:, None, None])
    dist = np.arange(S)[None, None, :] - s_all
    pf, pb = np.maximum(dist, 0).reshape(P, -1), np.maximum(-dist, 0).reshape(P, -1)
    qc = i % GW
    kc = np.arange(GW)
    c0 = np.clip(qc - 8, 0, GW - 16)[:, None]
    nm = np.where((kc[None] >= c0) & (kc[None] < c0 + 16), 0.0, NEG)
    tok = (np.arange(NT)[None, :, None] * P + i[:, None, None])
    cend = np.arange(16)[None, None, :] * CS + CL - 1
    cv = (cend <= tok) & (np.arange(16)[None, None, :] < NCMP)
    cneg = np.where(cv, 0.0, NEG).reshape(P, -1)
    blk = (i[:, None] // 16 == np.arange(8)[None, :])
    parts = [("ident", ident), ("le", le), ("gt", gt), ("lt", lt), ("ge", ge), ("cos", cos), ("sin", sin),
             ("nm", nm), ("cneg", cneg), ("cval", cv.reshape(P, -1)), ("blk", blk)]
    at, n = {}, 0
    for name, a in parts:
        at[name] = (n, n + a.shape[1])
        n += a.shape[1]
    table = np.concatenate([a.astype(np.float32) for _, a in parts], 1)
    pfb = np.concatenate([pf, pb], 1).astype(np.float32)
    dd = 255 - np.arange(384)
    n_ = np.maximum(dd, 0)
    nf = np.maximum(n_, 16).astype(np.float32)
    large = 16 + (np.log(nf / np.float32(16)) / np.float32(np.log(64.0)) * np.float32(16)).astype(np.int32)
    bucket = np.where(n_ < 16, n_, np.minimum(large, 31))
    onehot = ((np.arange(32)[:, None] == bucket[None, :]) & (dd[None, :] >= 0)).astype(np.float32)
    negs = np.tile(np.where(dd >= 0, 0.0, NEG)[None, :], (16, 1)).astype(np.float32)
    return at, table, pfb, onehot, negs


CONST_AT, CONST_TABLE, CONST_PFB, CONST_ONEHOT, CONST_NEGS = shape_constants()
NCONST = CONST_TABLE.shape[1]


def vector_rows(I):
    r = lambda ap: ap.rearrange("(k p) -> k p", p=P)
    rows = []
    rows.append(("mix1", r(I["norm_mix_pre"][1])))
    for l in range(2):
        rows.append((f"ffn{l}", r(I["norm_ffn_pre"][l])))
    rows.append(("sec", r(I["norm_w_2"][0])))
    rows.append(("gn", r(I["ab_ret_gn_g"][0])))
    rows.append(("ssdn", r(I["c_norm_g"][0])))
    rows.append(("posk", I["cmp_pos_k_2"][0].rearrange("(j r) d -> j (r d)", r=2)))
    rows.append(("posv", I["cmp_pos_v_2"][0].rearrange("(j r) d -> j (r d)", r=2)))
    for k in range(5):
        rows.append((f"cw{k}", r(I["c_conv_w"][0, k])))
    rows.append(("cb", r(I["c_conv_b"][0])))
    for l in range(2):
        for k in range(3):
            rows.append((f"fw{l}{k}", r(I["ffn_conv_w"][l, k])))
        rows.append((f"fb{l}", r(I["ffn_conv_b"][l])))
    return rows


def build(nc, I, out, known):
    ctx = ExitStack()
    with ctx:
        C = Counts(nc, ctx, known)
        done, at = C.done, C.at

        def sb(name, shape, dt=F32):
            return ctx.enter_context(nc.sbuf_tensor(name, shape, dt))

        PS = ctx.enter_context(nc.psum_tensor("PS", [P, 8, 512], F32))
        x = sb("x", [P, NT, D])
        hn = sb("hn", [P, NT, D])
        Th = sb("Th", [P, 16, S], F32R)
        Tl = sb("Tl", [P, 16, S], F32R)
        aTh = sb("aTh", [P, 2, 2, S], F32R)
        aTl = sb("aTl", [P, 2, 2, S], F32R)
        raw = [sb(f"raw{i}", [P, SLOT]) for i in range(NRAW)]
        whi = [sb(f"whi{i}", [P, SLOT], F32R) for i in range(NHI)]
        wlo = [sb(f"wlo{i}", [P, SLOT], F32R) for i in range(NLO)]
        gpost = sb("gpost", [P, D])
        cst = sb("cst", [P, NCONST])
        rows = vector_rows(I)
        col_at, n = {}, 0
        for name, ap in rows:
            k = ap.shape[0]
            if n % P + k > P:
                n += P - n % P
            col_at[name] = n
            n += k
        NR = -(-(n + 1) // P)
        qn = NR * P
        cols = sb("cols", [P, NR * P + 16])
        col_at["mix0"] = NR * P + 8
        st = sb("st", [P, 160])
        eps = sb("eps", [P, 1])
        sqj = sb("sqj", [P, 512])
        A = sb("arena", [P, 14800])

        def cc(name):
            a, b = CONST_AT[name]
            return cst[:, a:b]

        ident = cc("ident")

        def col(name, j=0):
            c = col_at[name] + j
            return cols[:, c:c + 1]

        slots, slot_no = [], {}

        def add(name, parts, width):
            slot_no[name] = len(slots)
            slots.append((parts, width))

        def wide(name, w, k0, c0, nk, nc_):
            add(name, [((nk, nc_, 0, nc_), w[k0 * P:(k0 + nk) * P, c0:c0 + nc_])], nk * nc_)

        def tm(name, w, c0, k0=0):
            for hf in range(2):
                wide((name, hf), w, k0 + 4 * hf, c0, 4, 512)

        def fm(name, w, c0, k0=0, j=0):
            wide((name, j), w, k0, c0, 8, 256)

        def dn(name, w, n, k0=0):
            for j in range(n):
                wide((name, j), w, k0 + 2 * j, 0, 2, 1024)

        def ffn_down(i):
            return [] if i in (0, FI - 2) else [FI - 3, FI - 2] if i == FI - 1 else [i - 1]

        def ffn_slots(l):
            up, down = I["ffn_w_up"][l], I["ffn_w_down"][l]
            for i in range(FI + 1):
                if i < FI:
                    wide(("G", l, i), up, 0, 256 * i, 8, 256)
                    wide(("V", l, i), up, 0, FF + 256 * i, 8, 256)
                for j in ffn_down(i):
                    wide(("D", l, j), down, 2 * j, 0, 2, 1024)

        win = I["ab_w_in"][0]
        tm("rq", win, 0)
        tm("rk", win, 512)
        tm("rv", win, 1024)
        for j in range(2):
            fm("nq", win, 2048 + 256 * j, j=j)
        for j in range(2):
            fm("nk", win, 2560 + 256 * j, j=j)
        tm("nv", win, 3072)
        tm("rg", win, 1536)
        dn("mo0", I["ab_w_out"][0], 4)
        ffn_slots(0)
        cwin = I["c_w_in"][0]
        wide(("dt", 0), cwin, 0, SI + XBC, 8, 64)
        for g in range(SG):
            add((("bc", g), 0), [((8, 256, 128 * m, 128 * m + 128),
                                  cwin[:, 2 * SI + 512 * m + P * g:2 * SI + 512 * m + P * (g + 1)]) for m in range(2)],
                SLOT)
            for j in range(2):
                fm(("xs", g), cwin, SI + 512 * g + 256 * j, j=j)
            tm(("z", g), cwin, 512 * g)
        dn("mo1", I["c_w_out"][0], 8)
        ffn_slots(1)
        w2 = I["w_in_2"][0]
        KV = 2560
        tm("qa", w2, 0)
        tm("ka", w2, 512)
        tm("va", w2, 1024)
        tm("qb", w2, 2048)
        for n, nm in enumerate(("kc", "vc")):
            add((nm, 0), [((8, 256, 128 * g + 64 * r, 128 * g + 64 * r + 64),
                           w2[:, KV + 128 * n + 64 * g:KV + 128 * n + 64 * g + 64])
                          for g in range(2) for r in range(2)], SLOT)
        tm("ksv", w2, KV + 256)
        tm("za", w2, 1536)
        tm("zb", w2, KV + 792)
        wide(("gb", 0), w2, 0, KV + 768, 8, 24)
        for nm in ("k", "v"):
            for j in range(2):
                fm("w1" + nm, I["cmp_w1_" + nm + "_2"][0], 0, k0=8 * j, j=j)
        GM = KV + 792 + 512
        for a, nm in enumerate(("GA", "GB")):
            for n in range(2):
                tm((nm, n), w2, GM + D * a + 512 * n)
        for nm, w in (("YA", I["w_branch_a_2"][0]), ("YB", I["w_branch_b_2"][0])):
            for n in range(2):
                wide(((nm, n), 0), w, 0, 512 * n, 4, 512)
        dn("fo", I["w_out_2"][0], 4)
        NS = len(slots)

        by_vector = {0} | {slot_no[("D", l, i)] for l in range(2) for i in range(FI - 2)} | {slot_no[("w1k", 0)], slot_no[("w1v", 0)]}

        def view(a, *shape):
            n = int(np.prod(shape))
            v = A[:, a:a + n]
            if len(shape) == 2:
                v = v.rearrange("p (a b) -> p a b", a=shape[0])
            elif len(shape) == 3:
                v = v.rearrange("p (a b c) -> p a b c", a=shape[0], b=shape[1])
            return v

        rqk = [view(1024 * i, NT, 512) for i in range(2)]
        nabias = view(0, NH, 6 * GW)
        rv, rg, nv = (view(3072 + 1024 * i, NT, 512) for i in range(3))
        rqT, rkT, nqT, nkT = (view(6144 + 1024 * i, 4, S) for i in range(4))
        gsq = view(6144, NT, 512)
        pfb = view(10240, 2, 512)
        dcy = [view(11264 + 512 * i, 512) for i in range(2)]
        msc = [view(12288 + 512 * i, 512) for i in range(2)]
        spxs = {"ret": view(13400, 8, 16), "ssd": view(8448, 8, 128)}
        lg = A[:, 14500:14516]
        brow = A[:, 14516:14532]
        zt = [view(1024 * i, NT, 512) for i in range(2)]
        xs = [view(2048 + 1024 * i, NT, 512) for i in range(2)]
        bct = [view(4096 + 512 * i, 2, S) for i in range(2)]
        btm = view(5120, NT, P)
        vfb = view(5376, 2, NT, 512)
        vt = view(7424, 2, 512)
        am = [view(8448 + 512 * i, 4, P) for i in range(2)]
        ee = [view(9472 + 512 * i, 4, P) for i in range(2)]
        cvb = view(10496, 6, S)
        qk = view(12032, 2, NT, P)
        stt = view(12544, 2, 512)
        dtt = view(13568, 12, 64)
        qaT, kaT, qbT = (view(1024 * i, 4, S) for i in range(3))
        va, za, zb = (view(3072 + 1024 * i, NT, 512) for i in range(3))
        kswT = view(6144, 4, S)
        vsw = view(7168, NT, 2, P)
        tb = view(7680, NH, S)
        sqb = view(9728, NT, 512)
        XC = [view(10752 + 512 * i, 16, 32) for i in range(2)]
        sc = [view(10752 + 512 * i, NT, S) for i in range(2)]
        pt = [view(11776 + 512 * i, 4, P) for i in range(2)]
        hid = view(12800, 2, 32)
        hidt = gpost[0:32, 0:512].rearrange("p (a c) -> p a c", a=2)
        hidr = view(12928, 2, P)
        vbd = view(13184, 8, DH)
        kcm = view(13696, 2, P)
        kcT = view(13952, 32)
        w2c = view(13984, 2, 2, DH)
        gb = view(14240, NT, 24)
        cpr = view(14288, NT, P)
        cpt = view(14544, NT, P)
        sg = {("GA", 0): view(0, NT, 512), ("GB", 0): view(1024, NT, 512), ("GA", 1): view(3072, NT, 512), ("GB", 1): sqb}
        fac = [view(1024 * i, 4, S) for i in range(2)]
        fpr = [view(2048 + 512 * i, 2, S) for i in range(2)]
        rowb = view(6144, NR + 1, P)
        rowm = A[0:8, 7040:7168]
        oneh = A[0:32, 7168:7552]
        negs = A[0:16, 7552:7936]
        relb = A[0:32, 7936:7952]
        t5r = A[0:16, 13600:13984]

        def also(table):
            def f(i):
                for g in table.get(i, ()):
                    g()
            return f

        chain = {}

        def link(eng, name, ins):
            chain[name] = chain.get(name, 0) + 1
            ins.then_inc(*done(name + "_chain", chain[name]))
            eng.wait_ge(*at(name + "_chain", chain[name]))

        def low(n):
            return at("w_lo_v" if n in by_vector else "w_lo", n)

        def xbc_bank(g, j):
            return (3, 2, 2 if g else 1)[j]

        def norm_bank(l):
            return 0 if l in (2, 4) else 4

        def read(key):
            by_scalar = known is None or ("read_a", key) in known
            return at("read_a" if by_scalar else "read_v", key)

        toe = nc.dram_tensor("t5_rows", [16, P, 384], F32, kind="Internal").ap()
        narep = nc.dram_tensor("na_rows", [NH, GW, 465], F32, kind="Internal").ap()
        block = ctx.enter_context(nc.Block())

        @block.sync
        def _(sp):
            def set_up_loads():
                sp.dma_start(cst[:, P:NCONST], I["const_table"][:, P:NCONST]).then_inc(*done("load_cst", 0, 16))
                sp.wait_ge(*at("rows_clear"))
                for name, ap in rows:
                    c = col_at[name]
                    sp.dma_start(rowb[c % P:c % P + ap.shape[0], c // P, :], ap).then_inc(*done("load_rows", 0, 16))
                for j, nm in enumerate(("q_norm_a_2", "k_norm_a_2", "q_norm_b_2", "k_norm_sel_2", "k_norm_win_2", "k_norm_cmp_2")):
                    sp.dma_start(rowb[j:j + 1, NR, :].rearrange("p (r d) -> p r d", r=2),
                                 bc(I[nm], 1, 2)).then_inc(*done("load_rows", 0, 16))
                sp.dma_start(oneh, I["const_onehot"]).then_inc(*done("load_t5", 0, 16))
                sp.dma_start(negs, I["const_negs"]).then_inc(*done("load_t5", 0, 16))
                sp.dma_start(relb, I["rel_bias_2"]).then_inc(*done("load_t5", 0, 16))
                sp.dma_start(brow, I["ab_ret_decay_logit"].rearrange("a b c -> a (b c)").to_broadcast([P, 16]))\
                    .then_inc(*done("load_dl", 0, 16))
                sp.dma_start(narep, bc(I["ab_na_rpb"][0].rearrange("h a b -> h (a b)"), 1, GW)).then_inc(*done("na_rows", 0, 16))

            for t in range(NT):
                sp.dma_start(x[:, t, :], I["x"][0, t * P:(t + 1) * P]).then_inc(*done(f"load_x{t}", 0, 16))
            for n, (parts, width) in enumerate(slots):
                if n == NRAW:
                    set_up_loads()
                if n == slot_no[("nv", 1)]:
                    sp.wait_ge(*at("na_rows"))
                    sp.wait_ge(*at("turned", ("rk", 3)))
                    for h in range(NH):
                        for q in range(2):
                            src = bass.AP(narep.tensor, h * GW * 465 + (5 - q) * 31 + 15, [[464, GW], [31, 6], [1, GW]])
                            sp.dma_start(nabias[q * GW:(q + 1) * GW, h, :].rearrange("p (a b) -> p a b", a=6), src)\
                                .then_inc(*done("load_na", 0, 16))
                if n >= NRAW:
                    sp.wait_ge(*low(n - NRAW))
                for (nk, nc_, a, b), src in parts:
                    dst = raw[n % NRAW][:, 0:nk * nc_].rearrange("p (k c) -> p k c", k=nk)[:, :, a:b]
                    sp.dma_start(dst, src.rearrange("(k p) c -> p k c", p=P))\
                        .then_inc(*done(f"w_raw{n % NRAW}", n, 16))
            for t in range(NT):
                sp.wait_ge(*at("x", (5, t)))
                sp.dma_start(out[0, t * P:(t + 1) * P], x[:, t, :]).then_inc(*done("stored", 0, 16))
            sp.wait_ge(*at("stored", 0))

        @block.gpsimd
        def _(pool):
            for n, (parts, width) in enumerate(slots):
                if n in by_vector:
                    continue
                pool.wait_ge(*at("w_hi", n))
                if n >= NLO:
                    pool.wait_ge(*at("w_used", n - NLO))
                nc.gpsimd.tensor_tensor(wlo[n % NLO][:, 0:width], raw[n % NRAW][:, 0:width],
                                        whi[n % NHI][:, 0:width].bitcast(F32), ALU.subtract)\
                    .then_inc(*done("w_lo", n))

        @block.tensor
        def _(pe):
            mm = nc.tensor.matmul

            def three(o, wh, wl, ah, al, first, last, moving_w):
                if moving_w:
                    mm(o, ah, wh, start=first, stop=False)
                    mm(o, ah, wl, start=False, stop=False)
                    return mm(o, al, wh, start=False, stop=last)
                mm(o, wh, ah, start=first, stop=False)
                mm(o, wh, al, start=False, stop=False)
                return mm(o, wl, ah, start=False, stop=last)

            def slot_tm(name, b0, kt0, first, last, ncol=512, nk=4, fresh=None, f0=None):
                n = slot_no[name]
                pe.wait_ge(*low(n))
                h, l = whi[n % NHI], wlo[n % NLO]
                for k in range(nk):
                    if fresh:
                        pe.wait_ge(*at("T_lo", (fresh, (kt0 % KD if f0 is None else f0) + k)))
                    for t in range(NT):
                        i = three(PS[:, b0 + t, 0:ncol], h[:, k * ncol:(k + 1) * ncol], l[:, k * ncol:(k + 1) * ncol],
                                  Th[:, kt0 + k, t * P:(t + 1) * P], Tl[:, kt0 + k, t * P:(t + 1) * P],
                                  first and k == 0, last and k == nk - 1, True)
                i.then_inc(*done("w_used", n))

            def block_tm(name, b0, fresh=None):
                slot_tm((name, 0), b0, 0, True, False, fresh=fresh)
                slot_tm((name, 1), b0, 4, False, True, fresh=fresh)

            def slot_fm(name, b, fresh=None):
                n = slot_no[name]
                pe.wait_ge(*low(n))
                h, l = whi[n % NHI], wlo[n % NLO]
                for m in range(2):
                    for k in range(KD):
                        if fresh and m == 0:
                            pe.wait_ge(*at("T_lo", (fresh, k)))
                        c = k * 256 + m * P
                        i = three(PS[:, b, m * S:(m + 1) * S], h[:, c:c + P], l[:, c:c + P], Th[:, k, :], Tl[:, k, :],
                                  k == 0, k == KD - 1, False)
                i.then_inc(*done("w_used", n))

            def slot_dn(name, ah, al, first, last, b0=4):
                n = slot_no[name]
                pe.wait_ge(*low(n))
                h, l = whi[n % NHI], wlo[n % NLO]
                order = [(k, t, hf) for t in range(NT) for hf in range(2) for k in range(2)] if last else \
                    [(k, t, hf) for k in range(2) for t in range(NT) for hf in range(2)]
                for j, (k, t, hf) in enumerate(order):
                    c = k * D + hf * 512
                    i = three(PS[:, b0 + 2 * t + hf, :], h[:, c:c + 512], l[:, c:c + 512], ah(k, t), al(k, t),
                              first and k == 0, last and k == 1, True)
                    if last and j % 2 == 1 and j < 7:
                        i.then_inc(*done("sum", (n, t, hf)))
                i.then_inc(*done("w_used", n))

            def tr(o, src, idn):
                return nc.tensor.transpose(o, src, idn)

            def to_T(name, src, nk, b0):
                for k in range(nk):
                    for t in range(NT):
                        i = tr(PS[:, b0 + k // 2, (k % 2) * S + t * P:(k % 2) * S + (t + 1) * P],
                               src[:, t, k * P:(k + 1) * P], ident)
                    i.then_inc(*done("turned", (name, k)))

            def norm_T(l):
                for t in range(NT):
                    pe.wait_ge(*at("n_hn", (l, t)))
                    for k in range(KD):
                        i = tr(PS[:, norm_bank(l) + k // 2, (k % 2) * S + t * P:(k % 2) * S + (t + 1) * P],
                               hn[:, t, k * P:(k + 1) * P], ident)
                        if t == NT - 1:
                            i.then_inc(*done("turned", (("n", l), k)))

            def out_slot(name, j, n, kt, fresh):
                pe.wait_ge(*at("T_lo", fresh))
                slot_dn((name, j), lambda k, t: Th[:, kt + k, t * P:(t + 1) * P],
                        lambda k, t: Tl[:, kt + k, t * P:(t + 1) * P], j == 0, j == n - 1, 0)

            def ffn(l):
                for i in range(FI + 1):
                    if i < FI:
                        if i >= 2:
                            pe.wait_ge(*at("f_conv", (l, i - 2)))
                        slot_fm(("G", l, i), 2 * (i % 2), ("n", 2 * l + 1) if i == 0 else None)
                        if i == 0:
                            pe.wait_ge(*at("T_lo", (("n", 2 * l + 1), KD - 1)))
                        slot_fm(("V", l, i), 2 * (i % 2) + 1)
                    for j in ffn_down(i):
                        pe.wait_ge(*at("f_alo", (l, j)))
                        p = j % 2
                        slot_dn(("D", l, j), lambda k, t: aTh[:, p, k, t * P:(t + 1) * P],
                                lambda k, t: aTl[:, p, k, t * P:(t + 1) * P], j == 0, j == FI - 1)

            pe.wait_ge(*at("load_ident"))
            pe.wait_ge(*at("load_mix0"))
            tr(PS[:, 0, 0:8], rowm, ident[0:8, 0:8]).then_inc(*done("mix0_T"))
            norm_T(0)
            pe.wait_ge(*at("mix0_col"))
            block_tm("rq", 0, ("n", 0))
            pe.wait_ge(*at("load_rows"))
            for r in range(NR):
                i = tr(PS[:, 4 + r // 4, (r % 4) * P:(r % 4 + 1) * P], rowb[:, r, :], ident)
            i = tr(PS[:, 6, 0:8], rowb[0:8, NR, :], ident[0:8, 0:8])
            pe.wait_ge(*at("load_t5"))
            mm(PS[0:16, 7, 0:384], relb, oneh, start=True, stop=True).then_inc(*done("set_up"))
            block_tm("rk", 2)
            pe.wait_ge(*at("load_cst"))
            pe.wait_ge(*read(("rq", 1)))
            block_tm("rv", 0)
            pe.wait_ge(*at("cols_act"))
            pe.wait_ge(*at("cols"))
            for a, nm in enumerate(("rq", "rk")):
                pe.wait_ge(*at("rope", (nm, 1)))
                to_T(nm, rqk[a], 4, 4 + 2 * a)
            pe.wait_ge(*read(("rk", 1)))
            slot_fm(("nq", 0), 2)
            pe.wait_ge(*at("rT", ("rq", 1)))
            pe.wait_ge(*at("rT", ("rk", 1)))

            def ret_scores(h):
                b, k = (h % 2) * DH, h // 2
                if h >= 2:
                    pe.wait_ge(*at("r_m", h - 2))
                for s in range(NT):
                    i = mm(PS[:, 4 + h % 2, s * S:(s + 1) * S], rkT[b:b + DH, k, s * P:(s + 1) * P],
                           rqT[b:b + DH, k, :], start=True, stop=True)
                i.then_inc(*done("r_s", h))

            def ret_out(h):
                pe.wait_ge(*at("r_m", h))
                if h == 0:
                    pe.wait_ge(*read(("rv", 1)))
                for t in range(NT):
                    for s in range(NT):
                        i = mm(PS[:, 6 + t, h * DH:(h + 1) * DH],
                               msc[h % 2][:, s * S + t * P:s * S + (t + 1) * P],
                               rv[:, s, h * DH:(h + 1) * DH], start=s == 0, stop=s == NT - 1)
                i.then_inc(*done("r_pv", h))

            for h in range(NH + 1):
                if h < NH:
                    ret_scores(h)
                if h >= 1:
                    ret_out(h - 1)
                if h == 1:
                    slot_fm(("nq", 1), 3)
                elif h in (2, 3):
                    slot_fm(("nk", h - 2), h - 2)
                elif h in (4, 5):
                    pe.wait_ge(*read(("nq", 1)))
                    slot_tm(("nv", h - 4), 2, 4 * (h - 4), h == 4, h == 5)
                elif h in (6, 8):
                    pe.wait_ge(*read(("nk", 1)))
                    slot_tm(("rg", h // 2 - 3), 0, 4 * (h // 2 - 3), h == 6, h == 8)

            def attention(tag, heads, after):
                def scores(i):
                    q, k, _, causal = heads[i]
                    if i >= 2:
                        pe.wait_ge(*at("a_sc", (tag, i - 2)))
                    for t in range(NT):
                        nk = P if causal and t == 0 else S
                        n = mm(PS[:, 4 + i % 2, t * S:t * S + nk], q(t), k(nk), start=True, stop=True)
                    n.then_inc(*done("a_s", (tag, i)))

                def turn(i):
                    causal = heads[i][3]
                    pe.wait_ge(*at("a_exp", (tag, i)))
                    if i >= 1:
                        pe.wait_ge(*at("a_pt", (tag, i - 1)))
                    for t in range(NT):
                        for c in range(1 if causal and t == 0 else 2):
                            n = tr(PS[:, 6, (2 * t + c) * P:(2 * t + c + 1) * P], sc[i % 2][:, t, c * P:(c + 1) * P], ident)
                    n.then_inc(*done("a_t", (tag, i)))

                def values(i):
                    causal = heads[i][3]
                    pe.wait_ge(*at("a_pt", (tag, i)))
                    if i >= 1:
                        pe.wait_ge(*at("a_o", (tag, i - 1)))
                    for t in range(NT):
                        nc_ = 1 if causal and t == 0 else 2
                        for c in range(nc_):
                            a = (i % 4) * P + t * DH
                            n = mm(PS[:, 7, a:a + DH], pt[i % 2][:, 2 * t + c, :], heads[i][2](c),
                                   start=c == 0, stop=c == nc_ - 1)
                    n.then_inc(*done("a_v", (tag, i)))

                n = len(heads)
                for i in range(n + 2):
                    if i < n:
                        scores(i)
                    if 1 <= i <= n:
                        turn(i - 1)
                    if i >= 2:
                        values(i - 2)
                    after(i)

            def operands(h, qT, kT, kk, v, causal):
                b = (h % 2) * DH
                return (lambda t: qT[b:b + DH, h // 2, t * P:(t + 1) * P], lambda nk: kT[b:b + DH, kk, 0:nk], v, causal)

            pe.wait_ge(*read(("nv", 1)))
            pe.wait_ge(*at("gn_c", 1))

            def turn_ret():
                pe.wait_ge(*read(("rg", 1)))
                pe.wait_ge(*at("y0a"))
                to_T("y0a", hn, 4, 0)

            attention("na", [operands(h, nqT, nkT, h // 2, lambda c, h=h: nv[:, c, h * DH:(h + 1) * DH], False)
                             for h in range(NH)],
                      also({2: (turn_ret,), 4: (lambda: pe.wait_ge(*at("T_lo", ("y0a", 3))),
                                                lambda: out_slot("mo0", 0, 4, 8, ("y0a", 1))),
                            7: (lambda: out_slot("mo0", 1, 4, 10, ("y0a", 3)),)}))
            pe.wait_ge(*at("a_o", ("na", NH - 1)))
            to_T("y0b", hn[:, :, 512:D], 4, 4)
            for j in (2, 3):
                out_slot("mo0", j, 4, 8 + 2 * j, ("y0b", 2 * j - 3))
            norm_T(1)
            ffn(0)
            norm_T(2)

            slot_tm(("dt", 0), 4, 0, True, True, 64, 8, fresh=("n", 2))

            def ssd_slot(g, j):
                if g == SG:
                    for j in (j, j + 1) if j == 4 else (j,):
                        ssd_out(j)
                elif j == 0:
                    if g >= 1:
                        pe.wait_ge(*at("c_cnv", (g - 1, 1)))
                    slot_fm((("bc", g), 0), xbc_bank(g, 2))
                elif j == 1:
                    if g >= 1:
                        pe.wait_ge(*at("c_cnv", (g - 1, 0)))
                    slot_fm((("xs", g), 0), 3)
                elif j == 2:
                    if g >= 1:
                        pe.wait_ge(*at("c_cnv", (g, 2)))
                    slot_fm((("xs", g), 1), 2)
                elif j == 3:
                    pe.wait_ge(*(read((("z", g - 1), 1)) if g else at("c_cnv", (0, 2))))
                    slot_tm((("z", g), 0), 0, 0, True, False)
                else:
                    slot_tm((("z", g), 1), 0, 4, False, True)

            def ssd_out(j):
                if j == 0:
                    pe.wait_ge(*read((("z", SG - 1), 1)))
                    pe.wait_ge(*at("c_cnv", (SG - 1, 0)))
                    pe.wait_ge(*at("c_cnv", (SG - 1, 1)))
                out_slot("mo1", j, 8, (8 + 2 * j) % 16, (("y", j // 2), 2 * (j % 2) + 1))

            def ssd_turn(g):
                pe.wait_ge(*at("s_y", g))
                to_T(("y", g), hn[:, :, (g % 2) * 512:(g % 2) * 512 + 512], 4, 6)

            def ssd(g):
                fill = lambda j: ssd_slot(g + 1, j)
                pe.wait_ge(*at("cv", (g, 1)))
                if g == 0:
                    pe.wait_ge(*at("ex"))
                for t in range(NT):
                    for j in range(4):
                        i = tr(PS[:, 4 + t, j * P:(j + 1) * P], cvb[:, j, t * P:(t + 1) * P], ident)
                i.then_inc(*done("s_xt", g))
                if g:
                    pe.wait_ge(*at("s_add", g - 1))
                for c in range(NT):
                    tr(PS[:, 6, c * P:(c + 1) * P], bct[g % 2][:, 0, c * P:(c + 1) * P], ident)
                for c in range(NT):
                    i = mm(PS[:, 6, S + c * P:S + (c + 1) * P], bct[g % 2][:, 0, c * P:(c + 1) * P],
                           bct[g % 2][:, 1, c * P:(c + 1) * P], start=True, stop=True)
                i.then_inc(*done("s_bq", g))
                fill(0)
                pe.wait_ge(*at("s_v", g))
                for r in range(2):
                    i = mm(PS[:, 4 + r, :], btm[:, r, :], vt[:, r, :], start=True, stop=True)
                i.then_inc(*done("s_st", g))
                fill(1)
                pe.wait_ge(*at("s_ste", g))
                for r in range(2):
                    c = 1 - r
                    i = mm(PS[:, 4 + r, :], bct[g % 2][:, 1, c * P:(c + 1) * P], stt[:, r, :], start=True, stop=True)
                i.then_inc(*done("s_yi", g))
                if g:
                    ssd_turn(g - 1)
                fill(2)
                pe.wait_ge(*at("s_yie", g))
                if g:
                    pe.wait_ge(*at("T_lo", (("y", g - 1), 3)))

                def seg(u):
                    c, r, hf = u // 4, (u // 2) % 2, u % 2
                    pe.wait_ge(*at("s_am", (g, u)))
                    if u >= 2:
                        pe.wait_ge(*at("s_e", (g, u - 2)))
                    mm(PS[:, 4 + u % 2, :], cc("gt" if r == 0 else "lt"), am[u % 2][:, :, :],
                       start=True, stop=True).then_inc(*done("s_l", (g, u)))

                def diag(u):
                    c, r, hf = u // 4, (u // 2) % 2, u % 2
                    pe.wait_ge(*at("s_m", (g, u)))
                    for k in range(4):
                        h = 4 * hf + k
                        i = mm(PS[:, 7 - c, h * DH:(h + 1) * DH], ee[u % 2][:, k, :], vfb[:, r, c, h * DH:(h + 1) * DH],
                               start=u % 4 == 0 and k == 0, stop=False, skip_group_check=True)
                    i.then_inc(*done("s_pv", (g, u)))

                for u in range(9):
                    if u < 8:
                        seg(u)
                    if u >= 1:
                        diag(u - 1)
                    if u == 4:
                        fill(3)
                fill(4)

            for j in range(5):
                ssd_slot(0, j)
                if j == 3:
                    pe.wait_ge(*at("la"))
                    for k, (m, c, dr) in enumerate((("gt", 0, 0), ("lt", 1, 1), ("le", 1, 0), ("ge", 0, 1))):
                        i = mm(PS[:, 4, 32 * k:32 * k + 32], cc(m), dtt[:, 2 + c, 32 * dr:32 * dr + 32], start=True, stop=True)
                    i.then_inc(*done("cums"))
            for g in range(SG):
                ssd(g)
            pe.wait_ge(*at("s_add", SG - 1))
            ssd_turn(SG - 1)
            for j in (6, 7):
                ssd_out(j)
            norm_T(3)
            ffn(1)

            norm_T(4)
            block_tm("qa", 4, ("n", 4))
            block_tm("ka", 2)

            def head_T(nm, a):
                pe.wait_ge(*read((nm, 1)))
                if a >= 2:
                    pe.wait_ge(*at("hT", (a - 2, 1)))
                to_T(nm, hn[:, :, 512 * (a % 2):512 * (a % 2) + 512], 4, 4 + 2 * (a % 2))

            pe.wait_ge(*read(("qa", 1)))
            block_tm("va", 0)
            head_T("qa", 0)
            head_T("ka", 1)
            block_tm("qb", 2)
            pe.wait_ge(*read(("va", 1)))
            slot_fm(("kc", 0), 0)
            slot_fm(("vc", 0), 1)
            head_T("qb", 2)
            block_tm("ksv", 2)
            pe.wait_ge(*read(("kc", 0)))
            pe.wait_ge(*read(("vc", 0)))
            block_tm("za", 0)
            head_T("ksv", 3)
            block_tm("zb", 2)
            pe.wait_ge(*read(("za", 1)))
            slot_tm(("gb", 0), 0, 0, True, True, 24, 8)
            pe.wait_ge(*at("hT", (3, 1)))

            def cmp_hidden(a, j):
                if (a, j) == (0, 0):
                    pe.wait_ge(*read(("gb", 1)))
                    pe.wait_ge(*read(("zb", 1)))
                pe.wait_ge(*at("x_lo", a))
                n = slot_no[("w1" + "kv"[a], j)]
                pe.wait_ge(*low(n))
                h, l = whi[n % NHI], wlo[n % NLO]
                for k in range(8):
                    kk = 8 * j + k
                    xh = Th[:, 8 + 2 * a:10 + 2 * a, :].rearrange("p a (b c) -> p (a b) c", c=32)[:, kk, :]
                    xl = Tl[:, 8 + 2 * a:10 + 2 * a, :].rearrange("p a (b c) -> p (a b) c", c=32)[:, kk, :]
                    i = three(PS[0:32, a, 0:256], h[:, k * 256:(k + 1) * 256], l[:, k * 256:(k + 1) * 256], xh, xl,
                              kk == 0, kk == 15, True)
                i.then_inc(*done("w_used", n))

            def cmp_hidden_T(a):
                pe.wait_ge(*at("c_gelu", a))
                for m in range(2):
                    i = tr(PS[:, 2 + a, 32 * m:32 * m + 32], hidt[0:32, a, m * P:(m + 1) * P], ident[0:32, 0:32])
                i.then_inc(*done("c_ht", a))

            def cmp_keys():
                pe.wait_ge(*at("c_hid"))
                pe.wait_ge(*at("load_w2"))
                for m in range(2):
                    i = mm(PS[0:32, 0, 0:DH], hid[:, m, :], w2c[:, 0, m, :], start=m == 0, stop=m == 1)
                i.then_inc(*done("c_k"))

            def cmp_values():
                pe.wait_ge(*at("c_rep"))
                for m in range(2):
                    i = mm(PS[:, 3, 0:DH], hidr[:, m, :], w2c[:, 1, m, :], start=m == 0, stop=m == 1)
                i.then_inc(*done("c_v"))

            def cmp_keys_T():
                pe.wait_ge(*at("c_kn"))
                tr(PS[:, 2, 0:32], kcm[0:32, 0, :], ident[0:32, 0:32]).then_inc(*done("c_kt"))

            def cmp_scores():
                pe.wait_ge(*at("c_kte"))
                for t in range(NT):
                    for h in range(NH):
                        b = (h % 2) * DH
                        a = 64 * t + 16 * (h // 2)
                        i = mm(PS[:, h % 2, a:a + 16], qbT[b:b + DH, h // 2, t * P:(t + 1) * P],
                               kcT[b:b + DH, 16 * (h // 4):16 * (h // 4) + 16], start=True, stop=True)
                i.then_inc(*done("c_s"))

            def cmp_turn():
                pe.wait_ge(*at("c_p"))
                for t in range(NT):
                    i = tr(PS[:, 2, t * P:(t + 1) * P], cpr[:, t, :], ident)
                i.then_inc(*done("c_pt"))

            def cmp_out():
                pe.wait_ge(*at("c_pte"))
                pe.wait_ge(*at("c_vbd"))
                for t in range(NT):
                    i = mm(PS[:, 2 + t, :], cpt[:, t, :], vbd[:, :, :], start=True, stop=True)
                i.then_inc(*done("c_o"))

            def gate(nm, n, hf):
                if hf == 0:
                    pe.wait_ge(*(read(((nm, 0), 1)) if n else at(*{"GA": ("c_sub",), "GB": ("c_om",)}[nm])))
                slot_tm(((nm, n), hf), 0 if nm == "GA" else 2, 4 * hf, hf == 0, hf == 1)

            def turn_a():
                pe.wait_ge(*read((("GA", 1), 1)))
                pe.wait_ge(*at("y2a"))
                to_T("y2a", hn, 4, 0)

            def branch_a(n):
                pe.wait_ge(*(read((("GB", 1), 1)) if n else at("T_lo", ("y2a", 3))))
                slot_tm((("YA", n), 0), 2 * n, 8, True, True, fresh="y2a", f0=0)

            moba_also = {0: (lambda: cmp_hidden(0, 0), lambda: cmp_hidden(0, 1)), 1: (lambda: cmp_hidden(1, 0),),
                         2: (lambda: cmp_hidden_T(0),), 3: (lambda: cmp_hidden(1, 1),), 4: (cmp_keys,),
                         5: (lambda: cmp_hidden_T(1),), 7: (cmp_keys_T, cmp_values), 9: (cmp_scores,)}
            nsa_also = {1: (lambda: gate("GA", 0, 0),), 2: (lambda: gate("GA", 0, 1),), 3: (cmp_turn,),
                        4: (lambda: gate("GA", 1, 0),), 5: (lambda: gate("GA", 1, 1), cmp_out),
                        7: (lambda: gate("GB", 0, 0),), 8: (lambda: gate("GB", 0, 1),), 9: (turn_a,),
                        10: (lambda: gate("GB", 1, 0),), 11: (lambda: gate("GB", 1, 1),),
                        15: (lambda: branch_a(0),), 17: (lambda: branch_a(1),)}

            pe.wait_ge(*read(("va", 1)))
            attention("moba", [operands(h, qaT, kaT, h // 2, lambda c, h=h: va[:, c, h * DH:(h + 1) * DH], True)
                               for h in range(NH)], also(moba_also))
            pe.wait_ge(*at("a_o", ("moba", NH - 1)))
            attention("nsa", [operands(h, qbT, kswT, 2 * w + h // 4,
                                       lambda c, h=h, w=w: vsw[:, c, w, DH * (h // 4):DH * (h // 4) + DH], True)
                              for w in range(2) for h in range(NH)], also(nsa_also))
            pe.wait_ge(*at("y2b"))
            to_T("y2b", hn[:, :, 512:D], 4, 4)
            slot_tm((("YB", 0), 0), 6, 12, True, True, fresh="y2b", f0=0)
            pe.wait_ge(*at("ya", 0))
            slot_tm((("YB", 1), 0), 0, 12, True, True)
            pe.wait_ge(*at("mrg", 0))
            to_T("mrg0", sg[("GA", 0)], 4, 4)
            pe.wait_ge(*at("mrg", 1))
            to_T("mrg1", sg[("GA", 1)], 4, 6)
            for j in range(4):
                out_slot("fo", j, 4, 2 * j, (("mrg0", "mrg1")[j // 2], 2 * (j % 2) + 1))

        @block.scalar
        def _(act):
            nxt = [0]

            def high(upto):
                while nxt[0] <= min(upto, NS - 1):
                    n = nxt[0]
                    parts, width = slots[n]
                    act.wait_ge(*at(f"w_raw{n % NRAW}", n))
                    if n >= NHI:
                        act.wait_ge(*at("w_used", n - NHI))
                    act.activation(whi[n % NHI][:, 0:width], raw[n % NRAW][:, 0:width], ACT.Copy)\
                        .then_inc(*done("w_hi", n))
                    nxt[0] += 1

            def used(name, ahead=True):
                n = slot_no[name]
                high(n + 2)
                act.wait_ge(*at("w_used", n))
                if ahead:
                    high(n + 3)

            def sqrt_of(key, o, i, width):
                act.activation(o, i, ACT.Sqrt, scale=1.0 / width, bias=eps[0:o.shape[0], 0:1]).then_inc(*done("root", key))

            def T_hi(name, nk, kt0, b0, gains):
                for k in range(nk):
                    if k % 2 == 0:
                        act.wait_ge(*at("turned", (name, k + 1)))
                    src = PS[:, b0 + k // 2, (k % 2) * S:(k % 2 + 1) * S]
                    g = gains(k)
                    act.activation(Th[:, kt0 + k, :], src, ACT.Identity, scale=1.0 if g is None else g)\
                        .then_inc(*done("T_hi", (name, k)))

            def norm(l, gain):
                for t in range(NT):
                    if l:
                        act.wait_ge(*at("x", (l - 1, t)))
                    else:
                        act.wait_ge(*at("eps"))
                        act.wait_ge(*at(f"load_x{t}"))
                    act.activation(hn[:, t, :], x[:, t, :], ACT.Square, accum_out=st[:, t:t + 1]).then_inc(*done("n_ss", (l, t)))
                    act.wait_ge(*at("n_ss", (l, t)))
                    sqrt_of(("n", l, t), st[:, 2 + t:3 + t], st[:, t:t + 1], D)
                    if l == 0 and t == 1:
                        high(0)
                    if l and t == 0:
                        high(nxt[0])
                if l == 0:
                    act.wait_ge(*at("mix0_T"))
                    act.activation(cols[:, col_at["mix0"]:col_at["mix0"] + 8], PS[:, 0, 0:8], ACT.Copy)\
                        .then_inc(*done("mix0_col"))
                    act.wait_ge(*at("mix0_col"))
                T_hi(("n", l), KD, 0, norm_bank(l), lambda k: col(gain, k))

            def post(l, last, b0=4):
                n = slot_no[last]
                act.activation(st[:, 157:158], eps[:, 0:1], ACT.Sqrt)
                high(n + 2)
                for t in range(NT):
                    for hf in range(2):
                        act.wait_ge(*(at("w_used", n) if (t, hf) == (1, 1) else at("sum", (n, t, hf))))
                        b = b0 + 2 * t + hf
                        if (t, hf) != (0, 0):
                            act.wait_ge(*at("p_ss", (l, (0, 0, 1)[2 * t + hf - 1], (0, 1, 0)[2 * t + hf - 1])))
                        c = 4 + 2 * t + hf
                        act.activation(sqj[:, :], PS[:, b, :], ACT.Square, accum_out=st[:, c:c + 1])\
                            .then_inc(*done("p_ss", (l, t, hf)))
                    act.wait_ge(*at("p_sum", (l, t)))
                    sqrt_of(("p", l, t), st[:, 10 + t:11 + t], st[:, 8 + t:9 + t], D)

            def load_gpost(l):
                src = (I["norm_mix_post"], I["norm_ffn_post"])[l % 2][l // 2:l // 2 + 1, :]
                act.dma_start(gpost[:, :], src.to_broadcast([P, D])).then_inc(*done("load_gpost", l, 16))

            def ffn(l):
                for i in range(FI + 1):
                    if i < FI:
                        for q in range(4):
                            if q % 2 == 0:
                                used(("GV"[q // 2], l, i))
                            if q == 0 and i >= 2:
                                act.wait_ge(*at("f_prod", (l, i - 2)))
                            j = (0, 1, 22, 23)[q] + 2 * i
                            act.activation(fac[i % 2][:, q, :],
                                           PS[:, 2 * (i % 2) + q // 2, (q % 2) * S:(q % 2 + 1) * S], ACT.Identity,
                                           scale=col(f"fw{l}1", j), bias=col(f"fb{l}", j)).then_inc(*done("f_ctr", (l, i, q)))
                        act.wait_ge(*at("f_cg", (l, i)))
                        act.activation(fac[i % 2][:, 0:2, :], fac[i % 2][:, 0:2, :], ACT.Gelu_apprx_tanh)\
                            .then_inc(*done("f_gelu", (l, i)))
                        if i >= 2:
                            act.wait_ge(*at("w_used", slot_no[("D", l, i - 2)]))
                        act.wait_ge(*at("f_prod", (l, i)))
                        act.activation(aTh[:, i % 2, :, :], fpr[i % 2][:, :, :], ACT.Copy).then_inc(*done("f_ahi", (l, i)))
                        high(slot_no[("V", l, i)] + 3)

            act.dma_start(cst[:, 0:P], I["const_table"][:, 0:P]).then_inc(*done("load_ident", 0, 16))
            act.dma_start(rowm, I["norm_mix_pre"][0].rearrange("(k p) -> k p", p=P)).then_inc(*done("load_mix0", 0, 16))
            def set_up():
                act.wait_ge(*at("set_up"))
                for b in range((NR + 3) // 4):
                    n = min(4, NR - 4 * b) * P
                    i = act.activation(cols[:, 512 * b:512 * b + n], PS[:, 4 + b, 0:n], ACT.Copy)
                i.then_inc(*done("cols_act"))
                act.wait_ge(*at("t5_sum"))
                act.dma_start(toe, bc(t5r, 1, P)).then_inc(*done("t5_out", 0, 16))
                act.dma_start(pfb[:, :, :], I["const_pfb"].rearrange("p (a b) -> p a b", a=2)).then_inc(*done("load_pfb", 0, 16))

            def softplus(key, neg, n):
                spx = spxs[key]
                act.wait_ge(*at("sp_x", key))
                act.activation(spx[:, 1, 0:n], spx[:, 0, 0:n], ACT.Abs).then_inc(*done("sp_abs", key))
                act.wait_ge(*at("sp_abs", key))
                act.activation(spx[:, 2, 0:n], spx[:, 1, 0:n], ACT.Exp, scale=-1.0).then_inc(*done("sp_exp", key))
                act.wait_ge(*at("sp_u", key))
                act.activation(spx[:, 4, 0:n], spx[:, 3, 0:n], ACT.Ln).then_inc(*done("sp_ln", key))

            norm(0, "mix0")
            high(3)
            load_gpost(0)
            high(slot_no[("rk", 0)] + 1)
            set_up()
            softplus("ret", True, 16)

            def copy_block(nm, dst, b0, scale=1.0, func=ACT.Copy):
                for t in range(NT):
                    i = act.activation(dst[:, t, :], PS[:, b0 + t, :], func, scale=scale)
                    i.then_inc(*done("read_a", (nm, t)))

            def copy_fm(nm, j, dst, b0, scale=1.0):
                used((nm, j))
                act.activation(dst[:, 2 * j:2 * j + 2, :], PS[:, b0 + j, :].rearrange("p (a b) -> p a b", a=2),
                               ACT.Copy, scale=scale).then_inc(*done("read_a", (nm, j)))

            used(("rk", 1))
            high(slot_no[("rv", 0)] + 2)
            used(("rv", 1))
            copy_block("rv", rv, 0)
            for a, nm in enumerate(("rq", "rk")):
                for j in range(2):
                    act.wait_ge(*at("turned", (nm, 2 * j + 1)))
                    act.activation((rqT, rkT)[a][:, 2 * j:2 * j + 2, :],
                                   PS[:, 4 + 2 * a + j, :].rearrange("p (a b) -> p a b", a=2),
                                   ACT.Copy, scale=(1.0, DH ** -0.5)[a]).then_inc(*done("rT", (nm, j)))
            for h in range(NH):
                act.wait_ge(*at("r_arg", h))
                act.activation(dcy[h % 2], dcy[h % 2], ACT.Exp).then_inc(*done("r_d", h))
                if h == 1:
                    act.wait_ge(*at("t5_out"))
                if h in (2, 3):
                    copy_fm("nq", h - 2, nqT, 2, DH ** -0.5)
                if h in (4, 5):
                    copy_fm("nk", h - 4, nkT, 0)
            used(("nv", 0))
            used(("nv", 1))
            copy_block("nv", nv, 2)
            for t in range(NT):
                act.wait_ge(*at("gn_c", t))
                act.activation(gsq[:, t, :], hn[:, t, 0:512], ACT.Square).then_inc(*done("gn_sq", t))

            def ret_gate():
                act.wait_ge(*at("gn_ss"))
                sqrt_of("gn", st[:, 48:64], st[:, 32:48], DH)
                copy_block("rg", rg, 0, scale=0.5, func=ACT.Tanh)

            used(("rg", 1))

            def attention(tag, n, causal, after=lambda i: None):
                for i in range(n + 1):
                    if i < n:
                        act.wait_ge(*at("a_nm", (tag, i)))
                        for t in range(NT):
                            nk = P if causal and t == 0 else S
                            e = act.activation(sc[i % 2][:, t, 0:nk], sc[i % 2][:, t, 0:nk], ACT.Exp,
                                               bias=st[:, 72 + 2 * (i % 4) + t:73 + 2 * (i % 4) + t],
                                               accum_out=st[:, 80 + 2 * (i % 4) + t:81 + 2 * (i % 4) + t])
                        e.then_inc(*done("a_exp", (tag, i)))
                    if i >= 1:
                        j = i - 1
                        act.wait_ge(*at("a_t", (tag, j)))
                        if j >= 2:
                            act.wait_ge(*at("a_v", (tag, j - 2)))
                        if causal:
                            act.activation(pt[j % 2][:, 0, :], PS[:, 6, 0:P], ACT.Copy)
                            e = act.activation(pt[j % 2][:, 2:4, :], PS[:, 6, S:2 * S].rearrange("p (a b) -> p a b", a=2), ACT.Copy)
                        else:
                            e = act.activation(pt[j % 2][:, :, :], PS[:, 6, :].rearrange("p (a b) -> p a b", a=4), ACT.Copy)
                        e.then_inc(*done("a_pt", (tag, j)))
                    after(i)

            def later(name):
                return lambda: high(slot_no[name] + 3)

            high(slot_no[("rg", 1)] + 3)
            attention("na", NH, False, also({0: (ret_gate,), 3: (lambda: T_hi("y0a", 4, 8, 0, lambda k: col("gn", k)),), 5: (later(("mo0", 0)),),
                                             8: (later(("mo0", 1)),)}))
            T_hi("y0b", 4, 12, 4, lambda k: None)
            post(0, ("mo0", 3), 0)
            norm(1, "ffn0")
            load_gpost(1)
            ffn(0)
            post(1, ("D", 0, FI - 1))
            norm(2, "mix1")
            load_gpost(2)
            for r, (nm, w) in enumerate((("c_dt_bias", 64), ("c_a_log", 64))):
                act.dma_start(dtt[:, 4 + r, 0:w], I[nm].rearrange("a b c -> a (b c)").to_broadcast([P, w]))\
                    .then_inc(*done("load_ssd", 0, 16))
            act.dma_start(dtt[:, 6, 0:32], I["c_d_skip"].to_broadcast([P, 32])).then_inc(*done("load_ssd", 0, 16))
            def ssd_centre(g, j):
                used(((("xs", g), j) if j < 2 else (("bc", g), 0)))
                for m in range(2):
                    ch = 4 * g + 2 * j + m if j < 2 else 16 + 4 * m + g
                    act.activation(cvb[:, 2 * j + m, :], PS[:, xbc_bank(g, j), m * S:(m + 1) * S], ACT.Identity,
                                   scale=col("cw2", ch), bias=col("cb", ch)).then_inc(*done("c_ctr", (g, 2 * j + m)))

            def ssd_silu(g):
                for j in (2, 0, 1):
                    act.wait_ge(*at("c_cnv", (g, j)))
                    act.activation(cvb[:, 2 * j:2 * j + 2, :] if j < 2 else bct[g % 2][:, :, :], cvb[:, 2 * j:2 * j + 2, :],
                                   ACT.Silu).then_inc(*done("cv", (g, j)))

            def ssd(g):
                more = g + 1 < SG
                b = slot_no[(("bc", g + 1), 0)] if more else slot_no[("mo1", 0)]
                def z_gate():
                    used((("z", g), 1))
                    if g >= 2:
                        act.wait_ge(*at("s_ss", g - 2))
                    copy_block(("z", g), zt[g % 2], 0, func=ACT.Silu)

                if not more:
                    z_gate()
                act.wait_ge(*at("s_xt", g))
                for t in range(NT):
                    i = act.activation(xs[g % 2][:, t, :], PS[:, 4 + t, :], ACT.Copy)
                i.then_inc(*done("s_xs", g))
                if more:
                    z_gate()
                high(b + 1)
                if g:
                    act.wait_ge(*at("s_ss", g - 1))
                    sqrt_of(("s", g - 1), st[:, 98:100], st[:, 96:98], 512)
                act.wait_ge(*at("s_st", g))
                for r in range(2):
                    i = act.activation(stt[:, r, :], PS[:, 4 + r, :], ACT.Copy)
                i.then_inc(*done("s_ste", g))
                high(b + 2)
                if more:
                    ssd_centre(g + 1, 2)
                high(b + 3)
                if g:
                    T_hi(("y", g - 1), 4, (4 + 4 * g) % 16, 6, lambda k: col("ssdn", 4 * g - 4 + k))
                if more:
                    ssd_centre(g + 1, 0)
                high(b + 4)
                for u in range(8):
                    act.wait_ge(*at("s_l", (g, u)))
                    if u >= 2:
                        act.wait_ge(*at("s_pv", (g, u - 2)))
                    act.activation(ee[u % 2][:, :, :], PS[:, 4 + u % 2, :].rearrange("p (a b) -> p a b", a=4), ACT.Exp)\
                        .then_inc(*done("s_e", (g, u)))
                    if u == 1:
                        if more:
                            ssd_centre(g + 1, 1)
                        high(b + 5)
                    if u == 5:
                        high(b + 6)
                if more:
                    ssd_silu(g + 1)

            for j in (2, 0, 1):
                ssd_centre(0, j)
                if j == 0:
                    softplus("ssd", False, 128)
                    act.wait_ge(*at("load_ssd"))
                    act.activation(dtt[:, 5, :], dtt[:, 5, :], ACT.Exp).then_inc(*done("ssd_a"))
            act.wait_ge(*at("cums"))
            act.activation(dtt[:, 8:10, :], PS[:, 4, 0:128].rearrange("p (a b) -> p a b", a=2), ACT.Exp).then_inc(*done("ex"))
            ssd_silu(0)
            for g in range(SG):
                ssd(g)
            high(slot_no[("mo1", 7)])
            act.wait_ge(*at("s_ss", SG - 1))
            sqrt_of(("s", SG - 1), st[:, 98:100], st[:, 96:98], 512)
            T_hi(("y", SG - 1), 4, (4 + 4 * SG) % 16, 6, lambda k: col("ssdn", 4 * SG - 4 + k))
            post(2, ("mo1", 7), 0)
            norm(3, "ffn1")
            load_gpost(3)
            ffn(1)
            post(3, ("D", 1, FI - 1))
            norm(4, "sec")

            def load_tb(k, heads):
                src = bass.AP(toe.tensor, (NH * k + heads[0]) * P * 384 + 127, [[383, P], [P * 384, len(heads)], [1, S]])
                act.dma_start(tb[:, heads[0]:heads[-1] + 1, :], src).then_inc(*done(f"load_tb{k}_{heads[0]}", 0, 16))

            load_tb(0, range(NH))
            for a, nm in enumerate("kv"):
                act.dma_start(w2c[:, a, :, :], I["cmp_w2_" + nm + "_2"][0].rearrange("(m p) d -> p m d", p=P))\
                    .then_inc(*done("load_w2", 0, 16))

            def head_norm(nm, b0):
                used((nm, 1))
                for t in range(NT):
                    if t == 0 and nm != "qa":
                        act.wait_ge(*at("q_ss", {"ka": "qa", "qb": "ka", "ksv": "qb"}[nm]))
                    act.activation(sqb[:, t, :], PS[:, b0 + t, :], ACT.Square).then_inc(*done("q_sq", (nm, t)))
                if nm == "ksv":
                    for t in range(NT):
                        v = PS[:, b0 + t, :].rearrange("p (w c d) -> p w c d", w=2, c=2)[:, :, 1, :]
                        act.activation(vsw[:, t, :, :], v, ACT.Copy).then_inc(*done("vsw", t))
                act.wait_ge(*at("q_ss", nm))
                sqrt_of(("q", nm), st[:, 120:136], st[:, 104:120], DH)

            def head_T(nm, a, dst, gains):
                for j in range(2):
                    act.wait_ge(*at("turned", (nm, 2 * j + 1)))
                    act.activation(dst[:, 2 * j:2 * j + 2, :], PS[:, 4 + 2 * (a % 2) + j, :].rearrange("p (a b) -> p a b", a=2),
                                   ACT.Identity, scale=cols[:, gains[j]:gains[j] + 1]).then_inc(*done("hT", (a, j)))

            head_norm("qa", 4)
            head_norm("ka", 2)
            used(("va", 1))
            copy_block("va", va, 0)
            head_T("qa", 0, qaT, (qn + 6, qn + 6))
            head_T("ka", 1, kaT, (qn + 1, qn + 1))
            head_norm("qb", 2)
            used(("vc", 0))
            head_T("qb", 2, qbT, (qn + 7, qn + 7))
            for a in range(2):
                act.wait_ge(*read((("kc", "vc")[a], 0)))
                act.activation(Th[:, 8 + 2 * a:10 + 2 * a, :].rearrange("p a (b c) -> p (a b) c", c=32), XC[a][:, :, :],
                               ACT.Copy).then_inc(*done("x_hi", a))
            head_norm("ksv", 2)
            used(("za", 1))
            copy_block("za", za, 0, func=ACT.Silu)
            head_T("ksv", 3, kswT, (qn + 3, qn + 4))
            used(("zb", 1))
            copy_block("zb", zb, 2, func=ACT.Silu)
            used(("gb", 0))
            for t in range(NT):
                act.activation(gb[:, t, :], PS[:, t, 0:24], ACT.Sigmoid).then_inc(*done("read_a", ("gb", t)))

            def cmp_gelu(a):
                used(("w1" + "kv"[a], 1), False)
                act.activation(hidt[0:32, a, :], PS[0:32, a, 0:256], ACT.Gelu_apprx_tanh).then_inc(*done("c_gelu", a))

            def cmp_norm():
                act.wait_ge(*at("c_k"))
                act.activation(kcm[0:32, 1, 0:DH], PS[0:32, 0, 0:DH], ACT.Square, accum_out=st[0:32, 12:13])\
                    .then_inc(*done("c_kss"))
                act.wait_ge(*at("c_kss"))
                sqrt_of("ck", st[0:32, 13:14], st[0:32, 12:13], DH)

            def cmp_keys():
                act.wait_ge(*at("c_kt"))
                act.activation(kcT, PS[:, 2, 0:32], ACT.Identity, scale=cols[:, qn + 5:qn + 6]).then_inc(*done("c_kte"))

            def cmp_exp():
                act.wait_ge(*at("c_sub"))
                act.activation(cpr[:, :, :], cpr[:, :, :], ACT.Exp).then_inc(*done("c_exp"))

            def cmp_turned():
                act.wait_ge(*at("c_pt"))
                act.activation(cpt[:, :, :], PS[:, 2, 0:S].rearrange("p (a b) -> p a b", a=2), ACT.Copy).then_inc(*done("c_pte"))

            def gates(nm, n):
                used(((nm, n), 1), False)
                if (nm, n) == ("GB", 1):
                    act.wait_ge(*at("c_add"))
                copy_block((nm, n), sg[(nm, n)], 0 if nm == "GA" else 2, scale=0.5, func=ACT.Tanh)

            def next_tb(h):
                act.wait_ge(*at("a_sc", ("moba", h + 3)))
                load_tb(1, range(h, h + 4))

            high(slot_no[("gb", 0)] + 3)
            attention("moba", NH, True, also({
                1: (lambda: cmp_gelu(0), later(("w1k", 1))), 2: (later(("w1v", 0)),),
                4: (lambda: cmp_gelu(1), lambda: next_tb(0)), 5: (cmp_norm,), 8: (cmp_keys,)}))
            next_tb(4)
            attention("nsa", 2 * NH, True, also({
                1: (cmp_exp,), 2: (later((("GA", 0), 0)),), 3: (lambda: gates("GA", 0),), 4: (cmp_turned,),
                5: (later((("GA", 1), 0)),), 6: (lambda: gates("GA", 1),), 8: (later((("GB", 0), 0)),),
                9: (lambda: gates("GB", 0),), 10: (lambda: T_hi("y2a", 4, 8, 0, lambda k: None),),
                11: (later((("GB", 1), 0)),), 12: (lambda: gates("GB", 1),), 16: (later((("YA", 0), 0)),)}))
            T_hi("y2b", 4, 12, 4, lambda k: None)
            high(slot_no[(("YB", 0), 0)] + 3)
            T_hi("mrg0", 4, 0, 4, lambda k: None)
            T_hi("mrg1", 4, 4, 6, lambda k: None)
            used(("fo", 3))

        @block.vector
        def _(dve):
            tt, ts, stt3 = nc.vector.tensor_tensor, nc.vector.tensor_scalar, nc.vector.scalar_tensor_tensor
            lk = lambda ins: link(dve, "dve", ins)

            def T_lo(name, nk, kt0, b0, gains):
                for k in range(nk):
                    if k % 2 == 0:
                        dve.wait_ge(*at("T_hi", (name, k + 1)))
                    src = PS[:, b0 + k // 2, (k % 2) * S:(k % 2 + 1) * S]
                    g = gains(k)
                    stt3(out=Tl[:, kt0 + k, :], in0=src, scalar=1.0 if g is None else g,
                         in1=Th[:, kt0 + k, :].bitcast(F32), op0=ALU.mult, op1=ALU.subtract)\
                        .then_inc(*done("T_lo", (name, k)))

            def weights_low(n):
                dve.wait_ge(*at("w_hi", n))
                if n >= NLO:
                    dve.wait_ge(*at("w_used", n - NLO))
                tt(wlo[n % NLO][:, :], raw[n % NRAW][:, :], whi[n % NHI][:, :].bitcast(F32), ALU.subtract)\
                    .then_inc(*done("w_lo_v", n))

            def norm(l, gain):
                for t in range(NT):
                    dve.wait_ge(*at("root", ("n", l, t)))
                    lk(nc.vector.reciprocal(st[:, t:t + 1], st[:, 2 + t:3 + t]))
                    ts(hn[:, t, :], x[:, t, :], st[:, t:t + 1], None, ALU.mult).then_inc(*done("n_hn", (l, t)))
                if l == 0:
                    weights_low(0)
                T_lo(("n", l), KD, 0, norm_bank(l), lambda k: col(gain, k))

            def post(l, last, b0=4):
                dve.wait_ge(*at("load_gpost", l))
                for t in range(NT):
                    b, c, m = b0 + 2 * t, 4 + 2 * t, hn[:, t, :]
                    dve.wait_ge(*at("p_ss", (l, t, 0)))
                    tt(m[:, 0:512], PS[:, b, :], gpost[:, 0:512], ALU.mult)
                    dve.wait_ge(*at("p_ss", (l, t, 1)))
                    tt(st[:, 8 + t:9 + t], st[:, c:c + 1], st[:, c + 1:c + 2], ALU.add).then_inc(*done("p_sum", (l, t)))
                    lk(tt(m[:, 512:D], PS[:, b + 1, :], gpost[:, 512:D], ALU.mult))
                    dve.wait_ge(*at("root", ("p", l, t)))
                    lk(nc.vector.reciprocal(st[:, 14 + t:15 + t], st[:, 10 + t:11 + t]))
                    stt3(out=x[:, t, :], in0=m, scalar=st[:, 14 + t:15 + t], in1=x[:, t, :], op0=ALU.mult, op1=ALU.add)\
                        .then_inc(*done("x", (l, t)))

            def taps(dst, src, ws, shift):
                n = S - abs(shift)
                a, b = (-shift, 0) if shift < 0 else (0, shift)
                return stt3(out=dst[:, a:a + n], in0=src[:, b:b + n], scalar=ws, in1=dst[:, a:a + n], op0=ALU.mult, op1=ALU.add)

            def ffn(l):
                for i in range(FI):
                    p = i % 2
                    bank = lambda q: PS[:, 2 * p + q // 2, (q % 2) * S:(q % 2 + 1) * S]
                    j = lambda q: (0, 1, 22, 23)[q] + 2 * i
                    for hv in range(2):
                        dve.wait_ge(*at("f_ctr", (l, i, 2 * hv + 1)))
                        for q in (2 * hv, 2 * hv + 1):
                            o = taps(fac[p][:, q, :], bank(q), col(f"fw{l}0", j(q)), -1)
                        lk(o)
                        for q in (2 * hv, 2 * hv + 1):
                            o = taps(fac[p][:, q, :], bank(q), col(f"fw{l}2", j(q)), 1)
                        o.then_inc(*done(("f_cg", "f_conv")[hv], (l, i)))
                    dve.wait_ge(*at("f_gelu", (l, i)))
                    dve.wait_ge(*at("f_conv", (l, i)))
                    if i >= 2:
                        dve.wait_ge(*at("f_ahi", (l, i - 2)))
                    tt(fpr[p][:, :, :], fac[p][:, 0:2, :], fac[p][:, 2:4, :], ALU.mult).then_inc(*done("f_prod", (l, i)))
                    dve.wait_ge(*at("f_ahi", (l, i)))
                    if i >= 2:
                        dve.wait_ge(*at("w_used", slot_no[("D", l, i - 2)]))
                    tt(aTl[:, p, :, :], fpr[p][:, :, :], aTh[:, p, :, :].bitcast(F32), ALU.subtract).then_inc(*done("f_alo", (l, i)))
                    if i < FI - 3:
                        weights_low(slot_no[("D", l, i)])
                    elif i == FI - 2:
                        weights_low(slot_no[("D", l, FI - 3)])

            def softplus(key, n, dst):
                w = lambda k: spxs[key][:, k, 0:n]
                dve.wait_ge(*at("sp_exp", key))
                ts(w(3), w(2), 1.0, None, ALU.add).then_inc(*done("sp_u", key))
                dve.wait_ge(*at("sp_u", key))
                lk(ts(w(5), w(3), -1.0, None, ALU.add))
                lk(ts(w(6), w(5), 0.0, None, ALU.is_equal))
                lk(tt(w(5), w(5), w(6), ALU.add))
                lk(nc.vector.reciprocal(w(7), w(5)))
                dve.wait_ge(*at("sp_ln", key))
                lk(tt(w(7), w(7), w(4), ALU.mult))
                lk(tt(w(7), w(7), w(6), ALU.add))
                lk(tt(w(7), w(7), w(2), ALU.mult))
                lk(stt3(out=dst, in0=w(0), scalar=0.0, in1=w(7), op0=ALU.max, op1=ALU.add))

            nc.vector.memset(st[:, :], 0.0)
            nc.vector.memset(eps[:, :], EPS).then_inc(*done("eps"))
            nc.vector.memset(rowb[:, :, :], 0.0).then_inc(*done("rows_clear"))
            dve.wait_ge(*at("eps"))
            for t in range(NT):
                dve.wait_ge(*at(f"load_x{t}"))
            norm(0, "mix0")
            dve.wait_ge(*at("set_up"))
            lk(nc.vector.tensor_copy(cols[:, qn:qn + 6], PS[:, 6, 0:6]))
            tt(t5r, PS[0:16, 7, 0:384], negs, ALU.add).then_inc(*done("t5_sum"))
            ts(cols[:, qn + 6:qn + 8], cols[:, qn:qn + 3:2], DH ** -0.5, None, ALU.mult).then_inc(*done("cols"))
            dve.wait_ge(*at("load_dl"))
            ts(spxs["ret"][:, 0, 0:16], brow, -1.0, None, ALU.mult).then_inc(*done("sp_x", "ret"))
            dve.wait_ge(*at("sp_x", "ret"))
            softplus("ret", 16, lg)
            lk(ts(lg, lg, -1.0, None, ALU.mult))

            def rope(nm, a, b0):
                dve.wait_ge(*at("w_used", slot_no[(nm, 1)]))
                for t in range(NT):
                    src = PS[:, b0 + t, :]
                    o, tmp = rqk[a][:, t, :], hn[:, t, 512 * a:512 * a + 512]
                    h3 = lambda v: v.rearrange("p (h d) -> p h d", h=NH)
                    cosb = bc(cc("cos")[:, DH * t:DH * (t + 1)], 1, NH)
                    tt(h3(o), h3(src), cosb, ALU.mult)
                    for hf in range(2):
                        sn = bc(cc("sin")[:, DH * t + 32 * hf:DH * t + 32 * hf + 32], 1, NH)
                        i = tt(h3(tmp)[:, :, 32 * hf:32 * hf + 32], h3(src)[:, :, 32 * (1 - hf):32 * (1 - hf) + 32], sn, ALU.mult)
                    i.then_inc(*done("read_v", (nm, t)))
                    dve.wait_ge(*read((nm, t)))
                    tt(o, o, tmp, ALU.add).then_inc(*done("rope", (nm, t)))

            dve.wait_ge(*at("load_cst"))
            rope("rq", 0, 0)
            rope("rk", 1, 2)
            dve.wait_ge(*at("load_pfb"))

            def decay(h):
                if h >= 2:
                    dve.wait_ge(*at("r_m", h - 2))
                lk(ts(dcy[h % 2], pfb[:, 1, :], lg[:, 8 + h:9 + h], None, ALU.mult))
                stt3(out=dcy[h % 2], in0=pfb[:, 0, :], scalar=lg[:, h:h + 1], in1=dcy[h % 2], op0=ALU.mult, op1=ALU.add)\
                    .then_inc(*done("r_arg", h))

            decay(0)
            decay(1)
            for h in range(NH):
                dve.wait_ge(*at("r_s", h))
                dve.wait_ge(*at("r_d", h))
                if h >= 2:
                    dve.wait_ge(*at("r_pv", h - 2))
                tt(msc[h % 2], PS[:, 4 + h % 2, :], dcy[h % 2], ALU.mult).then_inc(*done("r_m", h))
                if h + 2 < NH:
                    decay(h + 2)
                if h == 4:
                    dve.wait_ge(*at("load_na"))
                if h >= 4:
                    for k in (2 * h - 8, 2 * h - 7):
                        v = nabias[:, k, :].rearrange("p (a b) -> p a b", a=6)
                        i = tt(v, v, bc(cc("nm"), 1, 6), ALU.add)
            lk(i)
            dve.wait_ge(*at("r_pv", NH - 1))
            h3 = lambda v: v.rearrange("p (h d) -> p h d", h=NH)
            for t in range(NT):
                i = nc.vector.tensor_reduce(st[:, 16 + 8 * t:24 + 8 * t], h3(PS[:, 6 + t, :]), AXX, ALU.add)
            lk(i)
            for t in range(NT):
                stt3(out=h3(hn[:, t, 0:512]), in0=bc(st[:, 16 + 8 * t:24 + 8 * t], 2, DH), scalar=-1.0 / DH,
                     in1=h3(PS[:, 6 + t, :]), op0=ALU.mult, op1=ALU.add).then_inc(*done("gn_c", t))
            def attention(tag, n, bias, causal, write, after=lambda i: None):
                def finish(j):
                    dve.wait_ge(*at("a_v", (tag, j)))
                    s = 80 + 2 * (j % 4)
                    lk(nc.vector.reciprocal(st[:, s + 8:s + 10], st[:, s:s + 2]))
                    write(j, st[:, s + 8:s + 10], PS[:, 7, (j % 4) * P:(j % 4 + 1) * P].rearrange("p (t d) -> p t d", t=NT))\
                        .then_inc(*done("a_o", (tag, j)))

                for i in range(n + 2):
                    if i < n:
                        dve.wait_ge(*at("a_s", (tag, i)))
                        if i >= 2:
                            dve.wait_ge(*at("a_t", (tag, i - 2)))
                        for t in range(NT):
                            nk = P if causal and t == 0 else S
                            o = nc.vector.tensor_tensor_reduce(
                                out=sc[i % 2][:, t, 0:nk], in0=PS[:, 4 + i % 2, t * S:t * S + nk], in1=bias(i, t),
                                scale=1.0, scalar=-3e38, op0=ALU.add, op1=ALU.max,
                                accum_out=st[:, 64 + 2 * (i % 4) + t:65 + 2 * (i % 4) + t])
                        o.then_inc(*done("a_sc", (tag, i)))
                        dve.wait_ge(*at("a_sc", (tag, i)))
                        ts(st[:, 72 + 2 * (i % 4):74 + 2 * (i % 4)], st[:, 64 + 2 * (i % 4):66 + 2 * (i % 4)], -1.0, None,
                           ALU.mult).then_inc(*done("a_nm", (tag, i)))
                    if i >= 2:
                        finish(i - 2)
                    after(i)

            def na_write(j, rc, o):
                return tt(hn[:, :, 512 + DH * j:512 + DH * (j + 1)], o, bc(rc, 2, DH), ALU.mult)

            def ret_var():
                for t in range(NT):
                    dve.wait_ge(*at("gn_sq", t))
                    i = nc.vector.tensor_reduce(st[:, 32 + 8 * t:40 + 8 * t], h3(gsq[:, t, :]), AXX, ALU.add)
                i.then_inc(*done("gn_ss"))

            def ret_out():
                dve.wait_ge(*at("root", "gn"))
                lk(nc.vector.reciprocal(st[:, 32:48], st[:, 48:64]))
                for t in range(NT):
                    i = tt(h3(hn[:, t, 0:512]), h3(hn[:, t, 0:512]), bc(st[:, 32 + 8 * t:40 + 8 * t], 2, DH), ALU.mult)
                lk(i)
                dve.wait_ge(*read(("rg", 1)))
                for t in range(NT):
                    i = ts(rg[:, t, :], rg[:, t, :], 0.5, 0.5, ALU.mult, ALU.add)
                lk(i)
                for t in range(NT):
                    i = tt(rg[:, t, :], rg[:, t, :], PS[:, t, :], ALU.mult)
                lk(i)
                for t in range(NT):
                    i = tt(hn[:, t, 0:512], hn[:, t, 0:512], rg[:, t, :], ALU.mult)
                i.then_inc(*done("y0a"))

            attention("na", NH, lambda i, t: nabias[:, i, 128 - 128 * t:384 - 128 * t], False, na_write,
                      also({0: (ret_var,), 1: (ret_out,), 3: (lambda: T_lo("y0a", 4, 8, 0, lambda k: col("gn", k)),)}))
            T_lo("y0b", 4, 12, 4, lambda k: None)
            post(0, ("mo0", 3), 0)
            norm(1, "ffn0")
            ffn(0)
            post(1, ("D", 0, FI - 1))
            norm(2, "mix1")

            dve.wait_ge(*at("load_ssd"))
            dve.wait_ge(*at("w_used", slot_no[("dt", 0)]))
            for t in range(NT):
                i = tt(spxs["ssd"][:, 0, 64 * t:64 * t + 64], PS[:, 4 + t, 0:64], dtt[:, 4, :], ALU.add)
            i.then_inc(*done("sp_x", "ssd"))

            def ssd_conv(g, j):
                b = xbc_bank(g, j)
                ch = lambda m: 4 * g + 2 * j + m if j < 2 else 16 + 4 * m + g
                dve.wait_ge(*at("c_ctr", (g, 2 * j + 1)))
                for k in (0, 1, 3, 4):
                    for m in range(2):
                        i = taps(cvb[:, 2 * j + m, :], PS[:, b, m * S:(m + 1) * S], col(f"cw{k}", ch(m)), k - 2)
                    if k < 4:
                        lk(i)
                i.then_inc(*done("c_cnv", (g, j)))

            def hb(v, n=8):
                return v.rearrange("p (h d) -> p h d", h=n)

            def decay_rows(g, u):
                c, r, hf = u // 4, (u // 2) % 2, u % 2
                if u >= 2:
                    dve.wait_ge(*at("s_l", (g, u - 2)))
                a0 = 32 * r + 8 * g + 4 * hf
                tt(am[u % 2][:, :, :], bc(cc("le" if r == 0 else "ge"), 1, 4), bc(dtt[:, 2 + c, a0:a0 + 4], 2, P), ALU.mult)\
                    .then_inc(*done("s_am", (g, u)))

            exv = dtt[:, 8:10, :].rearrange("p a b -> p (a b)")

            def ssd_scale(g):
                y = hn[:, :, (g % 2) * 512:(g % 2) * 512 + 512]
                dve.wait_ge(*at("root", ("s", g)))
                lk(nc.vector.reciprocal(st[:, 100:102], st[:, 98:100]))
                for c in range(NT):
                    i = ts(y[:, c, :], y[:, c, :], st[:, 100 + c:101 + c], None, ALU.mult)
                i.then_inc(*done("s_y", g))

            def ssd(g):
                more = g + 1 < SG
                X = xs[g % 2]
                y = hn[:, :, (g % 2) * 512:(g % 2) * 512 + 512]
                dve.wait_ge(*at("s_bq", g))
                nc.vector.tensor_copy(btm[:, :, :], PS[:, 6, 0:S].rearrange("p (a b) -> p a b", a=2))
                pq = PS[:, 6, S:2 * S].rearrange("p (a b) -> p a b", a=2)
                tt(qk[:, 0, :, :], pq, bc(cc("le"), 1, 2), ALU.mult)
                lk(tt(qk[:, 1, :, :], pq, bc(cc("gt"), 1, 2), ALU.mult))
                if g == 0:
                    dve.wait_ge(*at("ex"))
                dve.wait_ge(*at("s_xs", g))
                for r in range(2):
                    for t in range(NT):
                        i = tt(hb(vfb[:, r, t, :]), hb(X[:, t, :]),
                               bc(dtt[:, t, 32 * r + 8 * g:32 * r + 8 * g + 8], 2, DH), ALU.mult)
                lk(i)
                for r in range(2):
                    i = tt(hb(vt[:, r, :]), hb(vfb[:, r, r, :]), bc(exv[:, 32 * r + 8 * g:32 * r + 8 * g + 8], 2, DH), ALU.mult)
                i.then_inc(*done("s_v", g))
                if g:
                    ssd_scale(g - 1)
                if more:
                    ssd_conv(g + 1, 2)
                if g >= 2:
                    dve.wait_ge(*at("turned", (("y", g - 2), 3)))
                dve.wait_ge(*at("s_yi", g))
                for r in range(2):
                    i = tt(hb(y[:, 1 - r, :]), hb(PS[:, 4 + r, :]),
                           bc(exv[:, 64 + 32 * r + 8 * g:64 + 32 * r + 8 * g + 8], 2, DH), ALU.mult)
                i.then_inc(*done("s_yie", g))
                decay_rows(g, 0)
                decay_rows(g, 1)
                if g:
                    T_lo(("y", g - 1), 4, (4 + 4 * g) % 16, 6, lambda k: col("ssdn", 4 * g - 4 + k))
                if more:
                    ssd_conv(g + 1, 0)
                for u in range(8):
                    c, r, hf = u // 4, (u // 2) % 2, u % 2
                    dve.wait_ge(*at("s_e", (g, u)))
                    tt(ee[u % 2][:, :, :], ee[u % 2][:, :, :], bc(qk[:, r, c, :], 1, 4), ALU.mult).then_inc(*done("s_m", (g, u)))
                    if u + 2 < 8:
                        decay_rows(g, u + 2)
                    if u == 4 and more:
                        ssd_conv(g + 1, 1)
                dve.wait_ge(*at("s_pv", (g, 7)))
                dve.wait_ge(*at("s_yie", g))
                for c in range(NT):
                    i = tt(y[:, c, :], y[:, c, :], PS[:, 7 - c, :], ALU.add)
                i.then_inc(*done("s_add", g))
                for c in range(NT):
                    i = tt(hb(X[:, c, :]), hb(X[:, c, :]), bc(dtt[:, 6, 8 * g:8 * g + 8], 2, DH), ALU.mult)
                lk(i)
                dve.wait_ge(*at("s_add", g))
                for c in range(NT):
                    i = tt(y[:, c, :], y[:, c, :], X[:, c, :], ALU.add)
                lk(i)
                dve.wait_ge(*read((("z", g), 1)))
                for c in range(NT):
                    i = tt(y[:, c, :], y[:, c, :], zt[g % 2][:, c, :], ALU.mult)
                lk(i)
                for c in range(NT):
                    i = nc.vector.tensor_tensor_reduce(out=X[:, c, :], in0=y[:, c, :], in1=y[:, c, :], scale=1.0, scalar=0.0,
                                                       op0=ALU.mult, op1=ALU.add, accum_out=st[:, 96 + c:97 + c])
                i.then_inc(*done("s_ss", g))

            ssd_conv(0, 2)
            softplus("ssd", 128, dtt[:, 0:2, :].rearrange("p a b -> p (a b)"))
            dve.wait_ge(*at("ssd_a"))
            stt3(out=dtt[:, 2:4, :], in0=dtt[:, 0:2, :], scalar=-1.0, in1=bc(dtt[:, 5, :], 1, 2), op0=ALU.mult, op1=ALU.mult)\
                .then_inc(*done("la"))
            ssd_conv(0, 0)
            ssd_conv(0, 1)
            for g in range(SG):
                ssd(g)
            ssd_scale(SG - 1)
            T_lo(("y", SG - 1), 4, (4 + 4 * SG) % 16, 6, lambda k: col("ssdn", 4 * SG - 4 + k))
            post(2, ("mo1", 7), 0)
            norm(3, "ffn1")
            ffn(1)
            post(3, ("D", 1, FI - 1))
            norm(4, "sec")

            def head_norm(nm, a, b0):
                for t in range(NT):
                    dve.wait_ge(*at("q_sq", (nm, t)))
                    i = nc.vector.tensor_reduce(st[:, 104 + 8 * t:112 + 8 * t], h3(sqb[:, t, :]), AXX, ALU.add)
                i.then_inc(*done("q_ss", nm))
                dve.wait_ge(*at("root", ("q", nm)))
                lk(nc.vector.reciprocal(st[:, 136:152], st[:, 120:136]))
                if a >= 2:
                    dve.wait_ge(*at("turned", (("qa", "ka")[a - 2], 3)))
                for t in range(NT):
                    o = hn[:, t, 512 * (a % 2):512 * (a % 2) + 512]
                    if nm != "ksv":
                        i = tt(h3(o), h3(PS[:, b0 + t, :]), bc(st[:, 136 + 8 * t:144 + 8 * t], 2, DH), ALU.mult)
                    else:
                        for w in range(2):
                            for r in range(2):
                                i = tt(o[:, 256 * w:256 * w + 256].rearrange("p (g r d) -> p g r d", g=2, r=2)[:, :, r, :],
                                       PS[:, b0 + t, 256 * w:256 * w + 128].rearrange("p (g d) -> p g d", g=2),
                                       bc(st[:, 136 + 8 * t + 4 * w:138 + 8 * t + 4 * w], 2, DH), ALU.mult)
                    i.then_inc(*done("read_v", (nm, t)))

            head_norm("qa", 0, 4)
            head_norm("ka", 1, 2)
            head_norm("qb", 2, 2)

            def windows(a, b):
                lk(nc.vector.memset(XC[a][:, :, :], 0.0))
                pos = cols[:, col_at[("posk", "posv")[a]]:col_at[("posk", "posv")[a]] + 16]
                for g in range(2):
                    for r in range(2):
                        base = PS[64 * r:64 * r + 64, b, g * S + r:g * S + r + 1]
                        src = bass.AP(base.tensor, base.offset, [list(base.ap[0]), [2, 16], [16, NCMP]])
                        i = tt(XC[a][64 * r:64 * r + 64, :, 16 * g:16 * g + NCMP], src,
                               bc(pos[64 * r:64 * r + 64, :], 2, NCMP), ALU.add)
                i.then_inc(*done("read_v", (("kc", "vc")[a], 0)))
                dve.wait_ge(*read((("kc", "vc")[a], 0)))

            dve.wait_ge(*at("w_used", slot_no[("vc", 0)]))
            windows(0, 0)
            windows(1, 1)
            for a in range(2):
                dve.wait_ge(*at("x_hi", a))
                tt(Tl[:, 8 + 2 * a:10 + 2 * a, :].rearrange("p a (b c) -> p (a b) c", c=32), XC[a][:, :, :],
                   Th[:, 8 + 2 * a:10 + 2 * a, :].rearrange("p a (b c) -> p (a b) c", c=32).bitcast(F32), ALU.subtract)\
                    .then_inc(*done("x_lo", a))
            head_norm("ksv", 3, 2)

            def cmp_hidden():
                dve.wait_ge(*at("c_ht", 0))
                nc.vector.tensor_copy(hid[:, :, :], PS[:, 2, 0:64].rearrange("p (m c) -> p m c", m=2)).then_inc(*done("c_hid"))

            def cmp_repeat():
                dve.wait_ge(*at("c_ht", 1))
                for m in range(2):
                    i = nc.vector.tensor_copy(hidr[:, m, :].rearrange("p (g h c) -> p g h c", g=2, h=4),
                                              bc(PS[:, 3, 32 * m:32 * m + 32].rearrange("p (g c) -> p g c", g=2), 2, 4))
                i.then_inc(*done("c_rep"))

            def cmp_keys():
                dve.wait_ge(*at("root", "ck"))
                lk(nc.vector.reciprocal(st[0:32, 14:15], st[0:32, 13:14]))
                for r in range(2):
                    i = ts(kcm[0:32, 0, DH * r:DH * r + DH], PS[0:32, 0, 0:DH], st[0:32, 14:15], None, ALU.mult)
                i.then_inc(*done("c_kn"))

            def cmp_values():
                dve.wait_ge(*at("c_v"))
                tt(vbd[:, :, :], bc(PS[:, 3, 0:DH], 1, 8), bc(cc("blk"), 2, DH), ALU.mult).then_inc(*done("c_vbd"))

            c3 = cpr[:, :, :].rearrange("p t (h c) -> p (t h) c", h=NH)

            def cmp_max():
                dve.wait_ge(*at("c_s"))
                for t in range(NT):
                    for r in range(2):
                        i = tt(cpr[:, t, :].rearrange("p (h r c) -> p h r c", h=4, r=2)[:, :, r, :],
                               PS[:, r, 64 * t:64 * t + 64].rearrange("p (h c) -> p h c", h=4),
                               bc(cc("cneg")[:, 16 * t:16 * t + 16], 1, 4), ALU.add)
                lk(i)
                lk(nc.vector.tensor_reduce(st[:, 104:120], c3, AXX, ALU.max))
                tt(c3, c3, bc(st[:, 104:120], 2, 16), ALU.subtract).then_inc(*done("c_sub"))

            gates = lambda k: gb[:, :, :].rearrange("p t (h k) -> p t h k", k=3)[:, :, :, k]

            def cmp_probs():
                dve.wait_ge(*at("c_exp"))
                lk(nc.vector.tensor_reduce(st[:, 120:136], c3, AXX, ALU.add))
                for t in range(NT):
                    v = cpr[:, t, :].rearrange("p (h c) -> p h c", h=NH)
                    i = tt(v, v, bc(cc("cval")[:, 16 * t:16 * t + 16], 1, NH), ALU.mult)
                i.then_inc(*done("c_p"))
                lk(nc.vector.reciprocal(st[:, 136:152], st[:, 120:136]))
                dve.wait_ge(*read(("gb", 1)))
                c8 = st[:, 136:152].rearrange("p (t h) -> p t h", t=NT)
                lk(tt(c8, c8, gates(0), ALU.mult))

            def cmp_out():
                dve.wait_ge(*at("c_o"))
                for t in range(NT):
                    i = tt(h3(sqb[:, t, :]), h3(PS[:, 2 + t, :]), bc(st[:, 136 + 8 * t:144 + 8 * t], 2, DH), ALU.mult)
                i.then_inc(*done("c_om"))

            def cmp_add():
                dve.wait_ge(*at("c_om"))
                dve.wait_ge(*at("a_o", ("nsa", NH - 1)))
                for t in range(NT):
                    i = tt(hn[:, t, 512:D], hn[:, t, 512:D], sqb[:, t, :], ALU.add)
                i.then_inc(*done("c_add"))

            def gated_a():
                dve.wait_ge(*at("a_o", ("moba", NH - 1)))
                dve.wait_ge(*read(("za", 1)))
                for t in range(NT):
                    i = tt(hn[:, t, 0:512], hn[:, t, 0:512], za[:, t, :], ALU.mult)
                i.then_inc(*done("y2a"))

            def sigmoid(nm, n, t):
                g = sg[(nm, n)]
                dve.wait_ge(*read(((nm, n), t)))
                lk(ts(g[:, t, :], g[:, t, :], 0.5, 0.5, ALU.mult, ALU.add))

            def branch_a(n):
                dve.wait_ge(*at("w_used", slot_no[(("YA", n), 0)]))
                g = sg[("GA", n)]
                for t in range(NT):
                    i = tt(g[:, t, :], g[:, t, :], PS[:, 2 * n + t, :], ALU.mult)
                i.then_inc(*done("ya", n))

            weights_low(slot_no[("w1k", 0)])
            dve.wait_ge(*at("load_tb0_0"))

            def moba_write(j, rc, o):
                return tt(hn[:, :, DH * j:DH * (j + 1)], o, bc(rc, 2, DH), ALU.mult)

            def nsa_write(j, rc, o):
                w, h = j // NH, j % NH
                lk(tt(rc, rc, gates(1 + w)[:, :, h], ALU.mult))
                if w == 0:
                    return tt(hn[:, :, 512 + DH * h:512 + DH * (h + 1)], o, bc(rc, 2, DH), ALU.mult)
                if j == NH:
                    dve.wait_ge(*at("c_add"))
                for t in range(NT):
                    ob = hn[:, t, 512 + DH * h:512 + DH * (h + 1)]
                    i = stt3(out=ob, in0=o[:, t, :], scalar=rc[:, t:t + 1], in1=ob, op0=ALU.mult, op1=ALU.add)
                return i

            tbias = lambda i, t: tb[:, i % NH, P:S] if t == 0 else tb[:, i % NH, :]
            attention("moba", NH, tbias, True, moba_write,
                      also({0: (lambda: weights_low(slot_no[("w1v", 0)]),), 3: (cmp_hidden,), 6: (cmp_keys, cmp_repeat), 8: (cmp_values,)}))
            dve.wait_ge(*at("load_tb1_0"))
            attention("nsa", 2 * NH, tbias, True, nsa_write,
                      also({0: (cmp_max, gated_a), 3: (lambda: dve.wait_ge(*at("load_tb1_4")),), 2: (cmp_probs,),
                            4: (lambda: sigmoid("GA", 0, 0),), 5: (lambda: sigmoid("GA", 0, 1),), 6: (cmp_out,),
                            7: (lambda: sigmoid("GA", 1, 0),), 8: (lambda: sigmoid("GA", 1, 1),), 9: (cmp_add,),
                            10: (lambda: T_lo("y2a", 4, 8, 0, lambda k: None),), 11: (lambda: sigmoid("GB", 0, 0),),
                            12: (lambda: sigmoid("GB", 0, 1),), 13: (lambda: sigmoid("GB", 1, 0),),
                            14: (lambda: sigmoid("GB", 1, 1),), 16: (lambda: branch_a(0),)}))
            dve.wait_ge(*at("a_o", ("nsa", 2 * NH - 1)))
            dve.wait_ge(*read(("zb", 1)))
            for t in range(NT):
                i = tt(hn[:, t, 512:D], hn[:, t, 512:D], zb[:, t, :], ALU.mult)
            i.then_inc(*done("y2b"))
            T_lo("y2b", 4, 12, 4, lambda k: None)
            branch_a(1)
            for n in range(2):
                dve.wait_ge(*at("w_used", slot_no[(("YB", n), 0)]))
                ga, g = sg[("GA", n)], sg[("GB", n)]
                for t in range(NT):
                    i = tt(g[:, t, :], g[:, t, :], PS[:, 6 - 6 * n + t, :], ALU.mult)
                i.then_inc(*done("yb", n))
                dve.wait_ge(*at("yb", n))
                dve.wait_ge(*at("ya", n))
                for t in range(NT):
                    i = tt(ga[:, t, :], ga[:, t, :], g[:, t, :], ALU.add)
                i.then_inc(*done("mrg", n))
            T_lo("mrg0", 4, 0, 4, lambda k: None)
            T_lo("mrg1", 4, 4, 6, lambda k: None)
            for t in range(NT):
                for hf in range(2):
                    n = slot_no[("fo", 3)]
                    dve.wait_ge(*(at("w_used", n) if (t, hf) == (1, 1) else at("sum", (n, t, hf))))
                    o = x[:, t, 512 * hf:512 * hf + 512]
                    i = tt(o, o, PS[:, 2 * t + hf, :], ALU.add)
                i.then_inc(*done("x", (5, t)))
        return C.marks


_INS = ["x", "norm_mix_pre", "norm_mix_post", "norm_ffn_pre", "norm_ffn_post", "ab_w_in", "ab_ret_decay_logit",
        "ab_ret_gn_g", "ab_na_rpb", "ab_w_out", "c_w_in", "c_conv_w", "c_conv_b", "c_dt_bias", "c_a_log", "c_d_skip",
        "c_norm_g", "c_w_out", "ffn_w_up", "ffn_conv_w", "ffn_conv_b", "ffn_w_down", "norm_w_2", "w_in_2",
        "q_norm_a_2", "k_norm_a_2", "q_norm_b_2", "k_norm_cmp_2", "k_norm_sel_2", "k_norm_win_2", "cmp_pos_k_2",
        "cmp_w1_k_2", "cmp_w2_k_2", "cmp_pos_v_2", "cmp_w1_v_2", "cmp_w2_v_2", "rel_bias_2", "w_branch_a_2",
        "w_branch_b_2", "w_out_2"]


def kernel(**inputs):
    import numpy as _np
    import concourse.bacc as _bacc
    from concourse import mybir as _mybir
    from concourse.bass_utils import run_bass_kernel_spmd as _run

    arrays = {f"in_{n}_dram": _np.ascontiguousarray(inputs[n]) for n in _INS}
    for n, a in (("const_table", CONST_TABLE), ("const_pfb", CONST_PFB), ("const_onehot", CONST_ONEHOT),
                 ("const_negs", CONST_NEGS)):
        arrays[f"in_{n}_dram"] = a
    known = None
    for _ in range(2):
        nc = _bacc.Bacc("TRN2", target_bir_lowering=False, num_devices=1)
        handles = {name[3:-5]: nc.dram_tensor(name, a.shape, _mybir.dt.from_np(a.dtype), kind="ExternalInput").ap()
                   for name, a in arrays.items()}
        out = nc.dram_tensor("out_0_dram", (1, S, D), _mybir.dt.float32, kind="ExternalOutput").ap()
        known = build(nc, handles, out, known)
    r = _run(nc, [arrays], core_ids=[0])
    return r.results[0]["out_0_dram"]
```
